# Optimizing a Trainium2 kernel written in Bass

```python
import math
import jax
import jax.numpy as jnp
from jax import lax
import numpy as np

D_MODEL = 1024
BATCH = 1
SEQ = 256
DEPTH = 2

GRID_W = 64
CTX_LEN = 256
N_MOD = 6
HEAD_DIM = 64
N_HEADS_A = 8
KV_HEADS_A = 2
WINDOW = 128
ATTN_BLOCK = 128
N_HEADS_B = 4
N_HEADS_C = 4
HEAD_DIM_C = 128
MLSTM_CHUNK = 128
N_BRANCHES = 3
A_Q = N_HEADS_A * HEAD_DIM
A_KV = KV_HEADS_A * HEAD_DIM
B_QK = N_HEADS_B * 2 * HEAD_DIM
B_V = N_HEADS_B * 2 * HEAD_DIM
C_WIDTH = N_HEADS_C * HEAD_DIM_C
C_GATES = 4 * N_HEADS_C
SPLIT_SIZES = (A_Q, A_KV, A_KV, B_QK, B_QK, B_V, C_WIDTH, C_WIDTH, C_WIDTH, C_WIDTH, C_GATES, N_BRANCHES * D_MODEL)
N_IN = sum(SPLIT_SIZES)
N_EXPERTS = 64
N_GROUPS = 8
TOPK_GROUPS = 4
TOP_K = 8
D_EXPERT = 256
D_SHARED = 256
ROUTED_SCALE = 2.5
EXPERT_BLOCK = 128
ROPE_BASE = 10000.0
EPS = 1e-6

kernel_name = "hybrid_diffusion_mixer_moe_block"

def rms_norm(x, g):
    xf = x.astype(jnp.float32)
    y = xf * lax.rsqrt(jnp.mean(xf * xf, axis=-1, keepdims=True) + EPS)
    return (y * g.astype(jnp.float32)).astype(x.dtype)

def modulate(h, shift, scale):
    return h * (1 + scale) + shift

def to_heads(a, n_heads):
    return a.reshape(*a.shape[:-1], n_heads, a.shape[-1] // n_heads)

def from_heads(a):
    return a.reshape(*a.shape[:-2], a.shape[-2] * a.shape[-1])

def split_proj(p):
    parts, start = [], 0
    for size in SPLIT_SIZES:
        parts.append(p[..., start:start + size])
        start += size
    return parts

def diff_pair(a):
    a = a.reshape(*a.shape[:-2], a.shape[-2] // 2, 2, a.shape[-1])
    return a[..., 0, :], a[..., 1, :]

def axial_rope_tables(row, col):
    quarter = HEAD_DIM // 4
    inv = 1.0 / (ROPE_BASE ** (jnp.arange(quarter, dtype=jnp.float32) / quarter))
    ang = jnp.stack([row.astype(jnp.float32)[:, None] * inv, col.astype(jnp.float32)[:, None] * inv], axis=1)
    return jnp.cos(ang), jnp.sin(ang)

def apply_rope(x, cos, sin):
    b, n, h, dh = x.shape
    q = dh // 4
    xr = x.astype(jnp.float32).reshape(b, n, h, 2, 2, q)
    a, bb = xr[..., 0, :], xr[..., 1, :]
    cs, sn = cos[None, :, None], sin[None, :, None]
    out = jnp.stack([a * cs - bb * sn, bb * cs + a * sn], axis=-2)
    return out.reshape(b, n, h, dh).astype(x.dtype)

def softmax_with_sink(s, sink):
    m = jnp.maximum(jnp.max(s, axis=-1, keepdims=True), sink)
    p = jnp.exp(s - m)
    return p / (jnp.sum(p, axis=-1, keepdims=True) + jnp.exp(sink - m))

def window_sink_attention(q, k, v, kc, vc, sink):
    b, s_len, h, dh = q.shape
    g = h // KV_HEADS_A
    nb = s_len // ATTN_BLOCK
    scale = dh ** -0.5
    pad = ((0, 0), (ATTN_BLOCK, ATTN_BLOCK), (0, 0), (0, 0))
    kp, vp = jnp.pad(k, pad), jnp.pad(v, pad)
    qb = q.reshape(b, nb, ATTN_BLOCK, KV_HEADS_A, g, dh).swapaxes(0, 1)
    sk = sink.astype(jnp.float32).reshape(KV_HEADS_A, g)[:, :, None, None]
    offs_q = jnp.arange(ATTN_BLOCK)
    offs_k = jnp.arange(3 * ATTN_BLOCK) - ATTN_BLOCK
    band = jnp.abs(offs_q[:, None] - offs_k[None, :]) <= WINDOW

    def one_block(args):
        qi, bi = args
        start = bi * ATTN_BLOCK
        kb = lax.dynamic_slice_in_dim(kp, start, 3 * ATTN_BLOCK, axis=1)
        vb = lax.dynamic_slice_in_dim(vp, start, 3 * ATTN_BLOCK, axis=1)
        kpos = start + offs_k
        valid = band & ((kpos >= 0) & (kpos < s_len))[None, :]
        s_lat = jnp.einsum('bqkgd,bskd->bkgqs', qi, kb).astype(jnp.float32) * scale
        s_lat = jnp.where(valid, s_lat, -jnp.inf)
        s_ctx = jnp.einsum('bqkgd,bckd->bkgqc', qi, kc).astype(jnp.float32) * scale
        p = softmax_with_sink(jnp.concatenate([s_lat, s_ctx], axis=-1), sk).astype(v.dtype)
        return (jnp.einsum('bkgqs,bskd->bqkgd', p[..., :3 * ATTN_BLOCK], vb)
                + jnp.einsum('bkgqc,bckd->bqkgd', p[..., 3 * ATTN_BLOCK:], vc))

    out = lax.map(one_block, (qb, jnp.arange(nb)))
    return out.swapaxes(0, 1).reshape(b, s_len, h, dh)

def ctx_sink_attention(q, k, v, sink):
    b, n, h, dh = q.shape
    g = h // KV_HEADS_A
    s = jnp.einsum('bqkgd,bckd->bkgqc', q.reshape(b, n, KV_HEADS_A, g, dh), k).astype(jnp.float32) * dh ** -0.5
    p = softmax_with_sink(s, sink.astype(jnp.float32).reshape(KV_HEADS_A, g)[:, :, None, None]).astype(v.dtype)
    return jnp.einsum('bkgqc,bckd->bqkgd', p, v).reshape(b, n, h, dh)

def diff_attend(q1, q2, k1, k2, v, lam):
    b, sq, h, dh = q1.shape
    nb = sq // ATTN_BLOCK
    scale = dh ** -0.5

    def blocks(a):
        return a.reshape(b, nb, ATTN_BLOCK, h, dh).swapaxes(0, 1)

    def one_block(args):
        a1, a2 = args
        p1 = jax.nn.softmax(jnp.einsum('bqhd,bkhd->bhqk', a1, k1).astype(jnp.float32) * scale, axis=-1)
        p2 = jax.nn.softmax(jnp.einsum('bqhd,bkhd->bhqk', a2, k2).astype(jnp.float32) * scale, axis=-1)
        att = (p1 - lam * p2).astype(v.dtype)
        return jnp.einsum('bhqk,bkhe->bqhe', att, v)

    out = lax.map(one_block, (blocks(q1), blocks(q2)))
    return out.swapaxes(0, 1).reshape(b, sq, h, v.shape[-1])

def mlstm_scan(q, k, v, log_i, log_f, state):
    b, n_tok, h, _ = q.shape
    dv = v.shape[-1]
    t = MLSTM_CHUNK
    nc = n_tok // t

    def chunks(a):
        a = jnp.moveaxis(a, 2, 1)
        a = a.reshape(b, h, nc, t, *a.shape[3:])
        return jnp.moveaxis(a, 2, 0)

    tril = jnp.tril(jnp.ones((t, t), dtype=bool))

    def step(carry, inp):
        c_st, n_st, m_st = carry
        qc, kc, vc, ic, fc = inp
        bcum = jnp.cumsum(fc, axis=-1)
        dmat = jnp.where(tril, bcum[..., :, None] - bcum[..., None, :] + ic[..., None, :], -jnp.inf)
        inter = bcum + m_st[..., None]
        m_t = jnp.maximum(inter, jnp.max(dmat, axis=-1))
        s = jnp.einsum('bhtd,bhsd->bhts', qc, kc) * jnp.exp(dmat - m_t[..., None])
        a_inter = jnp.exp(inter - m_t)
        num = jnp.einsum('bhts,bhse->bhte', s, vc) + a_inter[..., None] * jnp.einsum('bhtd,bhde->bhte', qc, c_st)
        den = jnp.sum(s, axis=-1) + a_inter * jnp.einsum('bhtd,bhd->bht', qc, n_st)
        h_out = num / jnp.maximum(jnp.abs(den), jnp.exp(-m_t))[..., None]
        b_last = bcum[..., -1]
        gsum = b_last[..., None] - bcum + ic
        m_new = jnp.maximum(b_last + m_st, jnp.max(gsum, axis=-1))
        decay = jnp.exp(b_last + m_st - m_new)
        wk = jnp.exp(gsum - m_new[..., None])[..., None] * kc
        c_new = decay[..., None, None] * c_st + jnp.einsum('bhtd,bhte->bhde', wk, vc)
        n_new = decay[..., None] * n_st + jnp.sum(wk, axis=-2)
        return (c_new, n_new, m_new), h_out

    state, hs = lax.scan(step, state, (chunks(q), chunks(k), chunks(v), chunks(log_i), chunks(log_f)))
    hs = jnp.moveaxis(hs, 0, 2).reshape(b, h, n_tok, dv)
    return jnp.moveaxis(hs, 1, 2), state

def mlstm_inputs(q, k, v, g, b_gate):
    gates = g.reshape(*g.shape[:-1], 4, N_HEADS_C).astype(jnp.float32) + b_gate.astype(jnp.float32)
    return (to_heads(q, N_HEADS_C).astype(jnp.float32),
            to_heads(k, N_HEADS_C).astype(jnp.float32) * HEAD_DIM_C ** -0.5,
            to_heads(v, N_HEADS_C).astype(jnp.float32), gates)

def bidir_mlstm(q, k, v, gates, qc, kc, vc, gates_c):
    b, _, h, dk = q.shape
    dv = v.shape[-1]
    zero = (jnp.zeros((b, h, dk, dv), jnp.float32), jnp.zeros((b, h, dk), jnp.float32), jnp.zeros((b, h), jnp.float32))
    flip = lambda a: jnp.flip(a, axis=1)
    logsig = jax.nn.log_sigmoid
    hc_f, st_f = mlstm_scan(qc, kc, vc, gates_c[..., 0, :], logsig(gates_c[..., 1, :]), zero)
    hl_f, _ = mlstm_scan(q, k, v, gates[..., 0, :], logsig(gates[..., 1, :]), st_f)
    hc_b, st_b = mlstm_scan(flip(qc), flip(kc), flip(vc), flip(gates_c[..., 2, :]), flip(logsig(gates_c[..., 3, :])), zero)
    hl_b, _ = mlstm_scan(flip(q), flip(k), flip(v), flip(gates[..., 2, :]), flip(logsig(gates[..., 3, :])), st_b)
    return hl_f + flip(hl_b), hc_f + flip(hc_b)

def token_mixers(hl, hc, cos, sin, lam_init, need_ctx, w_in, b_gate, sink, lam_q1, lam_k1,
                 lam_q2, lam_k2, g_diff, g_mlstm, w_a, w_b, w_c, w_out):
    (aq, ak, av, bq, bk, bv, cq, ck, cv, co, cg, gt) = split_proj(hl @ w_in)
    (aq_c, ak_c, av_c, bq_c, bk_c, bv_c, cq_c, ck_c, cv_c, co_c, cg_c, gt_c) = split_proj(hc @ w_in)
    f32 = jnp.float32

    ka_c, va_c = to_heads(ak_c, KV_HEADS_A), to_heads(av_c, KV_HEADS_A)
    oa = window_sink_attention(apply_rope(to_heads(aq, N_HEADS_A), cos, sin),
                               apply_rope(to_heads(ak, KV_HEADS_A), cos, sin),
                               to_heads(av, KV_HEADS_A), ka_c, va_c, sink)

    lam = (jnp.exp(jnp.sum(lam_q1.astype(f32) * lam_k1.astype(f32)))
           - jnp.exp(jnp.sum(lam_q2.astype(f32) * lam_k2.astype(f32))) + lam_init)
    q1, q2 = diff_pair(apply_rope(to_heads(bq, 2 * N_HEADS_B), cos, sin))
    k1, k2 = diff_pair(apply_rope(to_heads(bk, 2 * N_HEADS_B), cos, sin))
    k1_c, k2_c = diff_pair(to_heads(bk_c, 2 * N_HEADS_B))
    vb_c = to_heads(bv_c, N_HEADS_B)
    ob = diff_attend(q1, q2, jnp.concatenate([k1, k1_c], axis=1), jnp.concatenate([k2, k2_c], axis=1),
                     jnp.concatenate([to_heads(bv, N_HEADS_B), vb_c], axis=1), lam)

    h_lat, h_ctx = bidir_mlstm(*mlstm_inputs(cq, ck, cv, cg, b_gate), *mlstm_inputs(cq_c, ck_c, cv_c, cg_c, b_gate))

    def diff_out(o):
        return from_heads(rms_norm(o, g_diff) * (1.0 - lam_init))

    def mlstm_out(hh, o):
        normed = rms_norm(hh, g_mlstm.reshape(N_HEADS_C, HEAD_DIM_C))
        return from_heads(normed * jax.nn.sigmoid(to_heads(o, N_HEADS_C).astype(f32))).astype(o.dtype)

    def merge(oa_, ob_, oc_, gt_):
        g = jax.nn.sigmoid(gt_.reshape(*gt_.shape[:-1], N_BRANCHES, D_MODEL))
        y = (g[..., 0, :] * (from_heads(oa_) @ w_a) + g[..., 1, :] * (diff_out(ob_) @ w_b)
             + g[..., 2, :] * (oc_ @ w_c))
        return y @ w_out

    out_l = merge(oa, ob, mlstm_out(h_lat, co), gt)
    if not need_ctx:
        return out_l, None
    oa_c = ctx_sink_attention(to_heads(aq_c, N_HEADS_A), ka_c, va_c, sink)
    q1_c, q2_c = diff_pair(to_heads(bq_c, 2 * N_HEADS_B))
    ob_c = diff_attend(q1_c, q2_c, k1_c, k2_c, vb_c, lam)
    out_c = merge(oa_c, ob_c, mlstm_out(h_ctx, co_c), gt_c)
    return out_l, out_c

def swiglu(h, wg, wu, wd):
    return (jax.nn.silu(h @ wg) * (h @ wu)) @ wd

def route(h, w_router, b_router):
    s = jax.nn.sigmoid((h @ w_router).astype(jnp.float32))
    sel = s + b_router.astype(jnp.float32)
    per = N_EXPERTS // N_GROUPS
    grp = sel.reshape(*sel.shape[:-1], N_GROUPS, per)
    grp_score = jnp.sum(lax.top_k(grp, 2)[0], axis=-1)
    top_g = lax.top_k(grp_score, TOPK_GROUPS)[1]
    g_mask = jnp.sum(jax.nn.one_hot(top_g, N_GROUPS, dtype=jnp.float32), axis=-2)
    e_mask = jnp.repeat(g_mask, per, axis=-1) > 0
    idx = lax.top_k(jnp.where(e_mask, sel, -jnp.inf), TOP_K)[1]
    w = jnp.take_along_axis(s, idx, axis=-1)
    w = w / jnp.sum(w, axis=-1, keepdims=True) * ROUTED_SCALE
    return idx, w.astype(h.dtype)

def grouped_experts(hs, idx, wts, w_eg, w_eu, w_ed):
    n_tok, d = hs.shape
    n_assign = n_tok * TOP_K
    flat_e = idx.reshape(n_assign)
    order = jnp.argsort(flat_e)
    sorted_e = flat_e[order]
    tok = order // TOP_K
    counts = jnp.bincount(flat_e, length=N_EXPERTS)
    padded = (counts + EXPERT_BLOCK - 1) // EXPERT_BLOCK * EXPERT_BLOCK
    pad_end = jnp.cumsum(padded)
    pad_start = pad_end - padded
    grp_start = jnp.cumsum(counts) - counts
    dest = pad_start[sorted_e] + jnp.arange(n_assign) - grp_start[sorted_e]
    n_blocks = -(-n_assign // EXPERT_BLOCK) + N_EXPERTS
    rows = jnp.full((n_blocks * EXPERT_BLOCK,), n_tok, dtype=jnp.int32).at[dest].set(tok)
    block_e = jnp.minimum(jnp.searchsorted(pad_end, jnp.arange(n_blocks) * EXPERT_BLOCK, side='right'), N_EXPERTS - 1)
    xs = jnp.concatenate([hs, jnp.zeros((1, d), hs.dtype)], axis=0)[rows].reshape(n_blocks, EXPERT_BLOCK, d)

    def run_block(args):
        xb, e = args
        return swiglu(xb, w_eg[e], w_eu[e], w_ed[e])

    ys = lax.map(run_block, (xs, block_e)).reshape(n_blocks * EXPERT_BLOCK, d)
    contrib = ys[dest] * wts.reshape(n_assign)[order][:, None]
    return jnp.zeros((n_tok, d), ys.dtype).at[tok].add(contrib)

def moe_ffn(h, w_router, b_router, w_eg, w_eu, w_ed, w_sg, w_su, w_sd):
    idx, wts = route(h, w_router, b_router)
    routed = lax.map(lambda a: grouped_experts(a[0], a[1], a[2], w_eg, w_eu, w_ed), (h, idx, wts))
    return routed + swiglu(h, w_sg, w_su, w_sd)

def setup_inputs(seed: int = 0) -> dict:
    key = jax.random.key(seed)
    ks = jax.random.split(key, 32)
    f32 = jnp.float32
    d = D_MODEL

    def nrm(k, shape, scale):
        return jax.random.normal(k, shape, f32) * scale

    b_i = nrm(ks[9], (DEPTH, 2, N_HEADS_C), 0.1)
    b_f = 3.0 + 3.0 * jax.random.uniform(ks[10], (DEPTH, 2, N_HEADS_C), f32)
    return {
        'x': nrm(ks[0], (BATCH, SEQ, d), 1.0),
        'c': nrm(ks[1], (BATCH, d), 1.0),
        'ctx': nrm(ks[2], (BATCH, CTX_LEN, d), 1.0),
        'c_ctx': nrm(ks[3], (d,), 1.0),
        'w_mod': nrm(ks[4], (DEPTH, d, N_MOD * d), 0.5 * d ** -0.5),
        'b_mod': nrm(ks[5], (DEPTH, N_MOD * d), 0.02),
        'g_mix': 1.0 + nrm(ks[6], (DEPTH, d), 0.05),
        'g_ffn': 1.0 + nrm(ks[7], (DEPTH, d), 0.05),
        'w_in': nrm(ks[8], (DEPTH, d, N_IN), d ** -0.5),
        'b_gate': jnp.stack([b_i[:, 0], b_f[:, 0], b_i[:, 1], b_f[:, 1]], axis=1),
        'sink': nrm(ks[11], (DEPTH, N_HEADS_A), 0.5),
        'lam_q1': nrm(ks[12], (DEPTH, HEAD_DIM), 0.1),
        'lam_k1': nrm(ks[13], (DEPTH, HEAD_DIM), 0.1),
        'lam_q2': nrm(ks[14], (DEPTH, HEAD_DIM), 0.1),
        'lam_k2': nrm(ks[15], (DEPTH, HEAD_DIM), 0.1),
        'g_diff': 1.0 + nrm(ks[16], (DEPTH, 2 * HEAD_DIM), 0.05),
        'g_mlstm': 1.0 + nrm(ks[17], (DEPTH, C_WIDTH), 0.05),
        'w_a': nrm(ks[18], (DEPTH, A_Q, d), A_Q ** -0.5),
        'w_b': nrm(ks[19], (DEPTH, B_V, d), B_V ** -0.5),
        'w_c': nrm(ks[20], (DEPTH, C_WIDTH, d), C_WIDTH ** -0.5),
        'w_out': nrm(ks[21], (DEPTH, d, d), d ** -0.5),
        'w_router': nrm(ks[22], (DEPTH, d, N_EXPERTS), d ** -0.5),
        'b_router': nrm(ks[23], (DEPTH, N_EXPERTS), 0.01),
        'w_exp_gate': nrm(ks[24], (DEPTH, N_EXPERTS, d, D_EXPERT), d ** -0.5),
        'w_exp_up': nrm(ks[25], (DEPTH, N_EXPERTS, d, D_EXPERT), d ** -0.5),
        'w_exp_down': nrm(ks[26], (DEPTH, N_EXPERTS, D_EXPERT, d), D_EXPERT ** -0.5),
        'w_sh_gate': nrm(ks[27], (DEPTH, d, D_SHARED), d ** -0.5),
        'w_sh_up': nrm(ks[28], (DEPTH, d, D_SHARED), d ** -0.5),
        'w_sh_down': nrm(ks[29], (DEPTH, D_SHARED, d), D_SHARED ** -0.5),
        'g_final': 1.0 + nrm(ks[30], (d,), 0.05),
    }

def reference(x, c, ctx, c_ctx, w_mod, b_mod, g_mix, g_ffn, w_in, b_gate, sink, lam_q1, lam_k1,
              lam_q2, lam_k2, g_diff, g_mlstm, w_a, w_b, w_c, w_out, w_router, b_router,
              w_exp_gate, w_exp_up, w_exp_down, w_sh_gate, w_sh_up, w_sh_down, g_final):
    b, s_len, d = x.shape
    ctx_len = ctx.shape[1]
    rows = s_len // GRID_W
    row = jnp.repeat(jnp.arange(rows), GRID_W)
    col = jnp.tile(jnp.arange(GRID_W), rows)
    cos, sin = axial_rope_tables(row, col)
    xc = ctx
    for layer in range(DEPTH):
        need_ctx = layer < DEPTH - 1
        lam_init = 0.8 - 0.6 * math.exp(-0.3 * layer)
        mod = (jax.nn.silu(c) @ w_mod[layer] + b_mod[layer]).reshape(b, N_MOD, 1, d)
        mod_c = (jax.nn.silu(c_ctx) @ w_mod[layer] + b_mod[layer]).reshape(N_MOD, d)
        hl = modulate(rms_norm(x, g_mix[layer]), mod[:, 0], mod[:, 1])
        hc = modulate(rms_norm(xc, g_mix[layer]), mod_c[0], mod_c[1])
        out_l, out_c = token_mixers(hl, hc, cos, sin, lam_init, need_ctx, w_in[layer], b_gate[layer],
                                    sink[layer], lam_q1[layer], lam_k1[layer], lam_q2[layer], lam_k2[layer],
                                    g_diff[layer], g_mlstm[layer], w_a[layer], w_b[layer], w_c[layer], w_out[layer])
        x = x + mod[:, 2] * out_l
        hl = modulate(rms_norm(x, g_ffn[layer]), mod[:, 3], mod[:, 4])
        moe = (w_router[layer], b_router[layer], w_exp_gate[layer], w_exp_up[layer], w_exp_down[layer],
               w_sh_gate[layer], w_sh_up[layer], w_sh_down[layer])
        if need_ctx:
            xc = xc + mod_c[2] * out_c
            hc = modulate(rms_norm(xc, g_ffn[layer]), mod_c[3], mod_c[4])
            y = moe_ffn(jnp.concatenate([hc, hl], axis=1), *moe)
            xc = xc + mod_c[5] * y[:, :ctx_len]
            x = x + mod[:, 5] * y[:, ctx_len:]
        else:
            x = x + mod[:, 5] * moe_ffn(hl, *moe)
    return rms_norm(x, g_final)


_drawn_inputs = setup_inputs


def setup_inputs(seed=0):
    import zlib

    import numpy as np

    out = dict(_drawn_inputs(seed))
    spreads = {}
    factors = {'sink': 8.0}
    for name, (base, spread) in spreads.items():
        noise = np.random.default_rng([zlib.crc32(name.encode()), seed]).standard_normal(out[name].shape)
        drawn = base * np.exp(spread * noise) if base else spread * noise
        out[name] = jnp.asarray(drawn.astype(out[name].dtype))
    for name, factor in factors.items():
        out[name] = (out[name] * factor).astype(out[name].dtype)
    return out
```

```python
import math
from contextlib import ExitStack

import concourse.bass as bass
from concourse import mybir

P = 128
D, L = 1024, 2
KT = D // P
NCTX = NLAT = 256
NTOK = NCTX + NLAT
TT = NTOK // P
LAT0 = NCTX // P
HB, DH = 4, 64
EPS = 1e-6
NE, NG, TOPK, DE = 64, 8, 8, 256
PER = NE // NG
ROUTED_SCALE = 2.5
SLOT = KT * 2 * DE + 2 * D
NSLOT = 4
RING = 2
NBLK = NTOK // P
MAXOVER = NTOK * TOPK // P
BIG = 1e30

MOD0, IN0, MERGE0, OUT0, SHARED0, NCHUNK = 0, 12, 21, 27, 29, 30
AQ, BQ, BK, CQ, CK, MISC, BV, CV, CO = range(IN0, IN0 + 9)
CHUNK = {**{c: KT * 512 for c in range(NCHUNK)}, MISC: KT * 272,
         **{c: KT * 512 + 4 * 512 for c in range(MERGE0, OUT0)}, SHARED0: SLOT}

R_BROUTER, R_SINK, R_GDIFF, R_GMLSTM, R_BGATE, R_LAM = 0, 64, 72, 200, 712, 728
NROW = R_LAM + 4 * DH
C_ID, C_ONES, C_LE, C_GE, C_ROT, C_COS, C_SIN, C_BAND, C_MF, C_MB, C_IOTA = (
    0, 128, 256, 384, 512, 640, 896, 1152, 1152 + 1024, 2304, 2432)
C_TOK, C_PIDX1, C_OVER = 2560, 2564, 2568
NCONST = 2568 + 2 * 192

ALU = mybir.AluOpType
ACT = mybir.ActivationFunctionType
F32 = mybir.dt.float32
FP16 = mybir.dt.float16
I32 = mybir.dt.int32
U32 = mybir.dt.uint32
AX = mybir.AxisListType.X


class Space:
    pass


def build(nc, a):
    ctx = ExitStack()
    with ctx:
        layer_sems = []

        def sem(name):
            layer_sems.append(nc.alloc_semaphore(name=name))
            return layer_sems[-1]

        def kept_sem(name):
            return ctx.enter_context(nc.semaphore(name))

        def sb(stack, name, shape, dt=F32):
            return stack.enter_context(nc.sbuf_tensor(name, shape, dt))

        V, A, T, G = nc.vector, nc.scalar, nc.tensor, nc.gpsimd
        PS = ctx.enter_context(nc.psum_tensor("banks", [P, 8, 512], F32))
        ring = [sb(ctx, f"weights{i}", [P, SLOT]) for i in range(RING)]
        X = sb(ctx, "x_resident", [P, TT, D])
        hT = sb(ctx, "hT", [P, KT, NTOK])
        cst = sb(ctx, "constants", [P, NCONST])
        rowp = sb(ctx, "row_params", [P, NROW])
        colp = sb(ctx, "col_params", [P, 64])
        cc = sb(ctx, "cond_cols", [P, KT, 2])
        sc = sb(ctx, "silu_cond", [P, KT, 2])
        modc = sb(ctx, "mod_cols", [P, 6, KT, 2])
        Amix = sb(ctx, "a_mix", [P, KT, 2])
        Affn = sb(ctx, "a_ffn", [P, KT, 2])
        eps_t = sb(ctx, "epsilon", [P, 1])
        eps = eps_t[:]
        ident, ones = cst[:, C_ID:C_ID + P], cst[:, C_ONES:C_ONES + P]
        iota = cst[:, C_IOTA:C_IOTA + P]

        s_dve, s_act = kept_sem("dve_chain"), kept_sem("act_chain")
        ld = [kept_sem(f"slot_loaded{i}") for i in range(NSLOT)]
        loads = [0] * NSLOT
        freed = {}
        issued = [0]
        s_written = kept_sem("out_written")
        s_par = kept_sem("params_loaded")
        nparam = [0]
        chain = [0, 0]

        def vlink(ins):
            chain[0] += 1
            ins.then_inc(s_dve, 1)
            V.wait_ge(s_dve, chain[0])

        def alink(ins):
            chain[1] += 1
            ins.then_inc(s_act, 1)
            A.wait_ge(s_act, chain[1])

        def bc(ap, *shape):
            return ap.to_broadcast(list(shape))

        def sp_loads(sp, upto):
            while issued[0] < min(upto, L * NCHUNK):
                n = issued[0]
                if n >= RING:
                    if freed[n - RING] is not None:
                        sp.wait_ge(*freed[n - RING])
                size = CHUNK[n % NCHUNK]
                sp.dma_start(ring[n % RING][:, 0:size], a["wseq"][n // NCHUNK, n % NCHUNK, :, 0:size]
                             ).then_inc(ld[n % RING], 16)
                loads[n % RING] += 1
                landed[n] = 16 * loads[n % RING]
                issued[0] += 1
        landed = {}

        def chunk_ready(pe, n):
            pe.wait_ge(ld[n % RING], landed[n])
            return ring[n % RING]

        def end_layer():
            with nc.Block() as block:
                @block.sync
                def _(sp):
                    for s in layer_sems:
                        sp.sem_clear(s)
            for s in layer_sems:
                nc.release_semaphore(s)
            layer_sems.clear()
            for n in freed:
                freed[n] = None


        with nc.Block() as block:
            s_x = sem("x_loaded")

            @block.sync
            def _(sp):
                sp.dma_start(cst[:], a["const"]).then_inc(s_x, 16)
                sp.dma_start(cc[:], a["cond"]).then_inc(s_x, 16)
                sp.dma_start(X[:], a["x"].rearrange("(t p) d -> p t d", p=P)).then_inc(s_x, 16)
                sp_loads(sp, RING)

            @block.vector
            def _(dve):
                V.memset(eps_t[:], EPS)

            @block.scalar
            def _(act):
                act.wait_ge(s_x, 48)
                A.activation(sc[:], cc[:], ACT.Silu)

        e = Space()
        e.V, e.A, e.T, e.G, e.PS = V, A, T, G, PS
        e.ring, e.X, e.hT, e.cst, e.rowp, e.colp = ring, X, hT, cst, rowp, colp
        e.sc, e.modc, e.Amix, e.Affn, e.eps = sc, modc, Amix, Affn, eps
        e.ident, e.ones, e.iota = ident, ones, iota
        e.ld, e.loads, e.freed, e.s_written, e.s_par, e.nparam = ld, loads, freed, s_written, s_par, nparam
        e.sem, e.sb, e.vlink, e.alink, e.bc = sem, sb, vlink, alink, bc
        e.sp_loads, e.chunk_ready = sp_loads, chunk_ready
        for l in range(L):
            layer(nc, a, e, l)
            end_layer()
        final_norm(nc, a, e)


def layer(nc, a, e, l):
    need_ctx = l < L - 1
    tiles = list(range(TT)) if need_ctx else list(range(LAT0, TT))
    mod_stage(nc, a, e, l)
    norm_stage(nc, a, e, l, "mix", range(TT), e.Amix, 0)
    with ExitStack() as mix:
        m = Space()
        m.aqT = e.sb(mix, f"aqT_{l}", [P, 4, NTOK])
        m.bqT = e.sb(mix, f"bqT_{l}", [P, 4, NTOK])
        m.cqT = e.sb(mix, f"cqT_{l}", [P, 4, NTOK])
        m.bkT = e.sb(mix, f"bkT_{l}", [P, 4, NTOK])
        m.ckT = e.sb(mix, f"ckT_{l}", [P, 4, NTOK])
        m.akT = e.sb(mix, f"akT_{l}", [P, 1, NTOK])
        m.misc = e.sb(mix, f"misc_{l}", [P, TT, 144])
        m.ck = e.sb(mix, f"ck_{l}", [P, TT, 512])
        m.bv = e.sb(mix, f"bv_{l}", [P, TT, 512])
        m.cv = e.sb(mix, f"cv_{l}", [P, TT, 4, P + 1])
        proj_stage(nc, a, e, m, l, tiles)
        attn_a_stage(nc, a, e, m, l, tiles)
        attn_b_stage(nc, a, e, m, l, tiles)
        mlstm_stage(nc, a, e, m, l, tiles)
        merge_stage(nc, a, e, m, l, tiles)
    norm_stage(nc, a, e, l, "ffn", tiles, e.Affn, 3)
    moe(nc, a, e, l, tiles)


def mod_stage(nc, a, e, l):
    V, A, T, PS, sem = e.V, e.A, e.T, e.PS, e.sem
    with nc.Block() as block:
        s_mod = sem(f"mod_chunk_done{l}")
        for c in range(12):
            e.freed[l * NCHUNK + c] = (s_mod, c + 1)

        @block.sync
        def _(sp):
            sp.dma_start(e.rowp[:], a["rowp"][l]).then_inc(e.s_par, 16)
            sp.dma_start(e.colp[:], a["colp"][l]).then_inc(e.s_par, 16)
            e.nparam[0] += 32
            e.sp_loads(sp, l * NCHUNK + IN0 + RING)

        @block.tensor
        def _(pe):
            for c in range(12):
                w = e.chunk_ready(pe, l * NCHUNK + c)
                for nt in range(4):
                    at = (c * 4 + nt) * 2
                    for k in range(KT):
                        last = T.matmul(PS[:, 0, at:at + 2], w[:, k * 512 + nt * P:k * 512 + nt * P + P],
                                        e.sc[:, k, :], start=k == 0, stop=k == KT - 1)
                last.then_inc(s_mod, 1)

        @block.vector
        def _(dve):
            dve.wait_ge(e.s_par, e.nparam[0])
            dve.wait_ge(s_mod, 12)
            mod = e.modc[:].rearrange("p m k v -> p (m k) v")
            e.vlink(V.tensor_tensor(mod, PS[:, 0, 0:96].rearrange("p (n v) -> p n v", v=2),
                                    e.bc(e.colp[:, 0:48].unsqueeze(2), P, 48, 2), ALU.add))
            for dst, g, m in ((e.Amix, 48, 1), (e.Affn, 56, 4)):
                V.scalar_tensor_tensor(dst[:], e.modc[:, m], 1.0,
                                       e.bc(e.colp[:, g:g + KT].unsqueeze(2), P, KT, 2), ALU.add, ALU.mult)


def norm_stage(nc, a, e, l, tag, tiles, scale, shift):
    V, A, T, PS, sem = e.V, e.A, e.T, e.PS, e.sem
    tiles = list(tiles)
    t0 = tiles[0]
    with ExitStack() as st, nc.Block() as block:
        xn = e.sb(st, f"xn_{tag}{l}", [P, 2, D])
        ms = e.sb(st, f"ms_{tag}{l}", [P, TT])
        s_xn, s_tp = sem(f"xn_ready_{tag}{l}"), sem(f"transposed_{tag}{l}")
        s_va, s_vb = sem(f"evac_dve_{tag}{l}"), sem(f"evac_act_{tag}{l}")
        s_ms, s_rs = sem(f"mean_square_{tag}{l}"), sem(f"inv_rms_{tag}{l}")

        def evac(i, t, ks, on_dve, done):
            v = 0 if t < LAT0 else 1
            for k in ks:
                src = PS[:, 2 * (i % 4) + k // 4, (k % 4) * P:(k % 4) * P + P]
                dst = e.hT[:, k, t * P:t * P + P]
                sc_, sh_ = scale[:, k, v:v + 1], e.modc[:, shift, k, v:v + 1]
                if on_dve:
                    last = V.tensor_scalar(dst, src, sc_, sh_, ALU.mult, ALU.add)
                else:
                    last = A.activation(dst, src, ACT.Identity, bias=sh_, scale=sc_)
            last.then_inc(done, 1)

        @block.vector
        def _(dve):
            for i, t in enumerate(tiles):
                V.tensor_tensor_reduce(out=xn[:, i % 2], in0=e.X[:, t], in1=e.X[:, t], scale=1.0 / D, scalar=0.0,
                                       op0=ALU.mult, op1=ALU.add, accum_out=ms[:, t:t + 1]).then_inc(s_ms, 1)
                dve.wait_ge(s_ms, i + 1)
            dve.wait_ge(s_rs, 1)
            e.vlink(V.reciprocal(ms[:, t0:TT], ms[:, t0:TT]))
            for i, t in enumerate(tiles):
                if i >= 2:
                    dve.wait_ge(s_tp, i - 1)
                V.tensor_scalar(xn[:, i % 2], e.X[:, t], ms[:, t:t + 1], None, ALU.mult).then_inc(s_xn, 1)
                dve.wait_ge(s_tp, i + 1)
                evac(i, t, range(0, 4), True, s_va)

        @block.tensor
        def _(pe):
            for i, t in enumerate(tiles):
                pe.wait_ge(s_xn, i + 1)
                for k in range(KT):
                    last = T.transpose(PS[:, 2 * (i % 4) + k // 4, (k % 4) * P:(k % 4) * P + P],
                                       xn[:, i % 2, k * P:k * P + P], e.ident)
                last.then_inc(s_tp, 1)

        @block.scalar
        def _(act):
            act.wait_ge(s_ms, len(tiles))
            A.activation(ms[:, t0:TT], ms[:, t0:TT], ACT.Sqrt, bias=e.eps).then_inc(s_rs, 1)
            for i, t in enumerate(tiles):
                act.wait_ge(s_tp, i + 1)
                evac(i, t, range(4, KT), False, s_vb)


def proj_stage(nc, a, e, m, l, tiles):
    V, A, T, PS, sem = e.V, e.A, e.T, e.PS, e.sem
    base = l * NCHUNK
    q0 = tiles[0] * P
    kscale = float(P) ** -0.5
    units = []
    for c, dst, rope, lo, sc in ((AQ, m.aqT, 1, q0, 1.0), (BQ, m.bqT, 1, q0, 1.0), (BK, m.bkT, 1, 0, 1.0),
                                 (CQ, m.cqT, 0, q0, 1.0), (CK, m.ckT, 0, 0, kscale)):
        for j in range(4):
            units.append(("T", c, 512, j * P, P, dst[:, j, :], rope, lo, sc))
        if c == CK:
            for t in range(TT):
                units.append(("tok", c, 512, 0, 512, m.ck[:, t], 0, t, kscale))
    units.append(("T", MISC, 272, 0, P, m.akT[:, 0], 1, 0, 1.0))
    for t in range(TT):
        units.append(("tok", MISC, 272, P, 144, m.misc[:, t], 0, t, 1.0))
    for t in range(TT):
        units.append(("tok", BV, 512, 0, 512, m.bv[:, t], 0, t, 1.0))
    for t in range(TT):
        units.append(("tok", CV, 512, 0, 512, m.cv[:, t, :, 0:P], 0, t, 1.0))
    ropes = [u for u, x in enumerate(units) if x[6]]

    with ExitStack() as st, nc.Block() as block:
        tmp = e.sb(st, f"rope_tmp{l}", [P, 2, NLAT])
        s_mm, s_ev = sem(f"proj_done{l}"), sem(f"proj_evacuated{l}")
        s_rot, s_rope = sem(f"rotated{l}"), sem(f"roped{l}")
        for u, x in enumerate(units):
            e.freed[base + x[1]] = (s_mm, u + 1)

        @block.sync
        def _(sp):
            e.sp_loads(sp, base + CO + RING)

        @block.tensor
        def _(pe):
            def rotate(u):
                r = ropes.index(u)
                pe.wait_ge(s_ev, u + 1)
                if r >= 2:
                    pe.wait_ge(s_rope, r - 1)
                T.matmul(PS[:, 4 + r % 2, 0:NLAT], e.cst[:, C_ROT:C_ROT + P], units[u][5][:, NCTX:NTOK],
                         start=True, stop=True).then_inc(s_rot, 1)

            for u, (kind, c, width, col, n, dst, rope, lo, sc) in enumerate(units):
                w = e.chunk_ready(pe, base + c)
                if u >= 4:
                    pe.wait_ge(s_ev, u - 3)
                for k in range(KT):
                    wk = w[:, k * width + col:k * width + col + n]
                    if kind == "T":
                        last = T.matmul(PS[:, u % 4, lo:NTOK], wk, e.hT[:, k, lo:NTOK], start=k == 0, stop=k == KT - 1)
                    else:
                        last = T.matmul(PS[:, u % 4, 0:n], e.hT[:, k, lo * P:lo * P + P], wk,
                                        start=k == 0, stop=k == KT - 1)
                last.then_inc(s_mm, 1)
                if u >= 1 and units[u - 1][6]:
                    rotate(u - 1)

        @block.scalar
        def _(act):
            for u, (kind, c, width, col, n, dst, rope, lo, sc) in enumerate(units):
                act.wait_ge(s_mm, u + 1)
                if kind == "T":
                    A.activation(dst[:, lo:NTOK], PS[:, u % 4, lo:NTOK], ACT.Copy, scale=sc).then_inc(s_ev, 1)
                else:
                    src = PS[:, u % 4, 0:n]
                    if c == CV:
                        src = src.rearrange("p (h d) -> p h d", h=4)
                    A.activation(dst, src, ACT.Copy, scale=sc).then_inc(s_ev, 1)

        @block.vector
        def _(dve):
            V.memset(m.cv[:, :, :, P:P + 1], 1.0)
            for r, u in enumerate(ropes):
                lat = units[u][5][:, NCTX:NTOK]
                dve.wait_ge(s_rot, r + 1)
                V.tensor_tensor(tmp[:, r % 2], PS[:, 4 + r % 2, 0:NLAT], e.cst[:, C_SIN:C_SIN + NLAT], ALU.mult)
                e.vlink(V.tensor_tensor(lat, lat, e.cst[:, C_COS:C_COS + NLAT], ALU.mult))
                V.tensor_tensor(lat, lat, tmp[:, r % 2], ALU.add).then_inc(s_rope, 1)


def attn_a_stage(nc, a, e, m, l, tiles):
    V, A, T, PS, sem = e.V, e.A, e.T, e.PS, e.sem
    units = [(t, g) for t in tiles for g in range(2)]
    with ExitStack() as st, nc.Block() as block:
        S = e.sb(st, f"a_probs{l}", [P, 4, NTOK])
        PT = e.sb(st, f"a_probsT{l}", [P, 4, 4, P])
        O = e.sb(st, f"a_out{l}", [P, 2, 8, DH])
        mx = e.sb(st, f"a_stats{l}", [P, 6, 4])
        s_sc, s_m, s_ex, s_tr, s_pt, s_pv, s_o, s_ot, s_oev = (sem(f"{n}{l}") for n in (
            "a_scores", "a_max", "a_exp", "a_transposed", "a_probsT_ready", "a_pv", "a_out_ready",
            "a_outT", "a_outT_stored"))

        def nk(t):
            return NTOK if t >= LAT0 else NCTX

        @block.tensor
        def _(pe):
            for u, (t, g) in enumerate(units):
                n = nk(t)
                if u >= 1:
                    pe.wait_ge(s_o, u)
                for h in range(4):
                    last = T.matmul(PS[:, h, 0:n], m.aqT[g * DH:g * DH + DH, h, t * P:t * P + P],
                                    m.akT[g * DH:g * DH + DH, 0, 0:n], start=True, stop=True)
                last.then_inc(s_sc, 1)
                pe.wait_ge(s_ex, u + 1)
                for h in range(4):
                    for k in range(n // P):
                        last = T.transpose(PS[:, 4 + h, k * P:k * P + P], S[:, h, k * P:k * P + P], e.ident)
                last.then_inc(s_tr, 1)
                pe.wait_ge(s_pt, 2 * u + 2)
                for h in range(4):
                    for k in range(n // P):
                        last = T.matmul(PS[:, 0, h * DH:h * DH + DH], PT[:, h, k, :],
                                        m.misc[:, k, g * DH:g * DH + DH], start=k == 0, stop=k == n // P - 1)
                last.then_inc(s_pv, 1)
                if g == 1:
                    i = u // 2
                    pe.wait_ge(s_o, u + 1)
                    for j in range(4):
                        last = T.transpose(PS[:, 1, j * P:j * P + P],
                                           O[:, i % 2].rearrange("p h d -> p (h d)")[:, j * P:j * P + P], e.ident)
                    last.then_inc(s_ot, 1)
                    pe.wait_ge(s_oev, i + 1)

        @block.vector
        def _(dve):
            for u, (t, g) in enumerate(units):
                n = nk(t)
                sink = e.rowp[:, R_SINK + 4 * g:R_SINK + 4 * g + 4]
                dve.wait_ge(s_sc, u + 1)
                if t >= LAT0:
                    band = e.cst[:, C_BAND + (t - LAT0) * NTOK:C_BAND + (t - LAT0) * NTOK + n]
                    e.vlink(V.scalar_tensor_tensor(S[:, :, 0:n], PS[:, 0:4, 0:n], DH ** -0.5,
                                                   e.bc(band.unsqueeze(1), P, 4, n), ALU.mult, ALU.add))
                else:
                    e.vlink(V.tensor_scalar(S[:, :, 0:n], PS[:, 0:4, 0:n], DH ** -0.5, None, ALU.mult))
                e.vlink(V.reduce_max(mx[:, 0], S[:, :, 0:n], AX))
                e.vlink(V.tensor_tensor(mx[:, 0], mx[:, 0], sink, ALU.max))
                e.vlink(V.tensor_scalar(mx[:, 1], mx[:, 0], -1.0, None, ALU.mult))
                V.tensor_tensor(mx[:, 2], sink, mx[:, 0], ALU.subtract).then_inc(s_m, 1)
                dve.wait_ge(s_ex, u + 1)
                e.vlink(V.tensor_tensor(mx[:, 4], mx[:, 3], mx[:, 5], ALU.add))
                e.vlink(V.reciprocal(mx[:, 4], mx[:, 4]))
                dve.wait_ge(s_tr, u + 1)
                V.tensor_copy(PT[:, 0:2, 0:n // P].rearrange("p h k q -> p h (k q)"),
                              PS[:, 4:6, 0:n]).then_inc(s_pt, 1)
                dve.wait_ge(s_pv, u + 1)
                V.tensor_tensor(O[:, (u // 2) % 2, 4 * g:4 * g + 4], PS[:, 0, 0:4 * DH].rearrange("p (h d) -> p h d", h=4),
                                e.bc(mx[:, 4].unsqueeze(2), P, 4, DH), ALU.mult).then_inc(s_o, 1)
                if g == 1:
                    dve.wait_ge(s_ot, u // 2 + 1)
                    V.tensor_copy(m.aqT[:, :, t * P:t * P + P],
                                  PS[:, 1, :].rearrange("p (j q) -> p j q", j=4)).then_inc(s_oev, 1)

        @block.scalar
        def _(act):
            for u, (t, g) in enumerate(units):
                n = nk(t)
                act.wait_ge(s_m, u + 1)
                for h in range(4):
                    A.activation(S[:, h, 0:n], S[:, h, 0:n], ACT.Exp, bias=mx[:, 1, h:h + 1], accum_out=mx[:, 3, h:h + 1])
                A.activation(mx[:, 5], mx[:, 2], ACT.Exp).then_inc(s_ex, 1)
                act.wait_ge(s_tr, u + 1)
                A.activation(PT[:, 2:4, 0:n // P].rearrange("p h k q -> p h (k q)"), PS[:, 6:8, 0:n],
                             ACT.Copy).then_inc(s_pt, 1)


def attn_b_stage(nc, a, e, m, l, tiles):
    V, A, T, PS, sem = e.V, e.A, e.T, e.PS, e.sem
    lam_init = 0.8 - 0.6 * math.exp(-0.3 * l)
    with ExitStack() as st, nc.Block() as block:
        E = e.sb(st, f"b_probs{l}", [P, 2, 4, NTOK])
        O = e.sb(st, f"b_out{l}", [P, 4, P])
        mx = e.sb(st, f"b_stats{l}", [P, 8, 4])
        lam = e.sb(st, f"lam{l}", [P, 4])
        lt = e.sb(st, f"lam_tmp{l}", [P, 2, DH])
        gd = e.sb(st, f"g_diff_scaled{l}", [P, P])
        s_sc, s_m, s_ex, s_at, s_tr, s_pt, s_pv, s_o, s_ot, s_oev, s_l1, s_l2 = (sem(f"{n}{l}") for n in (
            "b_scores", "b_max", "b_exp", "b_att_ready", "b_transposed", "b_probsT_ready", "b_pv", "b_out_ready",
            "b_outT", "b_outT_stored", "lam_sums", "lam_exps"))
        PT = E[:, 1].rearrange("p h (k q) -> p h k q", k=4)
        s_ms, s_rs = sem(f"b_mean_square{l}"), sem(f"b_inv_rms{l}")

        def nk(t):
            return NTOK if t >= LAT0 else NCTX

        @block.tensor
        def _(pe):
            for u, t in enumerate(tiles):
                n = nk(t)
                if u >= 1:
                    pe.wait_ge(s_oev, u)
                for s in range(2):
                    for h in range(4):
                        last = T.matmul(PS[:, 4 * s + h, 0:n], m.bqT[s * DH:s * DH + DH, h, t * P:t * P + P],
                                        m.bkT[s * DH:s * DH + DH, h, 0:n], start=True, stop=True)
                    last.then_inc(s_sc, 1)
                pe.wait_ge(s_at, u + 1)
                for h in range(4):
                    for k in range(n // P):
                        last = T.transpose(PS[:, 4 + h, k * P:k * P + P], E[:, 0, h, k * P:k * P + P], e.ident)
                last.then_inc(s_tr, 1)
                pe.wait_ge(s_pt, 2 * u + 2)
                for h in range(4):
                    for k in range(n // P):
                        last = T.matmul(PS[:, 0, h * P:h * P + P], PT[:, h, k, :],
                                        m.bv[:, k, h * P:h * P + P], start=k == 0, stop=k == n // P - 1)
                last.then_inc(s_pv, 1)
                pe.wait_ge(s_o, u + 1)
                for j in range(4):
                    last = T.transpose(PS[:, 1, j * P:j * P + P], O[:, j], e.ident)
                last.then_inc(s_ot, 1)

        @block.vector
        def _(dve):
            lr = e.rowp[:, R_LAM:R_LAM + 4 * DH].rearrange("p (a b d) -> p a b d", a=2, b=2)
            e.vlink(V.tensor_tensor(lt[:], lr[:, :, 0], lr[:, :, 1], ALU.mult))
            V.reduce_sum(lam[:, 0:2], lt[:], AX).then_inc(s_l1, 1)
            dve.wait_ge(s_l2, 1)
            e.vlink(V.tensor_tensor(lam[:, 2:3], lam[:, 0:1], lam[:, 1:2], ALU.subtract))
            e.vlink(V.tensor_scalar(lam[:, 2:3], lam[:, 2:3], lam_init, None, ALU.add))
            e.vlink(V.tensor_scalar(gd[:], e.rowp[:, R_GDIFF:R_GDIFF + P], 1.0 - lam_init, None, ALU.mult))
            for u, t in enumerate(tiles):
                n = nk(t)
                for s in range(2):
                    dve.wait_ge(s_sc, 2 * u + s + 1)
                    e.vlink(V.reduce_max(mx[:, s], PS[:, 4 * s:4 * s + 4, 0:n], AX))
                    V.tensor_scalar(mx[:, s], mx[:, s], -DH ** -0.5, None, ALU.mult).then_inc(s_m, 1)
                dve.wait_ge(s_ex, 2 * u + 2)
                e.vlink(V.reciprocal(mx[:, 4:6], mx[:, 2:4]))
                e.vlink(V.tensor_tensor(mx[:, 6], mx[:, 2], mx[:, 5], ALU.mult))
                e.vlink(V.tensor_scalar(mx[:, 6], mx[:, 6], lam[:, 2:3], -1.0, ALU.mult, ALU.mult))
                for h in range(4):
                    last = V.scalar_tensor_tensor(E[:, 0, h, 0:n], E[:, 1, h, 0:n], mx[:, 6, h:h + 1],
                                                  E[:, 0, h, 0:n], ALU.mult, ALU.add)
                last.then_inc(s_at, 1)
                dve.wait_ge(s_tr, u + 1)
                V.tensor_copy(PT[:, 0:2, 0:n // P].rearrange("p h k q -> p h (k q)"), PS[:, 4:6, 0:n]).then_inc(s_pt, 1)
                dve.wait_ge(s_pv, u + 1)
                e.vlink(V.tensor_tensor(O[:], PS[:, 0, :].rearrange("p (h d) -> p h d", h=4),
                                        e.bc(mx[:, 4].unsqueeze(2), P, 4, P), ALU.mult))
                sq = E[:, 0, :, 0:P]
                e.vlink(V.tensor_tensor(sq, O[:], O[:], ALU.mult))
                e.vlink(V.reduce_sum(mx[:, 7], sq, AX))
                V.tensor_scalar(mx[:, 7], mx[:, 7], 1.0 / P, None, ALU.mult).then_inc(s_ms, 1)
                dve.wait_ge(s_rs, u + 1)
                e.vlink(V.reciprocal(mx[:, 7], mx[:, 7]))
                e.vlink(V.tensor_tensor(O[:], O[:], e.bc(mx[:, 7].unsqueeze(2), P, 4, P), ALU.mult))
                V.tensor_tensor(O[:], O[:], e.bc(gd[:].unsqueeze(1), P, 4, P), ALU.mult).then_inc(s_o, 1)
                dve.wait_ge(s_ot, u + 1)
                V.tensor_copy(m.bqT[:, :, t * P:t * P + P],
                              PS[:, 1, :].rearrange("p (j q) -> p j q", j=4)).then_inc(s_oev, 1)

        @block.scalar
        def _(act):
            act.wait_ge(s_l1, 1)
            A.activation(lam[:, 0:2], lam[:, 0:2], ACT.Exp).then_inc(s_l2, 1)
            for u, t in enumerate(tiles):
                n = nk(t)
                if u >= 1:
                    act.wait_ge(s_o, u)
                for s in range(2):
                    act.wait_ge(s_m, 2 * u + s + 1)
                    for h in range(4):
                        last = A.activation(E[:, s, h, 0:n], PS[:, 4 * s + h, 0:n], ACT.Exp, bias=mx[:, s, h:h + 1],
                                            scale=DH ** -0.5, accum_out=mx[:, 2 + s, h:h + 1])
                    last.then_inc(s_ex, 1)
                act.wait_ge(s_tr, u + 1)
                A.activation(PT[:, 2:4, 0:n // P].rearrange("p h k q -> p h (k q)"), PS[:, 6:8, 0:n],
                             ACT.Copy).then_inc(s_pt, 1)
                act.wait_ge(s_ms, u + 1)
                A.activation(mx[:, 7], mx[:, 7], ACT.Sqrt, bias=e.eps).then_inc(s_rs, 1)


def mlstm_stage(nc, a, e, m, l, tiles):
    V, A, T, PS, sem = e.V, e.A, e.T, e.PS, e.sem
    steps = [(d, t) for d, order in ((0, (0, 1, 2, 3)), (1, (1, 0, 3, 2))) for t in order]
    outs = [(u, d, t) for u, (d, t) in enumerate(steps) if t in tiles]
    H = m.bkT[:]
    Q = P + 1
    with ExitStack() as st, nc.Block() as block:
        gates = e.sb(st, f"gates{l}", [P, TT, 4, 4])
        logf = e.sb(st, f"logf{l}", [P, TT, 2, 4])
        C = e.sb(st, f"c_state{l}", [P, 4, Q])
        dg = e.sb(st, f"diag{l}", [P, 4, P])
        dm = e.sb(st, f"decay{l}", [P, 4, P])
        PT = e.sb(st, f"c_probsT{l}", [P, 4, P])
        wk = e.sb(st, f"wk{l}", [P, 4, P])
        num = e.sb(st, f"num{l}", [P, 4, Q])
        z = e.sb(st, f"c_stats{l}", [P, 16, 4])
        names = ("f_in", "f_out", "c_cum", "c_r", "c_rbc", "c_maxes", "c_exps", "c_scores", "c_dexp", "c_probs", "c_transposed",
                 "c_probsT_ready", "c_nums", "c_state_done", "c_wk", "c_dstate", "c_num_done")
        (s_f1, s_f2, s_cum, s_r, s_rbc, s_mx, s_ex, s_sc, s_de, s_p, s_tr, s_pt, s_nm, s_st, s_wk, s_ds,
         s_nd) = (sem(f"{n}{l}") for n in names)
        (BCUM, BLAST, RR, MAXR, MAXD, MST, UU, WW, AIN, DECAY, WKE, EXM, DEN, NEW, TMP, TMP2) = range(16)

        def heads(ap):
            return ap.rearrange("p (h d) -> p h d", h=4)

        def num_bank(b, h):
            return PS[:, b + h // 2, (h % 2) * Q:(h % 2) * Q + Q]

        def num_pair(b, i):
            return PS[:, b + i, 0:2 * Q].rearrange("p (h q) -> p h q", h=2)

        @block.tensor
        def _(pe):
            o = 0
            for u, (d, t) in enumerate(steps):
                out = t in tiles
                tri = e.cst[:, (C_LE if d == 0 else C_GE):(C_LE if d == 0 else C_GE) + P]
                if u == 0:
                    pe.wait_ge(s_f2, 2)
                if u >= 1:
                    pe.wait_ge(s_st, u)
                T.matmul(PS[:, 2, 0:4], tri, logf[:, t, d], start=True, stop=True)
                T.matmul(PS[:, 2, 4:8], e.ones, logf[:, t, d], start=True, stop=True).then_inc(s_cum, 1)
                if out:
                    for h in range(4):
                        last = T.matmul(PS[:, 1, h * P:h * P + P], m.cqT[:, h, t * P:t * P + P],
                                        m.ckT[:, h, t * P:t * P + P], start=True, stop=True)
                    last.then_inc(s_sc, 1)
                    for h in range(4):
                        last = T.matmul(num_bank(6, h), m.cqT[:, h, t * P:t * P + P], C[:, h], start=True, stop=True)
                pe.wait_ge(s_r, u + 1)
                T.matmul(PS[:, 0, :], e.ones, dg[:].rearrange("p h s -> p (h s)"), start=True, stop=True
                         ).then_inc(s_rbc, 1)
                if out:
                    pe.wait_ge(s_p, o + 1)
                    for h in range(4):
                        last = T.transpose(PS[:, 3, h * P:h * P + P], dm[:, h], e.ident)
                    last.then_inc(s_tr, 1)
                    pe.wait_ge(s_pt, o + 1)
                    for h in range(4):
                        last = T.matmul(num_bank(4, h), PT[:, h], m.cv[:, t, h], start=True, stop=True)
                    last.then_inc(s_nm, 1)
                    o += 1
                    pe.wait_ge(s_nd, o)
                pe.wait_ge(s_wk, u + 1)
                for h in range(4):
                    last = T.matmul(num_bank(4, h), wk[:, h], m.cv[:, t, h], start=True, stop=True)
                last.then_inc(s_ds, 1)

        @block.vector
        def _(dve):
            bg = e.rowp[:, R_BGATE:R_BGATE + 16]
            e.vlink(V.tensor_tensor(gates[:].rearrange("p t g h -> p t (g h)"), m.misc[:, :, P:P + 16],
                                    e.bc(bg.unsqueeze(1), P, TT, 16), ALU.add))
            f = gates[:].rearrange("p t (d i) h -> p t d i h", i=2)[:, :, :, 1]
            e.vlink(V.tensor_scalar(logf[:], f, -1.0, None, ALU.mult))
            V.tensor_tensor(logf[:], logf[:], f, ALU.min).then_inc(s_f1, 1)
            dve.wait_ge(s_f2, 1)
            e.vlink(V.tensor_scalar(dm[:, 0, 0:32].rearrange("p (t d h) -> p t d h", t=TT, d=2), f, 0.0, None, ALU.min))
            e.vlink(V.tensor_tensor(logf[:], dm[:, 0, 0:32].rearrange("p (t d h) -> p t d h", t=TT, d=2), logf[:],
                                    ALU.subtract))
            V.memset(C[:], 0.0).then_inc(s_f2, 1)
            o = 0
            for u, (d, t) in enumerate(steps):
                out = t in tiles
                if u in (0, 4):
                    e.vlink(V.memset(z[:] if u == 0 else z[:, MST], 0.0))
                dve.wait_ge(s_cum, u + 1)
                e.vlink(V.tensor_copy(z[:, BCUM:BCUM + 2].rearrange("p a h -> p (a h)"), PS[:, 2, 0:8]))
                e.vlink(V.tensor_tensor(z[:, RR], gates[:, t, 2 * d], z[:, BCUM], ALU.subtract))
                V.tensor_tensor(dg[:], e.bc(e.ident.unsqueeze(1), P, 4, P), e.bc(z[:, RR].unsqueeze(2), P, 4, P),
                                ALU.mult).then_inc(s_r, 1)
                dve.wait_ge(s_rbc, u + 1)
                rb = heads(PS[:, 0, :])
                e.vlink(V.reduce_max(z[:, MAXR], rb, AX))
                e.vlink(V.tensor_tensor(z[:, WW], z[:, MST], z[:, MAXR], ALU.max))
                if out:
                    mask = e.cst[:, (C_MF if d == 0 else C_MB):(C_MF if d == 0 else C_MB) + P]
                    e.vlink(V.tensor_tensor(dm[:], rb, e.bc(mask.unsqueeze(1), P, 4, P), ALU.add))
                    e.vlink(V.reduce_max(z[:, MAXD], dm[:], AX))
                    e.vlink(V.tensor_tensor(z[:, UU], z[:, MST], z[:, MAXD], ALU.max))
                    V.tensor_tensor(dm[:], dm[:], e.bc(z[:, UU].unsqueeze(2), P, 4, P), ALU.subtract)
                    V.tensor_tensor(z[:, AIN], z[:, MST], z[:, UU], ALU.subtract)
                    e.vlink(V.tensor_tensor(z[:, TMP], z[:, BCUM], z[:, UU], ALU.add))
                    V.tensor_scalar(z[:, EXM], z[:, TMP], -1.0, None, ALU.mult)
                V.tensor_tensor(z[:, DECAY], z[:, MST], z[:, WW], ALU.subtract)
                V.tensor_tensor(z[:, WKE], z[:, RR], z[:, WW], ALU.subtract).then_inc(s_mx, 1)
                dve.wait_ge(s_ex, u + 1)
                e.vlink(V.tensor_tensor(z[:, MST], z[:, BLAST], z[:, WW], ALU.add))
                if out:
                    dve.wait_ge(s_sc, o + 1)
                    V.tensor_tensor(dm[:], heads(PS[:, 1, :]), dm[:], ALU.mult).then_inc(s_p, 1)
                V.tensor_tensor(wk[:], heads(m.ck[:, t]), e.bc(z[:, WKE].unsqueeze(2), P, 4, P), ALU.mult
                                ).then_inc(s_wk, 1)
                if out:
                    dve.wait_ge(s_nm, o + 1)
                    for i in range(2):
                        e.vlink(V.tensor_tensor(num[:, 2 * i:2 * i + 2], num_pair(6, i),
                                                e.bc(z[:, AIN, 2 * i:2 * i + 2].unsqueeze(2), P, 2, Q), ALU.mult))
                        last = V.tensor_tensor(num[:, 2 * i:2 * i + 2], num[:, 2 * i:2 * i + 2], num_pair(4, i), ALU.add)
                    o += 1
                    last.then_inc(s_nd, 1)
                    dve.wait_ge(s_nd, o)
                    den = num[:, :, P]
                    e.vlink(V.tensor_scalar(z[:, TMP], den, -1.0, None, ALU.mult))
                    e.vlink(V.tensor_tensor(z[:, TMP], z[:, TMP], den, ALU.max))
                    e.vlink(V.tensor_tensor(z[:, TMP], z[:, TMP], z[:, EXM], ALU.max))
                    e.vlink(V.reciprocal(z[:, DEN], z[:, TMP]))
                    hs = H[:, t, :].rearrange("p (h d) -> p h d", h=4)
                    if d == 0:
                        V.tensor_tensor(hs, num[:, :, 0:P], e.bc(z[:, DEN].unsqueeze(2), P, 4, P), ALU.mult)
                    else:
                        e.vlink(V.tensor_tensor(num[:, :, 0:P], num[:, :, 0:P], e.bc(z[:, DEN].unsqueeze(2), P, 4, P),
                                                ALU.mult))
                        V.tensor_tensor(hs, hs, num[:, :, 0:P], ALU.add)
                if u == 3:
                    dve.wait_ge(s_ds, u + 1)
                    V.memset(C[:], 0.0).then_inc(s_st, 1)
                    continue
                e.vlink(V.tensor_tensor(C[:], C[:], e.bc(z[:, DECAY].unsqueeze(2), P, 4, Q), ALU.mult))
                dve.wait_ge(s_ds, u + 1)
                V.tensor_tensor(C[:, 0:2], C[:, 0:2], num_pair(4, 0), ALU.add)
                V.tensor_tensor(C[:, 2:4], C[:, 2:4], num_pair(4, 1), ALU.add).then_inc(s_st, 1)
                dve.wait_ge(s_st, u + 1)

        @block.scalar
        def _(act):
            act.wait_ge(s_f1, 1)
            e.alink(A.activation(logf[:], logf[:], ACT.Exp))
            A.activation(logf[:], logf[:], ACT.Ln, bias=1.0).then_inc(s_f2, 1)
            o = 0
            for u, (d, t) in enumerate(steps):
                out = t in tiles
                act.wait_ge(s_mx, u + 1)
                if out:
                    A.activation(dm[:], dm[:], ACT.Exp)
                A.activation(z[:, AIN:EXM + 1], z[:, AIN:EXM + 1], ACT.Exp).then_inc(s_ex, 1)
                if out:
                    act.wait_ge(s_tr, o + 1)
                    A.activation(PT[:].rearrange("p h t -> p (h t)"), PS[:, 3, :], ACT.Copy).then_inc(s_pt, 1)
                    o += 1

    with ExitStack() as st, nc.Block() as block:
        sg = e.sb(st, f"sig_o{l}", [P, 2, 512])
        sq = e.sb(st, f"c_sq{l}", [P, 4, P])
        ms = e.sb(st, f"c_ms{l}", [P, TT, 4])
        t0 = tiles[0]
        s_co, s_sg, s_oc, s_ot, s_oev = (sem(f"{n}{l}") for n in (
            "co_done", "co_sigmoid", "oc_ready", "ocT", "ocT_stored"))
        base = l * NCHUNK
        e.freed[base + CO] = (s_co, len(tiles))
        s_ms, s_rs = sem(f"c_mean_square{l}"), sem(f"c_inv_rms{l}")

        @block.sync
        def _(sp):
            e.sp_loads(sp, base + CO + 1 + RING)

        @block.tensor
        def _(pe):
            w = e.chunk_ready(pe, base + CO)

            def back(i, t):
                pe.wait_ge(s_oc, i + 1)
                if i >= 2:
                    pe.wait_ge(s_oev, i - 1)
                for j in range(4):
                    last = T.transpose(PS[:, 4 + i % 2, j * P:j * P + P], H[:, t, j * P:j * P + P], e.ident)
                last.then_inc(s_ot, 1)

            for i, t in enumerate(tiles):
                for k in range(KT):
                    last = T.matmul(PS[:, i, :], e.hT[:, k, t * P:t * P + P], w[:, k * 512:k * 512 + 512],
                                    start=k == 0, stop=k == KT - 1)
                last.then_inc(s_co, 1)
                if i >= 1:
                    back(i - 1, tiles[i - 1])
            back(len(tiles) - 1, tiles[-1])

        @block.scalar
        def _(act):
            act.wait_ge(s_ms, 1)
            A.activation(ms[:, t0:TT], ms[:, t0:TT], ACT.Sqrt, bias=e.eps).then_inc(s_rs, 1)
            for i, t in enumerate(tiles):
                act.wait_ge(s_co, i + 1)
                if i >= 2:
                    act.wait_ge(s_oc, i - 1)
                A.activation(sg[:, i % 2], PS[:, i, :], ACT.Sigmoid).then_inc(s_sg, 1)

        @block.vector
        def _(dve):
            gm = e.rowp[:, R_GMLSTM:R_GMLSTM + 512]
            for t in tiles:
                hs = heads(H[:, t, :])
                e.vlink(V.tensor_tensor(sq[:], hs, hs, ALU.mult))
                e.vlink(V.reduce_sum(ms[:, t], sq[:], AX))
            V.tensor_scalar(ms[:, t0:TT], ms[:, t0:TT], 1.0 / P, None, ALU.mult).then_inc(s_ms, 1)
            dve.wait_ge(s_rs, 1)
            e.vlink(V.reciprocal(ms[:, t0:TT], ms[:, t0:TT]))
            for i, t in enumerate(tiles):
                hs = heads(H[:, t, :])
                e.vlink(V.tensor_tensor(hs, hs, e.bc(ms[:, t].unsqueeze(2), P, 4, P), ALU.mult))
                e.vlink(V.tensor_tensor(H[:, t, :], H[:, t, :], gm, ALU.mult))
                dve.wait_ge(s_sg, i + 1)
                V.tensor_tensor(H[:, t, :], H[:, t, :], sg[:, i % 2], ALU.mult).then_inc(s_oc, 1)
                dve.wait_ge(s_ot, i + 1)
                V.tensor_copy(m.cqT[:, :, t * P:t * P + P],
                              PS[:, 4 + i % 2, :].rearrange("p (j q) -> p j q", j=4)).then_inc(s_oev, 1)


def gate_rows(nc, e, l, which, dst, tag):
    V, A, T, PS, sem = e.V, e.A, e.T, e.PS, e.sem
    vs = [0, 1] if l < L - 1 else [1]
    with ExitStack() as st, nc.Block() as block:
        dg = e.sb(st, f"row_diag_{tag}{l}", [P, 2, 4, P])
        s_dg, s_row, s_rs = sem(f"row_diag_ready_{tag}{l}"), sem(f"row_done_{tag}{l}"), sem(f"row_stored_{tag}{l}")
        jobs = [(v, j) for v in vs for j in range(2)]

        @block.vector
        def _(dve):
            for i, (v, j) in enumerate(jobs):
                if i >= 2:
                    dve.wait_ge(s_row, i - 1)
                V.tensor_tensor(dg[:, i % 2], e.bc(e.ident.unsqueeze(1), P, 4, P),
                                e.bc(e.modc[:, which, 4 * j:4 * j + 4, v:v + 1], P, 4, P), ALU.mult).then_inc(s_dg, 1)

        @block.tensor
        def _(pe):
            for i, (v, j) in enumerate(jobs):
                pe.wait_ge(s_dg, i + 1)
                T.matmul(PS[:, i, :], e.ones, dg[:, i % 2].rearrange("p k n -> p (k n)"), start=True, stop=True
                         ).then_inc(s_row, 1)

        @block.scalar
        def _(act):
            for i, (v, j) in enumerate(jobs):
                act.wait_ge(s_row, i + 1)
                A.activation(dst[:, v, j * 512:j * 512 + 512], PS[:, i, :], ACT.Copy)


def merge_stage(nc, a, e, m, l, tiles):
    V, A, T, PS, sem = e.V, e.A, e.T, e.PS, e.sem
    base = l * NCHUNK
    with ExitStack() as st:
        rows = e.sb(st, f"mix_rows{l}", [P, 2, D])
        gate_rows(nc, e, l, 2, rows, "mix")
        Y = m.bkT[:]
        Y2 = m.ckT[:]
        YY = [Y, Y2]
        with nc.Block() as block:
            sg = e.sb(st, f"sig_g{l}", [P, 2, 512])
            s_g, s_b, s_sg, s_y = (sem(f"{n}{l}") for n in ("gate_done", "branch_done", "gate_sigmoid", "y_updated"))
            units = [(j, b, t) for j in range(2) for b in range(3) for t in tiles]
            srcs = [m.aqT, m.bqT, m.cqT]
            nt = len(tiles)
            for c in range(6):
                e.freed[base + MERGE0 + c] = (s_b, nt * (c + 1))

            @block.sync
            def _(sp):
                e.sp_loads(sp, base + OUT0 + RING)

            @block.tensor
            def _(pe):
                for u, (j, b, t) in enumerate(units):
                    w = e.chunk_ready(pe, base + MERGE0 + 3 * j + b)
                    if u >= 2:
                        pe.wait_ge(s_y, u - 1)
                    for k in range(KT):
                        last = T.matmul(PS[:, u % 2, :], e.hT[:, k, t * P:t * P + P], w[:, k * 512:k * 512 + 512],
                                        start=k == 0, stop=k == KT - 1)
                    last.then_inc(s_g, 1)
                    for k in range(4):
                        at = KT * 512 + k * 512
                        last = T.matmul(PS[:, 2 + u % 2, :], srcs[b][:, k, t * P:t * P + P], w[:, at:at + 512],
                                        start=k == 0, stop=k == 3)
                    last.then_inc(s_b, 1)

            @block.scalar
            def _(act):
                for u in range(len(units)):
                    act.wait_ge(s_g, u + 1)
                    if u >= 2:
                        act.wait_ge(s_y, u - 1)
                    A.activation(sg[:, u % 2], PS[:, u % 2, :], ACT.Sigmoid).then_inc(s_sg, 1)

            @block.vector
            def _(dve):
                for u, (j, b, t) in enumerate(units):
                    dve.wait_ge(s_sg, u + 1)
                    dve.wait_ge(s_b, u + 1)
                    if b == 0:
                        V.tensor_tensor(YY[j][:, t], PS[:, 2 + u % 2, :], sg[:, u % 2], ALU.mult).then_inc(s_y, 1)
                    else:
                        e.vlink(V.tensor_tensor(sg[:, u % 2], PS[:, 2 + u % 2, :], sg[:, u % 2], ALU.mult))
                        V.tensor_tensor(YY[j][:, t], YY[j][:, t], sg[:, u % 2], ALU.add).then_inc(s_y, 1)

        with nc.Block() as block:
            s_yt, s_ys, s_out, s_xu, s_om = (sem(f"{n}{l}") for n in (
                "yT", "yT_stored", "out_done", "x_updated", "out_gated"))
            YT = [m.aqT, m.bqT]
            og = e.sb(st, f"out_gated{l}", [P, 2, 512])
            for j in range(2):
                e.freed[base + OUT0 + j] = (s_out, nt * (j + 1))

            @block.sync
            def _(sp):
                e.sp_loads(sp, base + NCHUNK)

            @block.tensor
            def _(pe):
                i = 0
                for t in tiles:
                    for j in range(2):
                        if i >= 4:
                            pe.wait_ge(s_ys, i - 3)
                        for k in range(4):
                            last = T.transpose(PS[:, i % 4, k * P:k * P + P], YY[j][:, t, k * P:k * P + P], e.ident)
                        last.then_inc(s_yt, 1)
                        i += 1
                pe.wait_ge(s_ys, i)
                for u, (j, t) in enumerate((j, t) for j in range(2) for t in tiles):
                    w = e.chunk_ready(pe, base + OUT0 + j)
                    if u >= 4:
                        pe.wait_ge(s_om, u - 3)
                    for k in range(KT):
                        last = T.matmul(PS[:, 4 + u % 4, :], YT[k // 4][:, k % 4, t * P:t * P + P],
                                        w[:, k * 512:k * 512 + 512], start=k == 0, stop=k == KT - 1)
                    last.then_inc(s_out, 1)

            @block.scalar
            def _(act):
                i = 0
                for t in tiles:
                    for j in range(2):
                        act.wait_ge(s_yt, i + 1)
                        A.activation(YT[j][:, :, t * P:t * P + P], PS[:, i % 4, :].rearrange("p (k q) -> p k q", k=4),
                                     ACT.Copy).then_inc(s_ys, 1)
                        i += 1

            @block.vector
            def _(dve):
                for u, (j, t) in enumerate((j, t) for j in range(2) for t in tiles):
                    v = 0 if t < LAT0 else 1
                    dve.wait_ge(s_out, u + 1)
                    V.tensor_tensor(og[:, u % 2], PS[:, 4 + u % 4, :], rows[:, v, j * 512:j * 512 + 512],
                                    ALU.mult).then_inc(s_om, 1)
                    dve.wait_ge(s_om, u + 1)
                    xs = e.X[:, t, j * 512:j * 512 + 512]
                    V.tensor_tensor(xs, xs, og[:, u % 2], ALU.add).then_inc(s_xu, 1)


def moe(nc, a, e, l, tiles):
    with ExitStack() as st:
        slots = [e.ring[0], e.ring[1]] + [e.sb(st, f"weights{i}_{l}", [P, SLOT]) for i in range(RING, NSLOT)]
        nt = len(tiles)
        r = Space()
        r.shared = e.sb(st, f"shared_out{l}", [P, nt, D])
        r.rows = e.sb(st, f"moe_rows{l}", [P, 2, D])
        r.weight = e.sb(st, f"route_weight{l}", [P, nt, TOPK])
        r.yrow = e.sb(st, f"y_row_index{l}", [P, nt, TOPK], I32)
        r.posb = e.sb(st, f"slot_position{l}", [P, NBLK, nt, NE])
        r.tokid = e.sb(st, f"token_id{l}", [P, nt], FP16)
        r.tok = e.sb(st, f"slot_token{l}", [P, NE], I32)
        r.over = e.sb(st, f"overflow_table{l}", [1, 3, P], I32)
        r.gate = e.sb(st, f"route_gate{l}", [P, nt, NE])
        gate_rows(nc, e, l, 5, r.rows, "moe")
        with ExitStack() as st2:
            S = e.sb(st2, f"scores{l}", [P, nt, NE])
            shared_stage(nc, a, e, r, l, tiles, S)
            route_stage(nc, a, e, r, l, tiles, S, slots)
        with ExitStack() as st2:
            b = Space()
            b.xg = e.sb(st2, f"gathered{l}", [P, 2, D])
            b.xT = e.sb(st2, f"gatheredT{l}", [P, 2, KT, P])
            b.sl = e.sb(st2, f"silu{l}", [P, 2, DE])
            b.ac = e.sb(st2, f"act{l}", [P, 2, DE])
            b.acT = e.sb(st2, f"actT{l}", [P, 2, 2, P])
            b.y = e.sb(st2, f"expert_out{l}", [P, 2, D])
            b.idx = e.sb(st2, f"gather_index{l}", [P, 2], I32)
            experts_stage(nc, a, e, r, b, l, slots)
            overflow_stage(nc, a, e, r, b, l, nt, slots)
        combine_stage(nc, a, e, r, l, tiles)


def shared_stage(nc, a, e, r, l, tiles, S):
    V, A, T, PS, sem = e.V, e.A, e.T, e.PS, e.sem
    n = l * NCHUNK + SHARED0
    with ExitStack() as st, nc.Block() as block:
        wr = e.sb(st, f"w_router{l}", [P, KT * NE])
        ht = e.sb(st, f"h_token_form{l}", [P, 2, D])
        sl = e.sb(st, f"sh_silu{l}", [P, 2, DE])
        ac = e.sb(st, f"sh_act{l}", [P, 2, DE])
        acT = e.sb(st, f"sh_actT{l}", [P, 2, 2, P])
        s_wr, s_rt, s_ht, s_hta, s_g, s_sl, s_ac, s_h, s_at, s_dn, s_ya = (sem(f"{x}{l}") for x in (
            "w_router_loaded", "router_done", "h_transposed", "h_token_ready", "sh_gate_up", "sh_silu_done",
            "sh_act_ready", "sh_act_transposed", "sh_actT_ready", "sh_down", "sh_stored"))
        s_hs = [sem(f"h_rows_written{i}_{l}") for i in range(2)]
        e.freed[n] = (s_dn, len(tiles))

        @block.sync
        def _(sp):
            sp.dma_start(wr[:], a["wr"][l]).then_inc(s_wr, 16)
            for i, t in enumerate(tiles):
                sp.wait_ge(s_hta, 2 * i + 2)
                sp.dma_start(a["h_rows"][t * P:t * P + P, :], ht[:, i % 2]).then_inc(s_hs[i % 2], 16)
            for i in range(2):
                sp.wait_ge(s_hs[i], 16 * (len(tiles) // 2))

        @block.tensor
        def _(pe):
            pe.wait_ge(s_wr, 16)
            for i, t in enumerate(tiles):
                for k in range(KT):
                    last = T.matmul(PS[:, 7, i * NE:i * NE + NE], e.hT[:, k, t * P:t * P + P],
                                    wr[:, k * NE:k * NE + NE], start=k == 0, stop=k == KT - 1)
            last.then_inc(s_rt, 1)
            w = e.chunk_ready(pe, n)
            for i, t in enumerate(tiles):
                if i >= 1:
                    pe.wait_ge(s_hta, 2 * i)
                for k in range(KT):
                    last = T.transpose(PS[:, k // 4, (k % 4) * P:(k % 4) * P + P], e.hT[:, k, t * P:t * P + P], e.ident)
                last.then_inc(s_ht, 1)
                if i >= 2:
                    pe.wait_ge(s_ac, i - 1)
                for k in range(KT):
                    last = T.matmul(PS[:, 2 + i % 2, :], e.hT[:, k, t * P:t * P + P], w[:, k * 512:k * 512 + 512],
                                    start=k == 0, stop=k == KT - 1)
                last.then_inc(s_g, 1)
                pe.wait_ge(s_ac, i + 1)
                for k in range(2):
                    last = T.transpose(PS[:, 6, k * P:k * P + P], ac[:, i % 2, k * P:k * P + P], e.ident)
                last.then_inc(s_h, 1)
                pe.wait_ge(s_at, i + 1)
                if i >= 1:
                    pe.wait_ge(s_ya, 2 * i)
                for j in range(2):
                    for k in range(2):
                        at = KT * 512 + k * D + j * 512
                        last = T.matmul(PS[:, 4 + j, :], acT[:, i % 2, k], w[:, at:at + 512], start=k == 0, stop=k == 1)
                last.then_inc(s_dn, 1)

        @block.scalar
        def _(act):
            act.wait_ge(s_rt, 1)
            A.activation(S[:].rearrange("p t e -> p (t e)"), PS[:, 7, 0:len(tiles) * NE], ACT.Sigmoid)
            for i, t in enumerate(tiles):
                act.wait_ge(s_ht, i + 1)
                if i >= 2:
                    act.wait_ge(s_hs[i % 2], 16 * (i // 2))
                A.activation(ht[:, i % 2, 0:512], PS[:, 0, :], ACT.Copy).then_inc(s_hta, 1)
                act.wait_ge(s_g, i + 1)
                A.activation(sl[:, i % 2], PS[:, 2 + i % 2, 0:DE], ACT.Silu).then_inc(s_sl, 1)
                act.wait_ge(s_dn, i + 1)
                A.activation(r.shared[:, i, 0:512], PS[:, 4, :], ACT.Copy).then_inc(s_ya, 1)

        @block.vector
        def _(dve):
            for i, t in enumerate(tiles):
                dve.wait_ge(s_ht, i + 1)
                if i >= 2:
                    dve.wait_ge(s_hs[i % 2], 16 * (i // 2))
                V.tensor_copy(ht[:, i % 2, 512:D], PS[:, 1, :]).then_inc(s_hta, 1)
                dve.wait_ge(s_sl, i + 1)
                V.tensor_tensor(ac[:, i % 2], sl[:, i % 2], PS[:, 2 + i % 2, DE:2 * DE], ALU.mult).then_inc(s_ac, 1)
                dve.wait_ge(s_h, i + 1)
                V.tensor_copy(acT[:, i % 2].rearrange("p k t -> p (k t)"), PS[:, 6, 0:2 * P]).then_inc(s_at, 1)
                dve.wait_ge(s_dn, i + 1)
                V.tensor_copy(r.shared[:, i, 512:D], PS[:, 5, :]).then_inc(s_ya, 1)


def route_stage(nc, a, e, r, l, tiles, S, slots):
    V, A, T, PS, sem = e.V, e.A, e.T, e.PS, e.sem
    nt = len(tiles)
    iota = e.iota
    EC = 4
    with ExitStack() as st, nc.Block() as block:
        sel = e.sb(st, f"sel{l}", [P, nt, NE])
        top = e.sb(st, f"group_top{l}", [P, nt, NG, 8])
        gs = e.sb(st, f"group_score{l}", [P, nt, NG])
        v8 = e.sb(st, f"top_values{l}", [P, nt, 8])
        i8 = e.sb(st, f"top_index{l}", [P, nt, 8], U32)
        f8 = e.sb(st, f"top_index_f{l}", [P, nt, 8])
        ohg = e.sb(st, f"group_onehot{l}", [P, nt, 4, NG])
        gm = e.sb(st, f"group_mask{l}", [P, nt, NG])
        oh = e.sb(st, f"expert_onehot{l}", [P, nt, 8, NE])
        tmp = e.sb(st, f"route_tmp{l}", [P, 8, NE])
        M = e.sb(st, f"expert_mask{l}", [P, nt, NE])
        ws = e.sb(st, f"weight_sum{l}", [P, nt])
        p8 = e.sb(st, f"top_pos{l}", [P, nt, 8])
        one = e.sb(st, f"slot_onehot{l}", [P, 2, nt, EC, P], FP16)
        ov = e.sb(st, f"over_tmp{l}", [P, 4, 3, NE])
        oc = e.sb(st, f"over_cols{l}", [P, 3])
        s_m, s_pos, s_one, s_tok, s_oc, s_or, s_c = (sem(f"{x}{l}") for x in (
            "masks_ready", "positions_done", "onehot_ready", "tokens_done", "over_cols_ready", "over_rows_done",
            "counts_done"))

        @block.sync
        def _(sp):
            for q in range(NSLOT):
                sp.dma_start(slots[q][:], a["wexp"][l, q]).then_inc(e.ld[q], 16)

        @block.vector
        def _(dve):
            e.vlink(V.tensor_tensor(sel[:], S[:], e.bc(e.rowp[:, R_BROUTER:R_BROUTER + NE].unsqueeze(1), P, nt, NE), ALU.add))
            for i in range(nt):
                for g in range(NG):
                    last = V.max(top[:, i, g], sel[:, i, g * PER:g * PER + PER])
            e.vlink(last)
            e.vlink(V.tensor_tensor(gs[:], top[:, :, :, 0], top[:, :, :, 1], ALU.add))
            for i in range(nt):
                last = V.max(v8[:, i], gs[:, i])
            e.vlink(last)
            for i in range(nt):
                last = V.max_index(i8[:, i], v8[:, i], gs[:, i])
            e.vlink(last)
            e.vlink(V.tensor_copy(f8[:], i8[:]))
            e.vlink(V.tensor_tensor(ohg[:], e.bc(iota[:, 0:NG].unsqueeze(1).unsqueeze(1), P, nt, 4, NG),
                                    e.bc(f8[:, :, 0:4].unsqueeze(3), P, nt, 4, NG), ALU.is_equal))
            e.vlink(V.reduce_sum(gm[:], ohg[:].rearrange("p t k g -> p t g k"), AX))
            e.vlink(V.tensor_scalar(gm[:], gm[:], BIG, -BIG, ALU.mult, ALU.add))
            e.vlink(V.tensor_tensor(sel[:].rearrange("p t (g e) -> p t g e", g=NG),
                                    sel[:].rearrange("p t (g e) -> p t g e", g=NG),
                                    e.bc(gm[:].unsqueeze(3), P, nt, NG, PER), ALU.add))
            for i in range(nt):
                last = V.max(v8[:, i], sel[:, i])
            e.vlink(last)
            for i in range(nt):
                last = V.max_index(i8[:, i], v8[:, i], sel[:, i])
            e.vlink(last)
            e.vlink(V.tensor_copy(f8[:], i8[:]))
            for i in range(nt):
                e.vlink(V.tensor_tensor(oh[:, i], e.bc(iota[:, 0:NE].unsqueeze(1), P, 8, NE),
                                        e.bc(f8[:, i].unsqueeze(2), P, 8, NE), ALU.is_equal))
                V.reduce_sum(M[:, i], oh[:, i].rearrange("p k e -> p e k"), AX).then_inc(s_m, 1)
                e.vlink(V.tensor_tensor(tmp[:], oh[:, i], e.bc(S[:, i].unsqueeze(1), P, 8, NE), ALU.mult))
                e.vlink(V.reduce_sum(r.weight[:, i], tmp[:], AX))
            e.vlink(V.reduce_sum(ws[:], r.weight[:], AX))
            e.vlink(V.reciprocal(ws[:], ws[:]))
            e.vlink(V.tensor_scalar(ws[:], ws[:], ROUTED_SCALE, None, ALU.mult))
            e.vlink(V.tensor_tensor(r.weight[:], r.weight[:], e.bc(ws[:].unsqueeze(2), P, nt, 8), ALU.mult))
            for i in range(nt):
                e.vlink(V.tensor_tensor(tmp[:], oh[:, i], e.bc(r.weight[:, i].unsqueeze(2), P, 8, NE), ALU.mult))
                e.vlink(V.reduce_sum(r.gate[:, i], tmp[:].rearrange("p k e -> p e k"), AX))
            e.vlink(V.tensor_copy(r.tokid[:], e.cst[:, C_TOK + tiles[0]:C_TOK + TT]))
            dve.wait_ge(s_pos, 1)
            pos = r.posb[:, 0]
            rank = PS[:, 0, 0:nt * NE].rearrange("p (t e) -> p t e", t=nt)
            e.vlink(V.tensor_tensor(pos, rank, M[:], ALU.mult))
            e.vlink(V.tensor_scalar(pos, pos, -1.0, None, ALU.add))
            for b in range(1, NBLK):
                V.tensor_scalar(r.posb[:, b], pos, -float(b * P), None, ALU.add)
            for i in range(nt):
                e.vlink(V.tensor_tensor(tmp[:], oh[:, i], e.bc(pos[:, i].unsqueeze(1), P, 8, NE), ALU.mult))
                e.vlink(V.reduce_sum(p8[:, i], tmp[:], AX))
            e.vlink(V.scalar_tensor_tensor(r.weight[:], p8[:], float(P), r.weight[:], ALU.is_lt, ALU.mult))
            e.vlink(V.tensor_scalar(p8[:], p8[:], float(P - 1), None, ALU.min))
            e.vlink(V.scalar_tensor_tensor(p8[:], f8[:], float(P), p8[:], ALU.mult, ALU.add))
            e.vlink(V.tensor_copy(r.yrow[:], p8[:]))
            count = PS[:, 1, 0:NE]
            cnt = ov[:, 3, 0]
            e.vlink(V.tensor_copy(cnt, count))
            flag, cum = ov[:, 0], ov[:, 1]
            for b in range(3):
                last = V.tensor_scalar(flag[:, b], cnt, float((b + 1) * P), None, ALU.is_gt)
            e.vlink(last)
            fl = flag.rearrange("p b e -> p (b e)")
            cf = cum.rearrange("p b e -> p (b e)")
            ovt = ov[:, 2].rearrange("p b e -> p (b e)")
            e.vlink(V.tensor_tensor_scan(cf, e.bc(e.ones[:, 0:1], P, 3 * NE), fl, 0.0, ALU.mult, ALU.add))
            e.vlink(V.tensor_copy(oc[:, 2:3], cf[:, 3 * NE - 1:3 * NE]))
            e.vlink(V.scalar_tensor_tensor(cf, cf, e.cst[:, C_PIDX1:C_PIDX1 + 1], fl, ALU.is_equal, ALU.mult))
            for c in range(2):
                e.vlink(V.tensor_tensor(ovt, cf, e.cst[:, C_OVER + c * 192:C_OVER + c * 192 + 192], ALU.mult))
                e.vlink(V.reduce_sum(oc[:, c:c + 1], ovt, AX))
            V.scalar_tensor_tensor(oc[:, 1:2], oc[:, 1:2], float(nt * NE), oc[:, 0:1], ALU.mult, ALU.add
                                   ).then_inc(s_oc, 1)
            for c in range(NE // EC):
                if c >= 2:
                    dve.wait_ge(s_tok, c - 1)
                V.tensor_tensor(one[:, c % 2], e.bc(iota.unsqueeze(1).unsqueeze(1), P, nt, EC, P),
                                e.bc(pos[:, :, c * EC:c * EC + EC].unsqueeze(3), P, nt, EC, P), ALU.is_equal
                                ).then_inc(s_one, 1)
            dve.wait_ge(s_or, 1)
            V.tensor_copy(r.over[:], PS[0:1, 3, 0:3 * P].rearrange("p (c i) -> p c i", c=3))
            dve.wait_ge(s_tok, NE // EC)
            V.tensor_copy(r.tok[:], PS[:, 2, 0:NE])

        @block.tensor
        def _(pe):
            pe.wait_ge(s_m, nt)
            for i in range(nt):
                for j in range(i + 1):
                    T.matmul(PS[:, 0, i * NE:i * NE + NE], e.cst[:, C_LE:C_LE + P] if j == i else e.ones, M[:, j],
                             start=j == 0, stop=j == i)
            for j in range(nt):
                last = T.matmul(PS[:, 1, 0:NE], e.ones, M[:, j], start=j == 0, stop=j == nt - 1)
            last.then_inc(s_pos, 1)
            pe.wait_ge(s_oc, 1)
            for c in range(3):
                last = T.matmul(PS[0:1, 3, c * P:c * P + P], oc[:, c:c + 1], e.ident, start=True, stop=True)
            last.then_inc(s_or, 1)
            for c in range(NE // EC):
                pe.wait_ge(s_one, c + 1)
                for x in range(EC):
                    for i in range(nt):
                        last = T.matmul(PS[:, 2, c * EC + x:c * EC + x + 1], one[:, c % 2, i, x], r.tokid[:, i:i + 1],
                                        start=i == 0, stop=i == nt - 1)
                last.then_inc(s_tok, 1)


def experts_stage(nc, a, e, r, b, l, slots):
    V, A, T, G, PS, sem = e.V, e.A, e.T, e.G, e.PS, e.sem
    with nc.Block() as block:
        s_t, s_xe, s_g, s_sl, s_ac, s_h, s_at, s_dn, s_ye, s_pi = (sem(f"{x}{l}") for x in (
            "tokens_transposed", "tokensT_ready", "gate_up_done", "silu_done", "act_ready", "act_transposed",
            "actT_ready", "down_done", "y_ready", "gather_index_ready"))
        s_xg = [sem(f"tokens_gathered{i}_{l}") for i in range(2)]
        s_st = [sem(f"y_stored{i}_{l}") for i in range(2)]
        base = [16 * e.loads[q] for q in range(NSLOT)]
        for q in range(NSLOT):
            e.loads[q] += NE // NSLOT

        def groups(eng, body):
            with eng.Fori(0, NE // NSLOT - 1) as g:
                for q in range(NSLOT):
                    body(g, q)
            for q in range(NSLOT):
                body(NE // NSLOT - 1, q)

        def later(g, q, by):
            gg, qq = g + (q + by) // NSLOT, (q + by) % NSLOT
            return None if isinstance(g, int) and gg >= NE // NSLOT else (gg, qq)

        @block.sync
        def _(sp):
            with sp.Fori(1, NE // NSLOT) as g:
                for q in range(NSLOT):
                    sp.wait_ge(s_dn, 4 * g + q - 3 + 2)
                    sp.wait_ge(e.ld[q], 16)
                    sp.dma_start(slots[q][:], a["wexp"][l, g * NSLOT + q]).then_inc(e.ld[q], 16)

        @block.gpsimd
        def _(pool):
            def gather(g, q):
                p = q % 2
                pool.wait_ge(s_t, 4 * g + q + 1)
                G.tensor_copy(b.idx[:, p:p + 1], r.tok[:, bass.ds(g * NSLOT + q, 1)]).then_inc(s_pi, 1)
                pool.wait_ge(s_pi, 1)
                pool.sem_clear(s_pi)
                G.indirect_dma_start(b.xg[:, p], None, a["h_rows"],
                                     bass.IndirectOffsetOnAxis(ap=b.idx[:, p:p + 1], axis=0)).then_inc(s_xg[p], 16)
            groups(pool, gather)

        @block.tensor
        def _(pe):
            pe.sem_inc(s_t, 2)
            pe.sem_inc(s_g, 2)
            pe.sem_inc(s_h, 2)
            pe.sem_inc(s_dn, 2)

            def tokens(g, q):
                p = q % 2
                pe.wait_ge(s_xg[p], 32 * g + 16 * (q // 2 + 1))
                pe.wait_ge(s_xe, 8 * g + 2 * q + 2)
                for k in range(KT):
                    last = T.transpose(PS[:, k // 4, (k % 4) * P:(k % 4) * P + P], b.xg[:, p, k * P:k * P + P], e.ident)
                last.then_inc(s_t, 1)

            def gate_up(g, q):
                p = q % 2
                pe.wait_ge(e.ld[q], base[q] + 16 * g + 16)
                pe.wait_ge(s_xe, 8 * g + 2 * q + 4)
                pe.wait_ge(s_ac, 4 * g + q + 1)
                for k in range(KT):
                    last = T.matmul(PS[:, 2 + p, :], b.xT[:, p, k], slots[q][:, k * 512:k * 512 + 512],
                                    start=k == 0, stop=k == KT - 1)
                last.then_inc(s_g, 1)

            def act_t(g, q):
                p = q % 2
                pe.wait_ge(s_ac, 4 * g + q + 3)
                pe.wait_ge(s_at, 4 * g + q + 1)
                for k in range(2):
                    last = T.transpose(PS[:, 6, k * P:k * P + P], b.ac[:, p, k * P:k * P + P], e.ident)
                last.then_inc(s_h, 1)

            def down(g, q):
                p = q % 2
                pe.wait_ge(s_at, 4 * g + q + 2)
                pe.wait_ge(s_ye, 8 * g + 2 * q + 2)
                for j in range(2):
                    for k in range(2):
                        at = KT * 512 + k * D + j * 512
                        last = T.matmul(PS[:, 4 + j, :], b.acT[:, p, k], slots[q][:, at:at + 512],
                                        start=k == 0, stop=k == 1)
                last.then_inc(s_dn, 1)

            def step(g, q):
                if n := later(g, q, 1):
                    gate_up(*n)
                act_t(g, q)
                if n := later(g, q, 2):
                    tokens(*n)
                down(g, q)

            tokens(0, 0)
            tokens(0, 1)
            gate_up(0, 0)
            groups(pe, step)

        @block.scalar
        def _(act):
            act.sem_inc(s_xe, 2)
            act.sem_inc(s_ye, 2)
            act.sem_inc(s_st[0], 16)
            act.sem_inc(s_st[1], 16)

            def tokens(g, q):
                p = q % 2
                act.wait_ge(s_t, 4 * g + q + 3)
                act.wait_ge(s_g, 4 * g + q + 1)
                A.activation(b.xT[:, p, 0:4].rearrange("p k t -> p (k t)"), PS[:, 0, :], ACT.Copy).then_inc(s_xe, 1)

            def silu(g, q):
                p = q % 2
                act.wait_ge(s_g, 4 * g + q + 3)
                act.wait_ge(s_ac, 4 * g + q + 1)
                A.activation(b.sl[:, p], PS[:, 2 + p, 0:DE], ACT.Silu).then_inc(s_sl, 1)

            def store(g, q):
                p = q % 2
                act.wait_ge(s_dn, 4 * g + q + 3)
                act.wait_ge(s_st[p], 32 * g + 16 * (q // 2) + 16)
                A.activation(b.y[:, p, 0:512], PS[:, 4, :], ACT.Copy).then_inc(s_ye, 1)
                act.wait_ge(s_ye, 8 * g + 2 * q + 4)
                act.dma_start(a["y_rows"].rearrange("(x r) d -> x r d", r=P)[g * NSLOT + q], b.y[:, p]
                              ).then_inc(s_st[p], 16)

            def step(g, q):
                if n := later(g, q, 1):
                    silu(*n)
                if n := later(g, q, 2):
                    tokens(*n)
                store(g, q)

            tokens(0, 0)
            tokens(0, 1)
            silu(0, 0)
            groups(act, step)
            for p in range(2):
                act.wait_ge(s_st[p], 16 * (NE // 2) + 16)

        @block.vector
        def _(dve):
            dve.sem_inc(s_ac, 2)
            dve.sem_inc(s_at, 1)

            def tokens(g, q):
                p = q % 2
                dve.wait_ge(s_t, 4 * g + q + 3)
                dve.wait_ge(s_g, 4 * g + q + 1)
                V.tensor_copy(b.xT[:, p, 4:KT].rearrange("p k t -> p (k t)"), PS[:, 1, :]).then_inc(s_xe, 1)

            def product(g, q):
                p = q % 2
                dve.wait_ge(s_sl, 4 * g + q + 1)
                dve.wait_ge(s_h, 4 * g + q + 1)
                V.tensor_tensor(b.ac[:, p], b.sl[:, p], PS[:, 2 + p, DE:2 * DE], ALU.mult).then_inc(s_ac, 1)

            def act_t(g, q):
                p = q % 2
                dve.wait_ge(s_h, 4 * g + q + 3)
                dve.wait_ge(s_dn, 4 * g + q + 1)
                V.tensor_copy(b.acT[:, p].rearrange("p k t -> p (k t)"), PS[:, 6, 0:2 * P]).then_inc(s_at, 1)

            def store(g, q):
                p = q % 2
                dve.wait_ge(s_dn, 4 * g + q + 3)
                dve.wait_ge(s_st[p], 32 * g + 16 * (q // 2) + 16)
                V.tensor_copy(b.y[:, p, 512:D], PS[:, 5, :]).then_inc(s_ye, 1)

            def step(g, q):
                act_t(g, q)
                if n := later(g, q, 1):
                    product(*n)
                if n := later(g, q, 2):
                    tokens(*n)
                store(g, q)

            tokens(0, 0)
            tokens(0, 1)
            product(0, 0)
            groups(dve, step)


def overflow_stage(nc, a, e, r, b, l, nt, slots):
    V, A, T, G, PS, sem = e.V, e.A, e.T, e.G, e.PS, e.sem
    with ExitStack() as st, nc.Block() as block:
        pc = e.sb(st, f"over_pos{l}", [P, 2, nt])
        one = e.sb(st, f"over_onehot{l}", [P, nt, P], FP16)
        wone, woneT = (slots[1][:, i * nt * P:(i + 1) * nt * P].rearrange("p (t s) -> p t s", t=nt) for i in range(2))
        s_w, s_pc, s_one, s_tok, s_idx, s_xg, s_t, s_xe, s_g, s_sl, s_ac, s_h, s_at, s_dn, s_ye, s_wt, s_wte, s_y, s_end = (
            sem(f"o_{x}{l}") for x in (
                "weights_loaded", "columns_ready", "onehot_ready", "tokens_found", "index_ready", "gathered", "transposed",
                "xT_ready", "gate_up", "silu", "act", "actT", "actT_ready", "down", "y_ready", "weighted_transposed",
                "weightedT_ready", "y_at_tokens", "item_done"))

        def items(eng, body, to_the_end=True):
            n = eng.value_load(r.over[0:1, 2, 0:1], min_val=0, max_val=MAXOVER)
            with eng.If(n > 0):
                with eng.Fori(0, n) as i:
                    body(i)
                    if to_the_end:
                        eng.wait_ge(s_end, i + 1)
                eng.nop()

        def field(eng, c, i, most):
            return eng.value_load(r.over[0:1, c, bass.ds(i, 1)], min_val=0, max_val=most)

        @block.sync
        def _(sp):
            def body(i):
                x = field(sp, 0, i, NE - 1)
                sp.wait_ge(s_dn, i + 1)
                sp.dma_start(slots[0][:], a["wexp"][l, x]).then_inc(s_w, 16)
            items(sp, body, False)

        @block.gpsimd
        def _(pool):
            def body(i):
                pool.wait_ge(s_idx, 1)
                pool.sem_clear(s_idx)
                G.indirect_dma_start(b.xg[:, 0], None, a["h_rows"],
                                     bass.IndirectOffsetOnAxis(ap=b.idx[:, 0:1], axis=0)).then_inc(s_xg, 16)
            items(pool, body)

        @block.vector
        def _(dve):
            def body(i):
                x = field(dve, 0, i, NE - 1)
                at = field(dve, 1, i, (NBLK - 1) * nt * NE + NE - 1)
                for t in range(nt):
                    V.tensor_copy(pc[:, 0, t:t + 1], r.posb[:].rearrange("p b t e -> p (b t e)")[:, bass.ds(at + t * NE, 1)])
                    last = V.tensor_copy(pc[:, 1, t:t + 1], r.gate[:, t, bass.ds(x, 1)])
                last.then_inc(s_pc, 1)
                dve.wait_ge(s_pc, i + 1)
                V.tensor_tensor(one[:], e.bc(e.iota.unsqueeze(1), P, nt, P), e.bc(pc[:, 0].unsqueeze(2), P, nt, P),
                                ALU.is_equal).then_inc(s_one, 1)
                dve.wait_ge(s_one, 2 * i + 1)
                V.tensor_tensor(wone, one[:], e.bc(pc[:, 1].unsqueeze(2), P, nt, P), ALU.mult).then_inc(s_one, 1)
                dve.wait_ge(s_tok, i + 1)
                V.tensor_copy(b.idx[:, 0:1], PS[:, 7, 0:1]).then_inc(s_idx, 1)
                dve.wait_ge(s_t, i + 1)
                V.tensor_copy(b.xT[:, 0, 4:KT].rearrange("p k t -> p (k t)"), PS[:, 1, :]).then_inc(s_xe, 1)
                dve.wait_ge(s_sl, i + 1)
                V.tensor_tensor(b.ac[:, 0], b.sl[:, 0], PS[:, 2, DE:2 * DE], ALU.mult).then_inc(s_ac, 1)
                dve.wait_ge(s_h, i + 1)
                V.tensor_copy(b.acT[:, 0].rearrange("p k t -> p (k t)"), PS[:, 6, 0:2 * P]).then_inc(s_at, 1)
                dve.wait_ge(s_dn, i + 2)
                V.tensor_copy(b.y[:, 0, 512:D], PS[:, 5, :]).then_inc(s_ye, 1)
                dve.wait_ge(s_y, i + 1)
                for t in range(nt):
                    for j in range(2):
                        ys = r.shared[:, t, j * 512:j * 512 + 512]
                        last = V.tensor_tensor(ys, ys, PS[:, 2 * t + j, :], ALU.add)
                last.then_inc(s_end, 1)
            items(dve, body)

        @block.tensor
        def _(pe):
            pe.sem_inc(s_dn, 1)

            def body(i):
                pe.wait_ge(s_one, 2 * i + 2)
                for t in range(nt):
                    last = T.matmul(PS[:, 7, 0:1], one[:, t], r.tokid[:, t:t + 1], start=t == 0, stop=t == nt - 1)
                last.then_inc(s_tok, 1)
                for t in range(nt):
                    last = T.transpose(PS[:, 3, t * P:t * P + P], wone[:, t], e.ident)
                last.then_inc(s_wt, 1)
                pe.wait_ge(s_xg, 16 * i + 16)
                for k in range(KT):
                    last = T.transpose(PS[:, k // 4, (k % 4) * P:(k % 4) * P + P], b.xg[:, 0, k * P:k * P + P], e.ident)
                last.then_inc(s_t, 1)
                pe.wait_ge(s_w, 16 * i + 16)
                pe.wait_ge(s_xe, 2 * i + 2)
                for k in range(KT):
                    last = T.matmul(PS[:, 2, :], b.xT[:, 0, k], slots[0][:, k * 512:k * 512 + 512],
                                    start=k == 0, stop=k == KT - 1)
                last.then_inc(s_g, 1)
                pe.wait_ge(s_ac, i + 1)
                for k in range(2):
                    last = T.transpose(PS[:, 6, k * P:k * P + P], b.ac[:, 0, k * P:k * P + P], e.ident)
                last.then_inc(s_h, 1)
                pe.wait_ge(s_at, i + 1)
                for j in range(2):
                    for k in range(2):
                        at = KT * 512 + k * D + j * 512
                        last = T.matmul(PS[:, 4 + j, :], b.acT[:, 0, k], slots[0][:, at:at + 512],
                                        start=k == 0, stop=k == 1)
                last.then_inc(s_dn, 1)
                pe.wait_ge(s_wte, i + 1)
                pe.wait_ge(s_ye, 2 * i + 2)
                for t in range(nt):
                    for j in range(2):
                        last = T.matmul(PS[:, 2 * t + j, :], woneT[:, t], b.y[:, 0, j * 512:j * 512 + 512],
                                        start=True, stop=True)
                last.then_inc(s_y, 1)
            items(pe, body)

        @block.scalar
        def _(act):
            def body(i):
                act.wait_ge(s_wt, i + 1)
                A.activation(woneT.rearrange("p t s -> p (t s)"), PS[:, 3, 0:nt * P], ACT.Copy).then_inc(s_wte, 1)
                act.wait_ge(s_t, i + 1)
                A.activation(b.xT[:, 0, 0:4].rearrange("p k t -> p (k t)"), PS[:, 0, :], ACT.Copy).then_inc(s_xe, 1)
                act.wait_ge(s_g, i + 1)
                A.activation(b.sl[:, 0], PS[:, 2, 0:DE], ACT.Silu).then_inc(s_sl, 1)
                act.wait_ge(s_dn, i + 2)
                A.activation(b.y[:, 0, 0:512], PS[:, 4, :], ACT.Copy).then_inc(s_ye, 1)
            items(act, body)


def combine_stage(nc, a, e, r, l, tiles):
    V, A, T, G, PS, sem = e.V, e.A, e.T, e.G, e.PS, e.sem
    NB = 4
    with ExitStack() as st, nc.Block() as block:
        yk = e.sb(st, f"y_gathered{l}", [P, NB, D])
        s_yk = [sem(f"y_gathered{i}_{l}") for i in range(NB)]
        s_acc = sem(f"y_added{l}")
        units = [(i, k) for i in range(len(tiles)) for k in range(TOPK)]

        @block.sync
        def _(sp):
            if l < L - 1:
                e.sp_loads(sp, (l + 1) * NCHUNK + RING)

        @block.gpsimd
        def _(pool):
            for u, (i, k) in enumerate(units):
                if u >= NB:
                    pool.wait_ge(s_acc, u - NB + 1)
                G.indirect_dma_start(yk[:, u % NB], None, a["y_rows"],
                                     bass.IndirectOffsetOnAxis(ap=r.yrow[:, i, k:k + 1], axis=0)
                                     ).then_inc(s_yk[u % NB], 16)

        @block.vector
        def _(dve):
            for u, (i, k) in enumerate(units):
                dve.wait_ge(s_yk[u % NB], 16 * (u // NB + 1))
                V.scalar_tensor_tensor(r.shared[:, i], yk[:, u % NB], r.weight[:, i, k:k + 1], r.shared[:, i],
                                       ALU.mult, ALU.add).then_inc(s_acc, 1)
                dve.wait_ge(s_acc, u + 1)
                if k == TOPK - 1:
                    t = tiles[i]
                    v = 0 if t < LAT0 else 1
                    e.vlink(V.tensor_tensor(r.shared[:, i], r.shared[:, i], r.rows[:, v], ALU.mult))
                    V.tensor_tensor(e.X[:, t], e.X[:, t], r.shared[:, i], ALU.add)


def final_norm(nc, a, e):
    V, A, T, PS, sem = e.V, e.A, e.T, e.PS, e.sem
    with ExitStack() as st, nc.Block() as block:
        g = e.sb(st, "g_final", [P, D])
        sq = e.sb(st, "final_sq", [P, 2, D])
        ms = e.sb(st, "final_ms", [P, 2])
        s_g, s_y, s_o = sem("g_final_loaded"), sem("final_ready"), e.s_written
        s_ms, s_rs = sem("final_mean_square"), sem("final_inv_rms")

        @block.sync
        def _(sp):
            sp.dma_start(g[:], a["gfinal"]).then_inc(s_g, 16)
            for i in range(2):
                sp.wait_ge(s_y, i + 1)
                sp.dma_start(a["out"][i * P:i * P + P, :], e.X[:, LAT0 + i]).then_inc(s_o, 16)
            sp.wait_ge(s_o, 32)

        @block.vector
        def _(dve):
            dve.wait_ge(s_g, 16)
            for i in range(2):
                x = e.X[:, LAT0 + i]
                V.tensor_tensor_reduce(out=sq[:, i], in0=x, in1=x, scale=1.0 / D, scalar=0.0, op0=ALU.mult,
                                       op1=ALU.add, accum_out=ms[:, i:i + 1]).then_inc(s_ms, 1)
            dve.wait_ge(s_ms, 2)
            dve.wait_ge(s_rs, 1)
            e.vlink(V.reciprocal(ms[:], ms[:]))
            for i in range(2):
                x = e.X[:, LAT0 + i]
                V.scalar_tensor_tensor(x, x, ms[:, i:i + 1], g[:], ALU.mult, ALU.mult).then_inc(s_y, 1)

        @block.scalar
        def _(act):
            act.wait_ge(s_ms, 2)
            A.activation(ms[:], ms[:], ACT.Sqrt, bias=e.eps).then_inc(s_rs, 1)


def constants():
    import numpy as np
    c = np.zeros((P, NCONST), np.float32)
    i = np.arange(P)
    c[:, C_ID:C_ID + P] = np.eye(P)
    c[:, C_ONES:C_ONES + P] = 1
    c[:, C_LE:C_LE + P] = i[:, None] <= i[None, :]
    c[:, C_GE:C_GE + P] = i[:, None] >= i[None, :]
    q = DH // 4
    half = (i // q) % 2
    for p in range(P):
        if half[p] == 0:
            c[p + q, C_ROT + p] = -1
        else:
            c[p - q, C_ROT + p] = 1
    tok = np.arange(NLAT)
    inv = (1.0 / (np.float32(10000.0) ** (np.arange(q, dtype=np.float32) / np.float32(q)))).astype(np.float32)
    pos = np.stack([tok // 64, tok % 64]).astype(np.float32)
    ang = pos[(i % DH) // (2 * q)] * inv[i % q][:, None]
    c[:, C_COS:C_COS + NLAT] = np.cos(ang.astype(np.float32))
    c[:, C_SIN:C_SIN + NLAT] = np.sin(ang.astype(np.float32))
    for b in range(2):
        at = C_BAND + b * NTOK + NCTX
        c[:, at:at + NLAT] = np.where(np.abs(i[:, None] + b * P - tok[None, :]) <= 128, 0.0, -BIG)
    c[:, C_MF:C_MF + P] = np.where(i[:, None] >= i[None, :], 0.0, -BIG)
    c[:, C_MB:C_MB + P] = np.where(i[:, None] <= i[None, :], 0.0, -BIG)
    c[:, C_IOTA:C_IOTA + P] = i[None, :]
    c[:, C_TOK:C_TOK + TT] = i[:, None] + P * np.arange(TT)[None, :]
    c[:, C_PIDX1] = i + 1
    b, x = np.divmod(np.arange(3 * NE), NE)
    c[:, C_OVER:C_OVER + 192] = x
    c[:, C_OVER + 192:C_OVER + 384] = b + 1
    return c


def pack(w, out=None):
    import numpy as np
    k, n = w.shape[0] // P, w.shape[1]
    return np.ascontiguousarray(w.reshape(k, P, n).transpose(1, 0, 2)).reshape(P, k * n)


def kernel(x, c, ctx, c_ctx, w_mod, b_mod, g_mix, g_ffn, w_in, b_gate, sink, lam_q1, lam_k1,
           lam_q2, lam_k2, g_diff, g_mlstm, w_a, w_b, w_c, w_out, w_router, b_router,
           w_exp_gate, w_exp_up, w_exp_down, w_sh_gate, w_sh_up, w_sh_down, g_final):
    import numpy as np
    import concourse.bacc as bacc
    from concourse.bass_utils import run_bass_kernel_spmd as run

    f = np.float32
    w_in = np.asarray(w_in)
    d = {}
    d["x"] = np.concatenate([np.asarray(ctx)[0], np.asarray(x)[0]], 0)
    d["cond"] = np.ascontiguousarray(np.stack([np.asarray(c_ctx), np.asarray(c)[0]], -1).reshape(KT, P, 2).transpose(1, 0, 2))
    d["const"] = constants()
    aq = np.concatenate([np.arange(h * DH, h * DH + DH) for j in range(4) for h in (j, j + 4)])
    o = np.cumsum([0, 512, 128, 128, 512, 512, 512, 512, 512, 512, 512, 16, 3072])
    r = [np.arange(o[i], o[i + 1]) for i in range(12)]
    cols = [aq, r[3], r[4], r[6], r[7], np.concatenate([r[1], r[2], r[10]]), r[5], r[8], r[9]]
    wseq = np.zeros((L, NCHUNK, P, SLOT), f)
    for l in range(L):
        wm = np.asarray(w_mod[l])
        for i in range(12):
            wseq[l, MOD0 + i, :, :KT * 512] = pack(wm[:, i * 512:i * 512 + 512])
        for i, cs in enumerate(cols):
            wseq[l, IN0 + i, :, :KT * len(cs)] = pack(w_in[l][:, cs])
        for j in range(2):
            for b, wb in enumerate((w_a, w_b, w_c)):
                gc = o[11] + b * D + j * 512
                wseq[l, MERGE0 + 3 * j + b, :, :KT * 512] = pack(w_in[l][:, gc:gc + 512])
                wseq[l, MERGE0 + 3 * j + b, :, KT * 512:] = pack(np.asarray(wb)[l][:, j * 512:j * 512 + 512])
            wseq[l, OUT0 + j, :, :KT * 512] = pack(np.asarray(w_out)[l][:, j * 512:j * 512 + 512])
        wseq[l, SHARED0, :, :KT * 512] = pack(np.concatenate([np.asarray(w_sh_gate)[l], np.asarray(w_sh_up)[l]], 1))
        wseq[l, SHARED0, :, KT * 512:] = pack(np.asarray(w_sh_down)[l])
    d["wseq"] = wseq
    wexp = np.empty((L, NE, P, SLOT), f)
    gu = wexp[..., :KT * 512].reshape(L, NE, P, KT, 2, DE)
    gu[..., 0, :] = np.asarray(w_exp_gate).reshape(L, NE, KT, P, DE).transpose(0, 1, 3, 2, 4)
    gu[..., 1, :] = np.asarray(w_exp_up).reshape(L, NE, KT, P, DE).transpose(0, 1, 3, 2, 4)
    wexp[..., KT * 512:].reshape(L, NE, P, 2, D)[:] = np.asarray(w_exp_down).reshape(L, NE, 2, P, D).transpose(0, 1, 3, 2, 4)
    d["wexp"] = wexp
    d["wr"] = np.stack([pack(np.asarray(w_router)[l]) for l in range(L)])
    row = np.concatenate([np.asarray(b_router), np.asarray(sink), np.asarray(g_diff), np.asarray(g_mlstm),
                          np.asarray(b_gate).reshape(L, 16), np.asarray(lam_q1), np.asarray(lam_k1),
                          np.asarray(lam_q2), np.asarray(lam_k2)], 1)
    d["rowp"] = np.ascontiguousarray(np.broadcast_to(row[:, None, :], (L, P, NROW)))
    d["colp"] = np.ascontiguousarray(np.concatenate(
        [np.asarray(b_mod).reshape(L, 48, P), np.asarray(g_mix).reshape(L, KT, P), np.asarray(g_ffn).reshape(L, KT, P)],
        1).transpose(0, 2, 1))
    d["gfinal"] = np.ascontiguousarray(np.broadcast_to(np.asarray(g_final)[None], (P, D)))

    nc = bacc.Bacc("TRN2", target_bir_lowering=False, num_devices=1)
    a = {n: nc.dram_tensor("in_" + n, v.shape, mybir.dt.from_np(v.dtype), kind="ExternalInput").ap() for n, v in d.items()}
    a["out"] = nc.dram_tensor("out_0", (NLAT, D), F32, kind="ExternalOutput").ap()
    a["h_rows"] = nc.dram_tensor("h_rows", (NTOK, D), F32, kind="Internal").ap()
    a["y_rows"] = nc.dram_tensor("y_rows", (NE * P, D), F32, kind="Internal").ap()
    build(nc, a)
    res = run(nc, [{"in_" + n: v for n, v in d.items()}], core_ids=[0])
    return res.results[0]["out_0"][None]
```

```python
import math
from contextlib import ExitStack

import concourse.bass as bass
from concourse import mybir

P = 128
D, L = 1024, 2
KT = D // P
NCTX = NLAT = 256
NTOK = NCTX + NLAT
TT = NTOK // P
LAT0 = NCTX // P
HB, DH = 4, 64
EPS = 1e-6
NE, NG, TOPK, DE = 64, 8, 8, 256
PER = NE // NG
ROUTED_SCALE = 2.5
SLOT = KT * 2 * DE + 2 * D
NSLOT = 4
RING = 2
NBLK = NTOK // P
MAXOVER = NTOK * TOPK // P
BIG = 1e30

AQ, BQ, BK, CQ, CK, MISC, BV, CV, CO = range(9)
NMOD = 12
MOD_FIRST = [(0, "mod", c) for c in range(4)]
MOD_BESIDE = [(0, "mod", c) for c in range(4, NMOD)] + [(1, "mod", c) for c in range(NMOD)]


def layer_chunks(l):
    return ([(l, "in", c) for c in range(CO)], [(l, "in", CO)] + [(l, "merge", c) for c in range(6)]
            + [(l, "out", c) for c in range(2)] + [(l, "shared", 0)])


SEQ = (MOD_FIRST + layer_chunks(0)[0] + MOD_BESIDE + layer_chunks(0)[1] + layer_chunks(1)[0] + layer_chunks(1)[1])
PLACE = {c: n for n, c in enumerate(SEQ)}


def chunk_size(chunk):
    kind, c = chunk[1:]
    return {"in": KT * (272 if c == MISC else 512), "merge": KT * 512 + 4 * 512, "shared": SLOT}.get(kind, KT * 512)


FILLS_A, FILLS_B = 8, 6

R_BROUTER, R_SINK, R_GDIFF, R_GMLSTM, R_BGATE, R_LAM = 0, 64, 72, 200, 712, 728
NROW = R_LAM + 4 * DH
C_ID, C_ONES, C_LE, C_GE, C_ROT, C_COS, C_SIN, C_BAND, C_MF, C_MB, C_IOTA = (
    0, 128, 256, 384, 512, 640, 896, 1152, 1152 + 1024, 2304, 2432)
C_TOK, C_PIDX1, C_OVER = 2560, 2564, 2568
NCONST = 2568 + 2 * 192

ALU = mybir.AluOpType
ACT = mybir.ActivationFunctionType
F32 = mybir.dt.float32
FP16 = mybir.dt.float16
I32 = mybir.dt.int32
U32 = mybir.dt.uint32
AX = mybir.AxisListType.X


class Space:
    pass


def build(nc, a):
    ctx = ExitStack()
    with ctx:
        layer_sems = []

        def sem(name):
            layer_sems.append(nc.alloc_semaphore(name=name))
            return layer_sems[-1]

        def kept_sem(name):
            return ctx.enter_context(nc.semaphore(name))

        def sb(stack, name, shape, dt=F32):
            return stack.enter_context(nc.sbuf_tensor(name, shape, dt))

        V, A, T, G = nc.vector, nc.scalar, nc.tensor, nc.gpsimd
        PS = ctx.enter_context(nc.psum_tensor("banks", [P, 8, 512], F32))
        ring = [sb(ctx, f"weights{i}", [P, SLOT]) for i in range(RING)]
        X = sb(ctx, "x_resident", [P, TT, D])
        hT = sb(ctx, "hT", [P, KT, NTOK])
        cst = sb(ctx, "constants", [P, NCONST])
        rowp = sb(ctx, "row_params", [P, NROW])
        colp = sb(ctx, "col_params", [P, L, 2 * KT])
        cc = sb(ctx, "cond_cols", [P, KT, 2])
        sc = sb(ctx, "silu_cond", [P, KT, 2])
        modc = sb(ctx, "mod_cols", [P, L, 6, KT, 2])
        mrow = sb(ctx, "mod_rows_out", [2, 2, 512])
        Amix = sb(ctx, "a_mix", [P, KT, 2])
        Affn = sb(ctx, "a_ffn", [P, KT, 2])
        eps_t = sb(ctx, "epsilon", [P, 1])
        eps = eps_t[:]
        ident, ones = cst[:, C_ID:C_ID + P], cst[:, C_ONES:C_ONES + P]
        iota = cst[:, C_IOTA:C_IOTA + P]

        s_dve, s_act = kept_sem("dve_chain"), kept_sem("act_chain")
        ld = [kept_sem(f"slot_loaded{i}") for i in range(NSLOT)]
        loads = [0] * NSLOT
        freed = {}
        issued = [0]
        s_written = kept_sem("out_written")
        s_par = kept_sem("row_params_loaded")
        s_params = kept_sem("col_params_loaded")
        chain = [0, 0]

        def vlink(ins):
            chain[0] += 1
            ins.then_inc(s_dve, 1)
            V.wait_ge(s_dve, chain[0])

        def alink(ins):
            chain[1] += 1
            ins.then_inc(s_act, 1)
            A.wait_ge(s_act, chain[1])

        def bc(ap, *shape):
            return ap.to_broadcast(list(shape))

        def sp_loads(sp, upto):
            while issued[0] < min(upto, len(SEQ)):
                n = issued[0]
                l, kind, c = SEQ[n]
                if n >= RING:
                    if freed[n - RING] is not None:
                        sp.wait_ge(*freed[n - RING])
                size = chunk_size(SEQ[n])
                sp.dma_start(ring[n % RING][:, 0:size], a["wseq"][n, :, 0:size]).then_inc(ld[n % RING], 16)
                loads[n % RING] += 1
                if kind == "mod":
                    sp.dma_start(ring[n % RING][0:2, KT * 512:KT * 512 + 512], a["bmod"][l, c]).then_inc(ld[n % RING], 16)
                    loads[n % RING] += 1
                landed[n] = 16 * loads[n % RING]
                issued[0] += 1
        landed = {}

        def chunk_ready(pe, n):
            pe.wait_ge(ld[n % RING], landed[n])
            return ring[n % RING]

        def end_layer():
            with nc.Block() as block:
                @block.sync
                def _(sp):
                    for s in layer_sems:
                        sp.sem_clear(s)
            for s in layer_sems:
                nc.release_semaphore(s)
            layer_sems.clear()
            for n in freed:
                freed[n] = None


        with nc.Block() as block:
            s_x = sem("x_loaded")

            @block.sync
            def _(sp):
                sp.dma_start(cst[:], a["const"]).then_inc(s_x, 16)
                sp.dma_start(cc[:], a["cond"]).then_inc(s_x, 16)
                sp.dma_start(colp[:], a["colp"].rearrange("l p k -> p l k")).then_inc(s_params, 16)
                sp.dma_start(X[:], a["x"].rearrange("(t p) d -> p t d", p=P)).then_inc(s_x, 16)
                sp_loads(sp, RING)

            @block.vector
            def _(dve):
                V.memset(eps_t[:], EPS)

            @block.scalar
            def _(act):
                act.wait_ge(s_x, 48)
                A.activation(sc[:], cc[:], ACT.Silu)

        e = Space()
        e.V, e.A, e.T, e.G, e.PS = V, A, T, G, PS
        e.ring, e.X, e.hT, e.cst, e.rowp, e.colp = ring, X, hT, cst, rowp, colp
        e.sc, e.modc, e.Amix, e.Affn, e.eps = sc, modc, Amix, Affn, eps
        e.ident, e.ones, e.iota = ident, ones, iota
        e.ld, e.loads, e.freed, e.s_written, e.s_par = ld, loads, freed, s_written, s_par
        e.sem, e.kept_sem, e.sb, e.vlink, e.alink, e.bc = sem, kept_sem, sb, vlink, alink, bc
        e.sp_loads, e.chunk_ready = sp_loads, chunk_ready
        e.mrow, e.s_params = mrow, s_params
        for l in range(L):
            layer(nc, a, e, l)
            end_layer()
        final_norm(nc, a, e)


def layer(nc, a, e, l):
    need_ctx = l < L - 1
    tiles = list(range(TT)) if need_ctx else list(range(LAT0, TT))
    if l == 0:
        e.fill = ModFill(nc, a, e)
        mod_stage(nc, a, e)
    norm_stage(nc, a, e, l, "mix", range(TT), e.Amix, 0)
    with ExitStack() as mix:
        m = Space()
        m.aqT = e.sb(mix, f"aqT_{l}", [P, 4, NTOK])
        m.bqT = e.sb(mix, f"bqT_{l}", [P, 4, NTOK])
        m.cqT = e.sb(mix, f"cqT_{l}", [P, 4, NTOK])
        m.bkT = e.sb(mix, f"bkT_{l}", [P, 4, NTOK])
        m.ckT = e.sb(mix, f"ckT_{l}", [P, 4, NTOK])
        m.akT = e.sb(mix, f"akT_{l}", [P, 1, NTOK])
        m.misc = e.sb(mix, f"misc_{l}", [P, TT, 144])
        m.ck = e.sb(mix, f"ck_{l}", [P, TT, 512])
        m.bv = e.sb(mix, f"bv_{l}", [P, TT, 512])
        m.cv = e.sb(mix, f"cv_{l}", [P, TT, 4, P + 1])
        proj_stage(nc, a, e, m, l, tiles)
        attn_a_stage(nc, a, e, m, l, tiles)
        attn_b_stage(nc, a, e, m, l, tiles)
        mlstm_stage(nc, a, e, m, l, tiles)
        merge_stage(nc, a, e, m, l, tiles)
    norm_stage(nc, a, e, l, "ffn", tiles, e.Affn, 3)
    moe(nc, a, e, l, tiles)


class ModFill:

    def __init__(self, nc, a, e):
        self.nc, self.a, self.e = nc, a, e
        self.jobs = MOD_FIRST + MOD_BESIDE
        self.s_mm, self.s_rows, self.s_tr, self.s_cols = (e.sem(n) for n in (
            "mod_rows_done", "mod_rows_ready", "mod_transposed", "mod_cols_ready"))
        self.s_out = [e.sem(f"mod_rows_written{i}") for i in range(2)]
        self.at = {"mm": 0, "rows": 0, "tr": 0, "cols": 0, "store": 0}
        for i, c in enumerate(self.jobs):
            e.freed[PLACE[c]] = (self.s_rows, i + 1)

    def products(self, pe, bank, lo=0, hi=KT):
        e, i = self.e, self.at["mm"]
        w = e.chunk_ready(pe, PLACE[self.jobs[i]])
        for k in range(lo, hi):
            last = e.T.matmul(e.PS[0:2, bank, :], e.sc[:, k, :], w[:, k * 512:k * 512 + 512], start=k == 0, stop=k == KT - 1)
        if hi == KT:
            last.then_inc(self.s_mm, 1)
            self.at["mm"] += 1

    def add_bias(self, dve, bank):
        e, i = self.e, self.at["rows"]
        dve.wait_ge(self.s_mm, i + 1)
        n = PLACE[self.jobs[i]]
        w = e.chunk_ready(dve, n)
        if i >= 2:
            dve.wait_ge(self.s_out[i % 2], 16 * (i // 2))
            dve.wait_ge(self.s_tr, i - 1)
        e.V.tensor_tensor(e.mrow[:, i % 2], e.PS[0:2, bank, :], w[0:2, KT * 512:KT * 512 + 512], ALU.add).then_inc(self.s_rows, 1)
        self.at["rows"] += 1

    def transpose(self, pe, bank):
        e, i = self.e, self.at["tr"]
        pe.wait_ge(self.s_rows, i + 1)
        for j in range(4):
            last = e.T.matmul(e.PS[:, bank, 2 * j:2 * j + 2], e.mrow[:, i % 2, j * P:j * P + P], e.cst[0:2, C_ID:C_ID + 2],
                              start=True, stop=True)
        last.then_inc(self.s_tr, 1)
        self.at["tr"] += 1

    def store_cols(self, dve, bank):
        e, i = self.e, self.at["cols"]
        l, _, c = self.jobs[i]
        dve.wait_ge(self.s_tr, i + 1)
        e.V.tensor_copy(e.modc[:, l, c // 2, 4 * (c % 2):4 * (c % 2) + 4],
                        e.PS[:, bank, 0:8].rearrange("p (k v) -> p k v", v=2)).then_inc(self.s_cols, 1)
        self.at["cols"] += 1

    def wait_cols(self, pe):
        pe.wait_ge(self.s_cols, self.at["tr"])

    def write_rows(self, sp, n):
        for _ in range(n):
            i = self.at["store"]
            l, _, c = self.jobs[i]
            sp.wait_ge(self.s_rows, i + 1)
            sp.dma_start(self.a["mod_rows"][l, :, c * 512:c * 512 + 512], self.e.mrow[:, i % 2]).then_inc(self.s_out[i % 2], 16)
            self.at["store"] += 1
        if self.at["store"] == len(self.jobs):
            for i in range(2):
                sp.wait_ge(self.s_out[i], 16 * (len(self.jobs) // 2))


def mod_stage(nc, a, e):
    n = len(MOD_FIRST)
    with nc.Block() as block:
        @block.sync
        def _(sp):
            for i in range(n):
                e.sp_loads(sp, i + 1 + RING)
                e.fill.write_rows(sp, 1)
            e.sp_loads(sp, n + RING)

        @block.tensor
        def _(pe):
            for i in range(n):
                e.fill.products(pe, i)
                if i:
                    e.fill.transpose(pe, 4 + (i - 1))
            e.fill.transpose(pe, 4 + n - 1)

        @block.vector
        def _(dve):
            for i in range(n):
                e.fill.add_bias(dve, i)
                if i:
                    e.fill.store_cols(dve, 4 + i - 1)
            e.fill.store_cols(dve, 4 + n - 1)


def norm_stage(nc, a, e, l, tag, tiles, scale, shift):
    V, A, T, PS, sem = e.V, e.A, e.T, e.PS, e.sem
    tiles = list(tiles)
    t0 = tiles[0]
    with ExitStack() as st, nc.Block() as block:
        xn = e.sb(st, f"xn_{tag}{l}", [P, 2, D])
        ms = e.sb(st, f"ms_{tag}{l}", [P, TT])
        s_xn, s_tp = sem(f"xn_ready_{tag}{l}"), sem(f"transposed_{tag}{l}")
        s_va, s_vb = sem(f"evac_dve_{tag}{l}"), sem(f"evac_act_{tag}{l}")
        s_ms, s_rs, s_sc = sem(f"mean_square_{tag}{l}"), sem(f"inv_rms_{tag}{l}"), sem(f"scale_ready_{tag}{l}")

        def evac(i, t, ks, on_dve, done):
            v = 0 if t < LAT0 else 1
            for k in ks:
                src = PS[:, 2 * (i % 4) + k // 4, (k % 4) * P:(k % 4) * P + P]
                dst = e.hT[:, k, t * P:t * P + P]
                sc_, sh_ = scale[:, k, v:v + 1], e.modc[:, l, shift, k, v:v + 1]
                if on_dve:
                    last = V.tensor_scalar(dst, src, sc_, sh_, ALU.mult, ALU.add)
                else:
                    last = A.activation(dst, src, ACT.Identity, bias=sh_, scale=sc_)
            last.then_inc(done, 1)

        if tag == "mix":
            @block.sync
            def _(sp):
                sp.dma_start(e.rowp[:], a["rowp"][l]).then_inc(e.s_par, 16)
                sp.wait_ge(e.s_par, 16 * (l + 1))

        @block.vector
        def _(dve):
            if l == 0:
                dve.wait_ge(e.s_params, 16)
            g = e.colp[:, l, 0:KT] if tag == "mix" else e.colp[:, l, KT:2 * KT]
            V.scalar_tensor_tensor(scale[:], e.modc[:, l, shift + 1], 1.0, e.bc(g.unsqueeze(2), P, KT, 2),
                                   ALU.add, ALU.mult).then_inc(s_sc, 1)
            dve.wait_ge(s_sc, 1)
            for i, t in enumerate(tiles):
                V.tensor_tensor_reduce(out=xn[:, i % 2], in0=e.X[:, t], in1=e.X[:, t], scale=1.0 / D, scalar=0.0,
                                       op0=ALU.mult, op1=ALU.add, accum_out=ms[:, t:t + 1]).then_inc(s_ms, 1)
                dve.wait_ge(s_ms, i + 1)
            dve.wait_ge(s_rs, 1)
            e.vlink(V.reciprocal(ms[:, t0:TT], ms[:, t0:TT]))
            for i, t in enumerate(tiles):
                if i >= 2:
                    dve.wait_ge(s_tp, i - 1)
                V.tensor_scalar(xn[:, i % 2], e.X[:, t], ms[:, t:t + 1], None, ALU.mult).then_inc(s_xn, 1)
                dve.wait_ge(s_tp, i + 1)
                evac(i, t, range(0, 4), True, s_va)

        @block.tensor
        def _(pe):
            for i, t in enumerate(tiles):
                pe.wait_ge(s_xn, i + 1)
                for k in range(KT):
                    last = T.transpose(PS[:, 2 * (i % 4) + k // 4, (k % 4) * P:(k % 4) * P + P],
                                       xn[:, i % 2, k * P:k * P + P], e.ident)
                last.then_inc(s_tp, 1)

        @block.scalar
        def _(act):
            act.wait_ge(s_sc, 1)
            act.wait_ge(s_ms, len(tiles))
            A.activation(ms[:, t0:TT], ms[:, t0:TT], ACT.Sqrt, bias=e.eps).then_inc(s_rs, 1)
            for i, t in enumerate(tiles):
                act.wait_ge(s_tp, i + 1)
                evac(i, t, range(4, KT), False, s_vb)


def proj_stage(nc, a, e, m, l, tiles):
    V, A, T, PS, sem = e.V, e.A, e.T, e.PS, e.sem
    q0 = tiles[0] * P
    kscale = float(P) ** -0.5
    units = []
    for c, dst, rope, lo, sc in ((AQ, m.aqT, 1, q0, 1.0), (BQ, m.bqT, 1, q0, 1.0), (BK, m.bkT, 1, 0, 1.0),
                                 (CQ, m.cqT, 0, q0, 1.0), (CK, m.ckT, 0, 0, kscale)):
        for j in range(4):
            units.append(("T", c, 512, j * P, P, dst[:, j, :], rope, lo, sc))
        if c == CK:
            for t in range(TT):
                units.append(("tok", c, 512, 0, 512, m.ck[:, t], 0, t, kscale))
    units.append(("T", MISC, 272, 0, P, m.akT[:, 0], 1, 0, 1.0))
    for t in range(TT):
        units.append(("tok", MISC, 272, P, 144, m.misc[:, t], 0, t, 1.0))
    for t in range(TT):
        units.append(("tok", BV, 512, 0, 512, m.bv[:, t], 0, t, 1.0))
    for t in range(TT):
        units.append(("tok", CV, 512, 0, 512, m.cv[:, t, :, 0:P], 0, t, 1.0))
    ropes = [u for u, x in enumerate(units) if x[6]]

    with ExitStack() as st, nc.Block() as block:
        tmp = e.sb(st, f"rope_tmp{l}", [P, 2, NLAT])
        s_mm, s_ev = sem(f"proj_done{l}"), sem(f"proj_evacuated{l}")
        s_rot, s_rope = sem(f"rotated{l}"), sem(f"roped{l}")
        for u, x in enumerate(units):
            e.freed[PLACE[l, "in", x[1]]] = (s_mm, u + 1)

        @block.sync
        def _(sp):
            e.sp_loads(sp, PLACE[l, "in", CV] + 1 + RING)

        @block.tensor
        def _(pe):
            def rotate(u):
                r = ropes.index(u)
                pe.wait_ge(s_ev, u + 1)
                if r >= 2:
                    pe.wait_ge(s_rope, r - 1)
                T.matmul(PS[:, 4 + r % 2, 0:NLAT], e.cst[:, C_ROT:C_ROT + P], units[u][5][:, NCTX:NTOK],
                         start=True, stop=True).then_inc(s_rot, 1)

            for u, (kind, c, width, col, n, dst, rope, lo, sc) in enumerate(units):
                w = e.chunk_ready(pe, PLACE[l, "in", c])
                if u >= 4:
                    pe.wait_ge(s_ev, u - 3)
                for k in range(KT):
                    wk = w[:, k * width + col:k * width + col + n]
                    if kind == "T":
                        last = T.matmul(PS[:, u % 4, lo:NTOK], wk, e.hT[:, k, lo:NTOK], start=k == 0, stop=k == KT - 1)
                    else:
                        last = T.matmul(PS[:, u % 4, 0:n], e.hT[:, k, lo * P:lo * P + P], wk,
                                        start=k == 0, stop=k == KT - 1)
                last.then_inc(s_mm, 1)
                if u >= 1 and units[u - 1][6]:
                    rotate(u - 1)

        @block.scalar
        def _(act):
            for u, (kind, c, width, col, n, dst, rope, lo, sc) in enumerate(units):
                act.wait_ge(s_mm, u + 1)
                if kind == "T":
                    A.activation(dst[:, lo:NTOK], PS[:, u % 4, lo:NTOK], ACT.Copy, scale=sc).then_inc(s_ev, 1)
                else:
                    src = PS[:, u % 4, 0:n]
                    if c == CV:
                        src = src.rearrange("p (h d) -> p h d", h=4)
                    A.activation(dst, src, ACT.Copy, scale=sc).then_inc(s_ev, 1)

        @block.vector
        def _(dve):
            V.memset(m.cv[:, :, :, P:P + 1], 1.0)
            for r, u in enumerate(ropes):
                lat = units[u][5][:, NCTX:NTOK]
                dve.wait_ge(s_rot, r + 1)
                V.tensor_tensor(tmp[:, r % 2], PS[:, 4 + r % 2, 0:NLAT], e.cst[:, C_SIN:C_SIN + NLAT], ALU.mult)
                e.vlink(V.tensor_tensor(lat, lat, e.cst[:, C_COS:C_COS + NLAT], ALU.mult))
                V.tensor_tensor(lat, lat, tmp[:, r % 2], ALU.add).then_inc(s_rope, 1)


def attn_a_stage(nc, a, e, m, l, tiles):
    V, A, T, PS, sem = e.V, e.A, e.T, e.PS, e.sem
    units = [(t, g) for t in tiles for g in range(2)]
    with ExitStack() as st, nc.Block() as block:
        S = e.sb(st, f"a_probs{l}", [P, 4, NTOK])
        PT = e.sb(st, f"a_probsT{l}", [P, 4, 4, P])
        O = e.sb(st, f"a_out{l}", [P, 2, 8, DH])
        mx = e.sb(st, f"a_stats{l}", [P, 6, 4])
        s_sc, s_m, s_ex, s_tr, s_pt, s_pv, s_o, s_ot, s_oev = (sem(f"{n}{l}") for n in (
            "a_scores", "a_max", "a_exp", "a_transposed", "a_probsT_ready", "a_pv", "a_out_ready",
            "a_outT", "a_outT_stored"))
        fills = FILLS_A if l == 0 else 0

        @block.sync
        def _(sp):
            for u in range(fills):
                e.fill.write_rows(sp, 1)
                e.sp_loads(sp, PLACE[MOD_BESIDE[0]] + u + 1 + RING)

        def nk(t):
            return NTOK if t >= LAT0 else NCTX

        @block.tensor
        def _(pe):
            for u, (t, g) in enumerate(units):
                n = nk(t)
                if u >= 1:
                    pe.wait_ge(s_o, u)
                for h in range(4):
                    last = T.matmul(PS[:, h, 0:n], m.aqT[g * DH:g * DH + DH, h, t * P:t * P + P],
                                    m.akT[g * DH:g * DH + DH, 0, 0:n], start=True, stop=True)
                last.then_inc(s_sc, 1)
                if u < fills:
                    pe.wait_ge(s_m, u + 1)
                    e.fill.products(pe, 3, 0, 4)
                pe.wait_ge(s_ex, u + 1)
                for h in range(4):
                    for k in range(n // P):
                        last = T.transpose(PS[:, 4 + h, k * P:k * P + P], S[:, h, k * P:k * P + P], e.ident)
                last.then_inc(s_tr, 1)
                if u < fills:
                    e.fill.products(pe, 3, 4, KT)
                pe.wait_ge(s_pt, 2 * u + 2)
                for h in range(4):
                    for k in range(n // P):
                        last = T.matmul(PS[:, 0, h * DH:h * DH + DH], PT[:, h, k, :],
                                        m.misc[:, k, g * DH:g * DH + DH], start=k == 0, stop=k == n // P - 1)
                last.then_inc(s_pv, 1)
                if u < fills:
                    e.fill.transpose(pe, 3)
                if g == 1:
                    i = u // 2
                    pe.wait_ge(s_o, u + 1)
                    for j in range(4):
                        last = T.transpose(PS[:, 1, j * P:j * P + P],
                                           O[:, i % 2].rearrange("p h d -> p (h d)")[:, j * P:j * P + P], e.ident)
                    last.then_inc(s_ot, 1)
                    pe.wait_ge(s_oev, i + 1)
                if u < fills:
                    e.fill.wait_cols(pe)

        @block.vector
        def _(dve):
            for u, (t, g) in enumerate(units):
                n = nk(t)
                sink = e.rowp[:, R_SINK + 4 * g:R_SINK + 4 * g + 4]
                dve.wait_ge(s_sc, u + 1)
                if t >= LAT0:
                    band = e.cst[:, C_BAND + (t - LAT0) * NTOK:C_BAND + (t - LAT0) * NTOK + n]
                    e.vlink(V.scalar_tensor_tensor(S[:, :, 0:n], PS[:, 0:4, 0:n], DH ** -0.5,
                                                   e.bc(band.unsqueeze(1), P, 4, n), ALU.mult, ALU.add))
                else:
                    e.vlink(V.tensor_scalar(S[:, :, 0:n], PS[:, 0:4, 0:n], DH ** -0.5, None, ALU.mult))
                e.vlink(V.reduce_max(mx[:, 0], S[:, :, 0:n], AX))
                e.vlink(V.tensor_tensor(mx[:, 0], mx[:, 0], sink, ALU.max))
                e.vlink(V.tensor_scalar(mx[:, 1], mx[:, 0], -1.0, None, ALU.mult))
                V.tensor_tensor(mx[:, 2], sink, mx[:, 0], ALU.subtract).then_inc(s_m, 1)
                dve.wait_ge(s_ex, u + 1)
                e.vlink(V.tensor_tensor(mx[:, 4], mx[:, 3], mx[:, 5], ALU.add))
                e.vlink(V.reciprocal(mx[:, 4], mx[:, 4]))
                dve.wait_ge(s_tr, u + 1)
                V.tensor_copy(PT[:, 0:2, 0:n // P].rearrange("p h k q -> p h (k q)"),
                              PS[:, 4:6, 0:n]).then_inc(s_pt, 1)
                if u < fills:
                    e.fill.add_bias(dve, 3)
                dve.wait_ge(s_pv, u + 1)
                V.tensor_tensor(O[:, (u // 2) % 2, 4 * g:4 * g + 4], PS[:, 0, 0:4 * DH].rearrange("p (h d) -> p h d", h=4),
                                e.bc(mx[:, 4].unsqueeze(2), P, 4, DH), ALU.mult).then_inc(s_o, 1)
                if u < fills:
                    e.fill.store_cols(dve, 3)
                if g == 1:
                    dve.wait_ge(s_ot, u // 2 + 1)
                    V.tensor_copy(m.aqT[:, :, t * P:t * P + P],
                                  PS[:, 1, :].rearrange("p (j q) -> p j q", j=4)).then_inc(s_oev, 1)

        @block.scalar
        def _(act):
            for u, (t, g) in enumerate(units):
                n = nk(t)
                act.wait_ge(s_m, u + 1)
                for h in range(4):
                    A.activation(S[:, h, 0:n], S[:, h, 0:n], ACT.Exp, bias=mx[:, 1, h:h + 1], accum_out=mx[:, 3, h:h + 1])
                A.activation(mx[:, 5], mx[:, 2], ACT.Exp).then_inc(s_ex, 1)
                act.wait_ge(s_tr, u + 1)
                A.activation(PT[:, 2:4, 0:n // P].rearrange("p h k q -> p h (k q)"), PS[:, 6:8, 0:n],
                             ACT.Copy).then_inc(s_pt, 1)


def attn_b_stage(nc, a, e, m, l, tiles):
    V, A, T, PS, sem = e.V, e.A, e.T, e.PS, e.sem
    lam_init = 0.8 - 0.6 * math.exp(-0.3 * l)
    with ExitStack() as st, nc.Block() as block:
        E = e.sb(st, f"b_probs{l}", [P, 2, 4, NTOK])
        O = e.sb(st, f"b_out{l}", [P, 4, P])
        mx = e.sb(st, f"b_stats{l}", [P, 8, 4])
        lam = e.sb(st, f"lam{l}", [P, 4])
        lt = e.sb(st, f"lam_tmp{l}", [P, 2, DH])
        gd = e.sb(st, f"g_diff_scaled{l}", [P, P])
        s_sc, s_m, s_ex, s_at, s_tr, s_pt, s_pv, s_o, s_ot, s_oev, s_l1, s_l2 = (sem(f"{n}{l}") for n in (
            "b_scores", "b_max", "b_exp", "b_att_ready", "b_transposed", "b_probsT_ready", "b_pv", "b_out_ready",
            "b_outT", "b_outT_stored", "lam_sums", "lam_exps"))
        PT = E[:, 1].rearrange("p h (k q) -> p h k q", k=4)
        fills = FILLS_B if l == 0 else 0

        def filled(u, i):
            return i * len(tiles) + u < fills

        @block.sync
        def _(sp):
            for f in range(fills):
                e.fill.write_rows(sp, 1)
                e.sp_loads(sp, PLACE[MOD_BESIDE[0]] + FILLS_A + f + 1 + RING)
        s_ms, s_rs = sem(f"b_mean_square{l}"), sem(f"b_inv_rms{l}")

        def nk(t):
            return NTOK if t >= LAT0 else NCTX

        @block.tensor
        def _(pe):
            for u, t in enumerate(tiles):
                n = nk(t)
                if u >= 1:
                    pe.wait_ge(s_oev, u)
                for s in range(2):
                    for h in range(4):
                        last = T.matmul(PS[:, 4 * s + h, 0:n], m.bqT[s * DH:s * DH + DH, h, t * P:t * P + P],
                                        m.bkT[s * DH:s * DH + DH, h, 0:n], start=True, stop=True)
                    last.then_inc(s_sc, 1)
                if filled(u, 0):
                    pe.wait_ge(s_ex, 2 * u + 1)
                    e.fill.products(pe, 3)
                pe.wait_ge(s_at, u + 1)
                for h in range(4):
                    for k in range(n // P):
                        last = T.transpose(PS[:, 4 + h, k * P:k * P + P], E[:, 0, h, k * P:k * P + P], e.ident)
                last.then_inc(s_tr, 1)
                if filled(u, 0):
                    e.fill.transpose(pe, 3)
                if filled(u, 1):
                    e.fill.products(pe, 2, 0, 3)
                pe.wait_ge(s_pt, 2 * u + 2)
                for h in range(4):
                    for k in range(n // P):
                        last = T.matmul(PS[:, 0, h * P:h * P + P], PT[:, h, k, :],
                                        m.bv[:, k, h * P:h * P + P], start=k == 0, stop=k == n // P - 1)
                last.then_inc(s_pv, 1)
                if filled(u, 1):
                    e.fill.products(pe, 2, 3, KT)
                pe.wait_ge(s_o, u + 1)
                for j in range(4):
                    last = T.transpose(PS[:, 1, j * P:j * P + P], O[:, j], e.ident)
                last.then_inc(s_ot, 1)
                if filled(u, 1):
                    e.fill.transpose(pe, 2)
                if filled(u, 0):
                    e.fill.wait_cols(pe)

        @block.vector
        def _(dve):
            lr = e.rowp[:, R_LAM:R_LAM + 4 * DH].rearrange("p (a b d) -> p a b d", a=2, b=2)
            e.vlink(V.tensor_tensor(lt[:], lr[:, :, 0], lr[:, :, 1], ALU.mult))
            V.reduce_sum(lam[:, 0:2], lt[:], AX).then_inc(s_l1, 1)
            dve.wait_ge(s_l2, 1)
            e.vlink(V.tensor_tensor(lam[:, 2:3], lam[:, 0:1], lam[:, 1:2], ALU.subtract))
            e.vlink(V.tensor_scalar(lam[:, 2:3], lam[:, 2:3], lam_init, None, ALU.add))
            e.vlink(V.tensor_scalar(gd[:], e.rowp[:, R_GDIFF:R_GDIFF + P], 1.0 - lam_init, None, ALU.mult))
            for u, t in enumerate(tiles):
                n = nk(t)
                for s in range(2):
                    dve.wait_ge(s_sc, 2 * u + s + 1)
                    e.vlink(V.reduce_max(mx[:, s], PS[:, 4 * s:4 * s + 4, 0:n], AX))
                    V.tensor_scalar(mx[:, s], mx[:, s], -DH ** -0.5, None, ALU.mult).then_inc(s_m, 1)
                dve.wait_ge(s_ex, 2 * u + 2)
                e.vlink(V.reciprocal(mx[:, 4:6], mx[:, 2:4]))
                e.vlink(V.tensor_tensor(mx[:, 6], mx[:, 2], mx[:, 5], ALU.mult))
                e.vlink(V.tensor_scalar(mx[:, 6], mx[:, 6], lam[:, 2:3], -1.0, ALU.mult, ALU.mult))
                for h in range(4):
                    last = V.scalar_tensor_tensor(E[:, 0, h, 0:n], E[:, 1, h, 0:n], mx[:, 6, h:h + 1],
                                                  E[:, 0, h, 0:n], ALU.mult, ALU.add)
                last.then_inc(s_at, 1)
                if filled(u, 0):
                    e.fill.add_bias(dve, 3)
                dve.wait_ge(s_tr, u + 1)
                V.tensor_copy(PT[:, 0:2, 0:n // P].rearrange("p h k q -> p h (k q)"), PS[:, 4:6, 0:n]).then_inc(s_pt, 1)
                if filled(u, 0):
                    e.fill.store_cols(dve, 3)
                dve.wait_ge(s_pv, u + 1)
                e.vlink(V.tensor_tensor(O[:], PS[:, 0, :].rearrange("p (h d) -> p h d", h=4),
                                        e.bc(mx[:, 4].unsqueeze(2), P, 4, P), ALU.mult))
                sq = E[:, 0, :, 0:P]
                e.vlink(V.tensor_tensor(sq, O[:], O[:], ALU.mult))
                e.vlink(V.reduce_sum(mx[:, 7], sq, AX))
                V.tensor_scalar(mx[:, 7], mx[:, 7], 1.0 / P, None, ALU.mult).then_inc(s_ms, 1)
                dve.wait_ge(s_rs, u + 1)
                e.vlink(V.reciprocal(mx[:, 7], mx[:, 7]))
                e.vlink(V.tensor_tensor(O[:], O[:], e.bc(mx[:, 7].unsqueeze(2), P, 4, P), ALU.mult))
                V.tensor_tensor(O[:], O[:], e.bc(gd[:].unsqueeze(1), P, 4, P), ALU.mult).then_inc(s_o, 1)
                if filled(u, 1):
                    e.fill.add_bias(dve, 2)
                dve.wait_ge(s_ot, u + 1)
                V.tensor_copy(m.bqT[:, :, t * P:t * P + P],
                              PS[:, 1, :].rearrange("p (j q) -> p j q", j=4)).then_inc(s_oev, 1)
                if filled(u, 1):
                    e.fill.store_cols(dve, 2)

        @block.scalar
        def _(act):
            act.wait_ge(s_l1, 1)
            A.activation(lam[:, 0:2], lam[:, 0:2], ACT.Exp).then_inc(s_l2, 1)
            for u, t in enumerate(tiles):
                n = nk(t)
                if u >= 1:
                    act.wait_ge(s_o, u)
                for s in range(2):
                    act.wait_ge(s_m, 2 * u + s + 1)
                    for h in range(4):
                        last = A.activation(E[:, s, h, 0:n], PS[:, 4 * s + h, 0:n], ACT.Exp, bias=mx[:, s, h:h + 1],
                                            scale=DH ** -0.5, accum_out=mx[:, 2 + s, h:h + 1])
                    last.then_inc(s_ex, 1)
                act.wait_ge(s_tr, u + 1)
                A.activation(PT[:, 2:4, 0:n // P].rearrange("p h k q -> p h (k q)"), PS[:, 6:8, 0:n],
                             ACT.Copy).then_inc(s_pt, 1)
                act.wait_ge(s_ms, u + 1)
                A.activation(mx[:, 7], mx[:, 7], ACT.Sqrt, bias=e.eps).then_inc(s_rs, 1)


def mlstm_stage(nc, a, e, m, l, tiles):
    V, A, T, PS, sem = e.V, e.A, e.T, e.PS, e.sem
    steps = [(d, t) for d, order in ((0, (0, 1, 2, 3)), (1, (1, 0, 3, 2))) for t in order]
    outs = [(u, d, t) for u, (d, t) in enumerate(steps) if t in tiles]
    H = m.bkT[:]
    Q = P + 1
    with ExitStack() as st, nc.Block() as block:
        gates = e.sb(st, f"gates{l}", [P, TT, 4, 4])
        logf = e.sb(st, f"logf{l}", [P, TT, 2, 4])
        C = e.sb(st, f"c_state{l}", [P, 4, Q])
        dg = e.sb(st, f"diag{l}", [P, 4, P])
        dm = e.sb(st, f"decay{l}", [P, 4, P])
        PT = e.sb(st, f"c_probsT{l}", [P, 4, P])
        wk = e.sb(st, f"wk{l}", [P, 4, P])
        num = e.sb(st, f"num{l}", [P, 4, Q])
        z = e.sb(st, f"c_stats{l}", [P, 16, 4])
        names = ("f_in", "f_out", "c_cum", "c_r", "c_rbc", "c_maxes", "c_exps", "c_scores", "c_dexp", "c_probs", "c_transposed",
                 "c_probsT_ready", "c_nums", "c_state_done", "c_wk", "c_dstate", "c_num_done")
        (s_f1, s_f2, s_cum, s_r, s_rbc, s_mx, s_ex, s_sc, s_de, s_p, s_tr, s_pt, s_nm, s_st, s_wk, s_ds,
         s_nd) = (sem(f"{n}{l}") for n in names)
        fills = len(MOD_BESIDE) - FILLS_A - FILLS_B if l == 0 else 0

        @block.sync
        def _(sp):
            for f in range(fills):
                e.fill.write_rows(sp, 1)
                e.sp_loads(sp, min(PLACE[MOD_BESIDE[0]] + FILLS_A + FILLS_B + f + 1, PLACE[MOD_BESIDE[-1]] + 1) + RING)

        (BCUM, BLAST, RR, MAXR, MAXD, MST, UU, WW, AIN, DECAY, WKE, EXM, DEN, NEW, TMP, TMP2) = range(16)

        def heads(ap):
            return ap.rearrange("p (h d) -> p h d", h=4)

        def num_bank(b, h):
            return PS[:, b + h // 2, (h % 2) * Q:(h % 2) * Q + Q]

        def num_pair(b, i):
            return PS[:, b + i, 0:2 * Q].rearrange("p (h q) -> p h q", h=2)

        @block.tensor
        def _(pe):
            o = 0
            for u, (d, t) in enumerate(steps):
                out = t in tiles
                tri = e.cst[:, (C_LE if d == 0 else C_GE):(C_LE if d == 0 else C_GE) + P]
                if u == 0:
                    pe.wait_ge(s_f2, 2)
                if u >= 1:
                    pe.wait_ge(s_st, u)
                T.matmul(PS[:, 2, 0:4], tri, logf[:, t, d], start=True, stop=True)
                T.matmul(PS[:, 2, 4:8], e.ones, logf[:, t, d], start=True, stop=True).then_inc(s_cum, 1)
                if out:
                    for h in range(4):
                        last = T.matmul(PS[:, 1, h * P:h * P + P], m.cqT[:, h, t * P:t * P + P],
                                        m.ckT[:, h, t * P:t * P + P], start=True, stop=True)
                    last.then_inc(s_sc, 1)
                    for h in range(4):
                        last = T.matmul(num_bank(6, h), m.cqT[:, h, t * P:t * P + P], C[:, h], start=True, stop=True)
                pe.wait_ge(s_r, u + 1)
                T.matmul(PS[:, 0, :], e.ones, dg[:].rearrange("p h s -> p (h s)"), start=True, stop=True
                         ).then_inc(s_rbc, 1)
                if u < fills:
                    e.fill.products(pe, 2, 0, 5)
                if out:
                    pe.wait_ge(s_p, o + 1)
                    for h in range(4):
                        last = T.transpose(PS[:, 3, h * P:h * P + P], dm[:, h], e.ident)
                    last.then_inc(s_tr, 1)
                if u < fills:
                    e.fill.products(pe, 2, 5, KT)
                if out:
                    pe.wait_ge(s_pt, o + 1)
                    for h in range(4):
                        last = T.matmul(num_bank(4, h), PT[:, h], m.cv[:, t, h], start=True, stop=True)
                    last.then_inc(s_nm, 1)
                    o += 1
                    if u < fills:
                        e.fill.transpose(pe, 2)
                    pe.wait_ge(s_nd, o)
                pe.wait_ge(s_wk, u + 1)
                for h in range(4):
                    last = T.matmul(num_bank(4, h), wk[:, h], m.cv[:, t, h], start=True, stop=True)
                last.then_inc(s_ds, 1)

        @block.vector
        def _(dve):
            bg = e.rowp[:, R_BGATE:R_BGATE + 16]
            e.vlink(V.tensor_tensor(gates[:].rearrange("p t g h -> p t (g h)"), m.misc[:, :, P:P + 16],
                                    e.bc(bg.unsqueeze(1), P, TT, 16), ALU.add))
            f = gates[:].rearrange("p t (d i) h -> p t d i h", i=2)[:, :, :, 1]
            e.vlink(V.tensor_scalar(logf[:], f, -1.0, None, ALU.mult))
            V.tensor_tensor(logf[:], logf[:], f, ALU.min).then_inc(s_f1, 1)
            dve.wait_ge(s_f2, 1)
            e.vlink(V.tensor_scalar(dm[:, 0, 0:32].rearrange("p (t d h) -> p t d h", t=TT, d=2), f, 0.0, None, ALU.min))
            e.vlink(V.tensor_tensor(logf[:], dm[:, 0, 0:32].rearrange("p (t d h) -> p t d h", t=TT, d=2), logf[:],
                                    ALU.subtract))
            V.memset(C[:], 0.0).then_inc(s_f2, 1)
            o = 0
            for u, (d, t) in enumerate(steps):
                out = t in tiles
                if u in (0, 4):
                    e.vlink(V.memset(z[:] if u == 0 else z[:, MST], 0.0))
                dve.wait_ge(s_cum, u + 1)
                e.vlink(V.tensor_copy(z[:, BCUM:BCUM + 2].rearrange("p a h -> p (a h)"), PS[:, 2, 0:8]))
                e.vlink(V.tensor_tensor(z[:, RR], gates[:, t, 2 * d], z[:, BCUM], ALU.subtract))
                V.tensor_tensor(dg[:], e.bc(e.ident.unsqueeze(1), P, 4, P), e.bc(z[:, RR].unsqueeze(2), P, 4, P),
                                ALU.mult).then_inc(s_r, 1)
                dve.wait_ge(s_rbc, u + 1)
                rb = heads(PS[:, 0, :])
                e.vlink(V.reduce_max(z[:, MAXR], rb, AX))
                e.vlink(V.tensor_tensor(z[:, WW], z[:, MST], z[:, MAXR], ALU.max))
                if out:
                    mask = e.cst[:, (C_MF if d == 0 else C_MB):(C_MF if d == 0 else C_MB) + P]
                    e.vlink(V.tensor_tensor(dm[:], rb, e.bc(mask.unsqueeze(1), P, 4, P), ALU.add))
                    e.vlink(V.reduce_max(z[:, MAXD], dm[:], AX))
                    e.vlink(V.tensor_tensor(z[:, UU], z[:, MST], z[:, MAXD], ALU.max))
                    V.tensor_tensor(dm[:], dm[:], e.bc(z[:, UU].unsqueeze(2), P, 4, P), ALU.subtract)
                    V.tensor_tensor(z[:, AIN], z[:, MST], z[:, UU], ALU.subtract)
                    e.vlink(V.tensor_tensor(z[:, TMP], z[:, BCUM], z[:, UU], ALU.add))
                    V.tensor_scalar(z[:, EXM], z[:, TMP], -1.0, None, ALU.mult)
                V.tensor_tensor(z[:, DECAY], z[:, MST], z[:, WW], ALU.subtract)
                V.tensor_tensor(z[:, WKE], z[:, RR], z[:, WW], ALU.subtract).then_inc(s_mx, 1)
                dve.wait_ge(s_ex, u + 1)
                e.vlink(V.tensor_tensor(z[:, MST], z[:, BLAST], z[:, WW], ALU.add))
                if out:
                    dve.wait_ge(s_sc, o + 1)
                    V.tensor_tensor(dm[:], heads(PS[:, 1, :]), dm[:], ALU.mult).then_inc(s_p, 1)
                V.tensor_tensor(wk[:], heads(m.ck[:, t]), e.bc(z[:, WKE].unsqueeze(2), P, 4, P), ALU.mult
                                ).then_inc(s_wk, 1)
                if u < fills:
                    e.fill.add_bias(dve, 2)
                if out:
                    dve.wait_ge(s_nm, o + 1)
                    for i in range(2):
                        e.vlink(V.tensor_tensor(num[:, 2 * i:2 * i + 2], num_pair(6, i),
                                                e.bc(z[:, AIN, 2 * i:2 * i + 2].unsqueeze(2), P, 2, Q), ALU.mult))
                        last = V.tensor_tensor(num[:, 2 * i:2 * i + 2], num[:, 2 * i:2 * i + 2], num_pair(4, i), ALU.add)
                    o += 1
                    last.then_inc(s_nd, 1)
                    if u < fills:
                        e.fill.store_cols(dve, 2)
                    dve.wait_ge(s_nd, o)
                    den = num[:, :, P]
                    e.vlink(V.tensor_scalar(z[:, TMP], den, -1.0, None, ALU.mult))
                    e.vlink(V.tensor_tensor(z[:, TMP], z[:, TMP], den, ALU.max))
                    e.vlink(V.tensor_tensor(z[:, TMP], z[:, TMP], z[:, EXM], ALU.max))
                    e.vlink(V.reciprocal(z[:, DEN], z[:, TMP]))
                    hs = H[:, t, :].rearrange("p (h d) -> p h d", h=4)
                    if d == 0:
                        V.tensor_tensor(hs, num[:, :, 0:P], e.bc(z[:, DEN].unsqueeze(2), P, 4, P), ALU.mult)
                    else:
                        e.vlink(V.tensor_tensor(num[:, :, 0:P], num[:, :, 0:P], e.bc(z[:, DEN].unsqueeze(2), P, 4, P),
                                                ALU.mult))
                        V.tensor_tensor(hs, hs, num[:, :, 0:P], ALU.add)
                if u == 3:
                    dve.wait_ge(s_ds, u + 1)
                    V.memset(C[:], 0.0).then_inc(s_st, 1)
                    continue
                e.vlink(V.tensor_tensor(C[:], C[:], e.bc(z[:, DECAY].unsqueeze(2), P, 4, Q), ALU.mult))
                dve.wait_ge(s_ds, u + 1)
                V.tensor_tensor(C[:, 0:2], C[:, 0:2], num_pair(4, 0), ALU.add)
                V.tensor_tensor(C[:, 2:4], C[:, 2:4], num_pair(4, 1), ALU.add).then_inc(s_st, 1)
                dve.wait_ge(s_st, u + 1)

        @block.scalar
        def _(act):
            act.wait_ge(s_f1, 1)
            e.alink(A.activation(logf[:], logf[:], ACT.Exp))
            A.activation(logf[:], logf[:], ACT.Ln, bias=1.0).then_inc(s_f2, 1)
            o = 0
            for u, (d, t) in enumerate(steps):
                out = t in tiles
                act.wait_ge(s_mx, u + 1)
                if out:
                    A.activation(dm[:], dm[:], ACT.Exp)
                A.activation(z[:, AIN:EXM + 1], z[:, AIN:EXM + 1], ACT.Exp).then_inc(s_ex, 1)
                if out:
                    act.wait_ge(s_tr, o + 1)
                    A.activation(PT[:].rearrange("p h t -> p (h t)"), PS[:, 3, :], ACT.Copy).then_inc(s_pt, 1)
                    o += 1

    with ExitStack() as st, nc.Block() as block:
        sg = e.sb(st, f"sig_o{l}", [P, 2, 512])
        sq = e.sb(st, f"c_sq{l}", [P, 4, P])
        ms = e.sb(st, f"c_ms{l}", [P, TT, 4])
        t0 = tiles[0]
        s_co, s_sg, s_oc, s_ot, s_oev = (sem(f"{n}{l}") for n in (
            "co_done", "co_sigmoid", "oc_ready", "ocT", "ocT_stored"))
        e.freed[PLACE[l, "in", CO]] = (s_co, len(tiles))
        s_ms, s_rs = sem(f"c_mean_square{l}"), sem(f"c_inv_rms{l}")

        @block.sync
        def _(sp):
            e.sp_loads(sp, PLACE[l, "in", CO] + 1 + RING)

        @block.tensor
        def _(pe):
            w = e.chunk_ready(pe, PLACE[l, "in", CO])

            def back(i, t):
                pe.wait_ge(s_oc, i + 1)
                if i >= 2:
                    pe.wait_ge(s_oev, i - 1)
                for j in range(4):
                    last = T.transpose(PS[:, 4 + i % 2, j * P:j * P + P], H[:, t, j * P:j * P + P], e.ident)
                last.then_inc(s_ot, 1)

            for i, t in enumerate(tiles):
                for k in range(KT):
                    last = T.matmul(PS[:, i, :], e.hT[:, k, t * P:t * P + P], w[:, k * 512:k * 512 + 512],
                                    start=k == 0, stop=k == KT - 1)
                last.then_inc(s_co, 1)
                if i >= 1:
                    back(i - 1, tiles[i - 1])
            back(len(tiles) - 1, tiles[-1])

        @block.scalar
        def _(act):
            act.wait_ge(s_ms, 1)
            A.activation(ms[:, t0:TT], ms[:, t0:TT], ACT.Sqrt, bias=e.eps).then_inc(s_rs, 1)
            for i, t in enumerate(tiles):
                act.wait_ge(s_co, i + 1)
                if i >= 2:
                    act.wait_ge(s_oc, i - 1)
                A.activation(sg[:, i % 2], PS[:, i, :], ACT.Sigmoid).then_inc(s_sg, 1)

        @block.vector
        def _(dve):
            gm = e.rowp[:, R_GMLSTM:R_GMLSTM + 512]
            for t in tiles:
                hs = heads(H[:, t, :])
                e.vlink(V.tensor_tensor(sq[:], hs, hs, ALU.mult))
                e.vlink(V.reduce_sum(ms[:, t], sq[:], AX))
            V.tensor_scalar(ms[:, t0:TT], ms[:, t0:TT], 1.0 / P, None, ALU.mult).then_inc(s_ms, 1)
            dve.wait_ge(s_rs, 1)
            e.vlink(V.reciprocal(ms[:, t0:TT], ms[:, t0:TT]))
            for i, t in enumerate(tiles):
                hs = heads(H[:, t, :])
                e.vlink(V.tensor_tensor(hs, hs, e.bc(ms[:, t].unsqueeze(2), P, 4, P), ALU.mult))
                e.vlink(V.tensor_tensor(H[:, t, :], H[:, t, :], gm, ALU.mult))
                dve.wait_ge(s_sg, i + 1)
                V.tensor_tensor(H[:, t, :], H[:, t, :], sg[:, i % 2], ALU.mult).then_inc(s_oc, 1)
                dve.wait_ge(s_ot, i + 1)
                V.tensor_copy(m.cqT[:, :, t * P:t * P + P],
                              PS[:, 4 + i % 2, :].rearrange("p (j q) -> p j q", j=4)).then_inc(s_oev, 1)


def load_gate_rows(sp, a, l, which, dst, done):
    for v in range(2):
        sp.dma_start(dst[:, v], a["mod_rows"][l, v:v + 1, which * D:which * D + D].to_broadcast([P, D])).then_inc(done, 16)


def merge_stage(nc, a, e, m, l, tiles):
    V, A, T, PS, sem = e.V, e.A, e.T, e.PS, e.sem
    with ExitStack() as st:
        rows = e.sb(st, f"mix_rows{l}", [P, 2, D])
        Y = m.bkT[:]
        Y2 = m.ckT[:]
        YY = [Y, Y2]
        with nc.Block() as block:
            sg = e.sb(st, f"sig_g{l}", [P, 2, 512])
            s_g, s_b, s_sg, s_y, s_rows = (sem(f"{n}{l}") for n in (
                "gate_done", "branch_done", "gate_sigmoid", "y_updated", "mix_rows_loaded"))
            units = [(j, b, t) for j in range(2) for b in range(3) for t in tiles]
            srcs = [m.aqT, m.bqT, m.cqT]
            nt = len(tiles)
            for c in range(6):
                e.freed[PLACE[l, "merge", c]] = (s_b, nt * (c + 1))

            @block.sync
            def _(sp):
                load_gate_rows(sp, a, l, 2, rows, s_rows)
                e.sp_loads(sp, PLACE[l, "out", 0] + RING)
                sp.wait_ge(s_rows, 32)

            @block.tensor
            def _(pe):
                for u, (j, b, t) in enumerate(units):
                    w = e.chunk_ready(pe, PLACE[l, "merge", 3 * j + b])
                    if u >= 2:
                        pe.wait_ge(s_y, u - 1)
                    for k in range(KT):
                        last = T.matmul(PS[:, u % 2, :], e.hT[:, k, t * P:t * P + P], w[:, k * 512:k * 512 + 512],
                                        start=k == 0, stop=k == KT - 1)
                    last.then_inc(s_g, 1)
                    for k in range(4):
                        at = KT * 512 + k * 512
                        last = T.matmul(PS[:, 2 + u % 2, :], srcs[b][:, k, t * P:t * P + P], w[:, at:at + 512],
                                        start=k == 0, stop=k == 3)
                    last.then_inc(s_b, 1)

            @block.scalar
            def _(act):
                for u in range(len(units)):
                    act.wait_ge(s_g, u + 1)
                    if u >= 2:
                        act.wait_ge(s_y, u - 1)
                    A.activation(sg[:, u % 2], PS[:, u % 2, :], ACT.Sigmoid).then_inc(s_sg, 1)

            @block.vector
            def _(dve):
                for u, (j, b, t) in enumerate(units):
                    dve.wait_ge(s_sg, u + 1)
                    dve.wait_ge(s_b, u + 1)
                    if b == 0:
                        V.tensor_tensor(YY[j][:, t], PS[:, 2 + u % 2, :], sg[:, u % 2], ALU.mult).then_inc(s_y, 1)
                    else:
                        e.vlink(V.tensor_tensor(sg[:, u % 2], PS[:, 2 + u % 2, :], sg[:, u % 2], ALU.mult))
                        V.tensor_tensor(YY[j][:, t], YY[j][:, t], sg[:, u % 2], ALU.add).then_inc(s_y, 1)

        with nc.Block() as block:
            s_yt, s_ys, s_out, s_xu, s_om = (sem(f"{n}{l}") for n in (
                "yT", "yT_stored", "out_done", "x_updated", "out_gated"))
            YT = [m.aqT, m.bqT]
            og = e.sb(st, f"out_gated{l}", [P, 2, 512])
            for j in range(2):
                e.freed[PLACE[l, "out", j]] = (s_out, nt * (j + 1))

            @block.sync
            def _(sp):
                e.sp_loads(sp, PLACE[l, "shared", 0] + 1)

            @block.tensor
            def _(pe):
                i = 0
                for t in tiles:
                    for j in range(2):
                        if i >= 4:
                            pe.wait_ge(s_ys, i - 3)
                        for k in range(4):
                            last = T.transpose(PS[:, i % 4, k * P:k * P + P], YY[j][:, t, k * P:k * P + P], e.ident)
                        last.then_inc(s_yt, 1)
                        i += 1
                pe.wait_ge(s_ys, i)
                for u, (j, t) in enumerate((j, t) for j in range(2) for t in tiles):
                    w = e.chunk_ready(pe, PLACE[l, "out", j])
                    if u >= 4:
                        pe.wait_ge(s_om, u - 3)
                    for k in range(KT):
                        last = T.matmul(PS[:, 4 + u % 4, :], YT[k // 4][:, k % 4, t * P:t * P + P],
                                        w[:, k * 512:k * 512 + 512], start=k == 0, stop=k == KT - 1)
                    last.then_inc(s_out, 1)

            @block.scalar
            def _(act):
                i = 0
                for t in tiles:
                    for j in range(2):
                        act.wait_ge(s_yt, i + 1)
                        A.activation(YT[j][:, :, t * P:t * P + P], PS[:, i % 4, :].rearrange("p (k q) -> p k q", k=4),
                                     ACT.Copy).then_inc(s_ys, 1)
                        i += 1

            @block.vector
            def _(dve):
                for u, (j, t) in enumerate((j, t) for j in range(2) for t in tiles):
                    v = 0 if t < LAT0 else 1
                    dve.wait_ge(s_out, u + 1)
                    V.tensor_tensor(og[:, u % 2], PS[:, 4 + u % 4, :], rows[:, v, j * 512:j * 512 + 512],
                                    ALU.mult).then_inc(s_om, 1)
                    dve.wait_ge(s_om, u + 1)
                    xs = e.X[:, t, j * 512:j * 512 + 512]
                    V.tensor_tensor(xs, xs, og[:, u % 2], ALU.add).then_inc(s_xu, 1)


def moe(nc, a, e, l, tiles):
    with ExitStack() as st:
        slots = [e.ring[0], e.ring[1]] + [e.sb(st, f"weights{i}_{l}", [P, SLOT]) for i in range(RING, NSLOT)]
        nt = len(tiles)
        r = Space()
        r.shared = e.sb(st, f"shared_out{l}", [P, nt, D])
        r.rows = e.sb(st, f"moe_rows{l}", [P, 2, D])
        r.weight = e.sb(st, f"route_weight{l}", [P, nt, TOPK])
        r.yrow = e.sb(st, f"y_row_index{l}", [P, nt, TOPK], I32)
        r.posb = e.sb(st, f"slot_position{l}", [P, NBLK, nt, NE])
        r.tokid = e.sb(st, f"token_id{l}", [P, nt], FP16)
        r.tok = e.sb(st, f"slot_token{l}", [P, NE], I32)
        r.over = e.sb(st, f"overflow_table{l}", [1, 3, P], I32)
        r.gate = e.sb(st, f"route_gate{l}", [P, nt, NE])
        with ExitStack() as st2, nc.Block() as block:
            S = e.sb(st2, f"scores{l}", [P, nt, NE])
            shared_route_stage(nc, a, e, r, l, tiles, S, slots, st2, block)
        with ExitStack() as st2:
            b = Space()
            b.xg, b.y = (e.hT[:, i:i + 4].rearrange("p k t -> p (k t)").rearrange("p (i d) -> p i d", i=2) for i in (0, 4))
            b.xT = e.sb(st2, f"gatheredT{l}", [P, 2, KT, P])
            b.sl = e.sb(st2, f"silu{l}", [P, 2, DE])
            b.ac = e.sb(st2, f"act{l}", [P, 2, DE])
            b.acT = e.sb(st2, f"actT{l}", [P, 2, 2, P])
            b.idx = e.sb(st2, f"gather_index{l}", [P, 2], I32)
            experts_stage(nc, a, e, r, b, l, slots)
            overflow_stage(nc, a, e, r, b, l, nt, slots)
        combine_stage(nc, a, e, r, l, tiles)


def shared_route_stage(nc, a, e, r, l, tiles, S, slots, st, block):
    V, A, T, G, PS, sem = e.V, e.A, e.T, e.G, e.PS, e.sem
    n = PLACE[l, "shared", 0]
    nt = len(tiles)
    iota = e.iota
    EC = 4

    last_slot = slots[NSLOT - 1]
    at = [0]

    def carve(cols, *shape):
        ap = last_slot[:, at[0]:at[0] + cols]
        at[0] += cols
        if len(shape) == 2:
            return ap.rearrange("p (i d) -> p i d", i=shape[0])
        if len(shape) == 3:
            return ap.rearrange("p (i k d) -> p i k d", i=shape[0], k=shape[1])
        return ap

    wr = carve(KT * NE)
    ht = carve(2 * D, 2, D)
    sl, up, ac = (carve(2 * DE, 2, DE) for _ in range(3))
    acT = carve(2 * DE, 2, 2, P)
    s_wr, s_rt, s_ht, s_hta, s_g, s_sl, s_ac, s_h, s_at, s_dn, s_ya = (sem(f"{x}{l}") for x in (
        "w_router_loaded", "router_done", "h_transposed", "h_token_ready", "sh_gate_up", "sh_silu_done",
        "sh_act_ready", "sh_act_transposed", "sh_actT_ready", "sh_down", "sh_stored"))
    s_hs = [sem(f"h_rows_written{i}_{l}") for i in range(2)]
    s_rows, s_S = sem(f"moe_rows_loaded{l}"), sem(f"scores_ready{l}")
    e.freed[n] = (s_dn, nt)

    sel = e.sb(st, f"sel{l}", [P, nt, NE])
    top = e.sb(st, f"group_top{l}", [P, nt, NG, 8])
    gs = e.sb(st, f"group_score{l}", [P, nt, NG])
    v8 = e.sb(st, f"top_values{l}", [P, nt, 8])
    i8 = e.sb(st, f"top_index{l}", [P, nt, 8], U32)
    f8 = e.sb(st, f"top_index_f{l}", [P, nt, 8])
    ohg = e.sb(st, f"group_onehot{l}", [P, nt, 4, NG])
    gm = e.sb(st, f"group_mask{l}", [P, nt, NG])
    oh = e.sb(st, f"expert_onehot{l}", [P, nt, 8, NE])
    tmp = e.sb(st, f"route_tmp{l}", [P, 8, NE])
    M = e.sb(st, f"expert_mask{l}", [P, nt, NE])
    ws = e.sb(st, f"weight_sum{l}", [P, nt])
    p8 = e.sb(st, f"top_pos{l}", [P, nt, 8])
    one = e.sb(st, f"slot_onehot{l}", [P, 2, nt, EC, P], FP16)
    ov = e.sb(st, f"over_tmp{l}", [P, 4, 3, NE])
    oc = e.sb(st, f"over_cols{l}", [P, 3])
    s_m, s_pos, s_one, s_tok, s_oc, s_or, s_c = (sem(f"{x}{l}") for x in (
        "masks_ready", "positions_done", "onehot_ready", "tokens_done", "over_cols_ready", "over_rows_done",
        "counts_done"))
    rank_ps, count_ps = PS[:, 7, 4 * NE:4 * NE + nt * NE], PS[:, 7, 0:NE]
    tok_ps, over_ps = PS[:, 7, NE:2 * NE], PS[0:1, 7, 2 * NE:2 * NE + 3 * P]

    @block.sync
    def _(sp):
        def expert(q):
            sp.dma_start(slots[q][:], a["wexp"][l, q]).then_inc(e.ld[q], 16)

        sp.dma_start(wr, a["wr"][l]).then_inc(s_wr, 16)
        load_gate_rows(sp, a, l, 5, r.rows, s_rows)
        expert((n + 1) % RING)
        expert(2)
        for i, t in enumerate(tiles):
            sp.wait_ge(s_hta, i + 1)
            sp.dma_start(a["h_rows"][t * P:t * P + P, :], ht[:, i % 2]).then_inc(s_hs[i % 2], 16)
        sp.wait_ge(s_dn, nt)
        expert(n % RING)
        for i in range(2):
            sp.wait_ge(s_hs[i], 16 * (nt // 2))
        sp.wait_ge(s_S, 1)
        expert(3)
        sp.wait_ge(s_rows, 32)

    @block.vector
    def _(dve):
        dve.wait_ge(s_S, 1)
        e.vlink(V.tensor_tensor(sel[:], S[:], e.bc(e.rowp[:, R_BROUTER:R_BROUTER + NE].unsqueeze(1), P, nt, NE), ALU.add))
        for i in range(nt):
            for g in range(NG):
                last = V.max(top[:, i, g], sel[:, i, g * PER:g * PER + PER])
        e.vlink(last)
        e.vlink(V.tensor_tensor(gs[:], top[:, :, :, 0], top[:, :, :, 1], ALU.add))
        for i in range(nt):
            last = V.max(v8[:, i], gs[:, i])
        e.vlink(last)
        for i in range(nt):
            last = V.max_index(i8[:, i], v8[:, i], gs[:, i])
        e.vlink(last)
        e.vlink(V.tensor_copy(f8[:], i8[:]))
        e.vlink(V.tensor_tensor(ohg[:], e.bc(iota[:, 0:NG].unsqueeze(1).unsqueeze(1), P, nt, 4, NG),
                                e.bc(f8[:, :, 0:4].unsqueeze(3), P, nt, 4, NG), ALU.is_equal))
        e.vlink(V.reduce_sum(gm[:], ohg[:].rearrange("p t k g -> p t g k"), AX))
        e.vlink(V.tensor_scalar(gm[:], gm[:], BIG, -BIG, ALU.mult, ALU.add))
        e.vlink(V.tensor_tensor(sel[:].rearrange("p t (g e) -> p t g e", g=NG),
                                sel[:].rearrange("p t (g e) -> p t g e", g=NG),
                                e.bc(gm[:].unsqueeze(3), P, nt, NG, PER), ALU.add))
        for i in range(nt):
            last = V.max(v8[:, i], sel[:, i])
        e.vlink(last)
        for i in range(nt):
            last = V.max_index(i8[:, i], v8[:, i], sel[:, i])
        e.vlink(last)
        e.vlink(V.tensor_copy(f8[:], i8[:]))
        for i in range(nt):
            e.vlink(V.tensor_tensor(oh[:, i], e.bc(iota[:, 0:NE].unsqueeze(1), P, 8, NE),
                                    e.bc(f8[:, i].unsqueeze(2), P, 8, NE), ALU.is_equal))
            V.reduce_sum(M[:, i], oh[:, i].rearrange("p k e -> p e k"), AX).then_inc(s_m, 1)
            e.vlink(V.tensor_tensor(tmp[:], oh[:, i], e.bc(S[:, i].unsqueeze(1), P, 8, NE), ALU.mult))
            e.vlink(V.reduce_sum(r.weight[:, i], tmp[:], AX))
        e.vlink(V.reduce_sum(ws[:], r.weight[:], AX))
        e.vlink(V.reciprocal(ws[:], ws[:]))
        e.vlink(V.tensor_scalar(ws[:], ws[:], ROUTED_SCALE, None, ALU.mult))
        e.vlink(V.tensor_tensor(r.weight[:], r.weight[:], e.bc(ws[:].unsqueeze(2), P, nt, 8), ALU.mult))
        for i in range(nt):
            e.vlink(V.tensor_tensor(tmp[:], oh[:, i], e.bc(r.weight[:, i].unsqueeze(2), P, 8, NE), ALU.mult))
            e.vlink(V.reduce_sum(r.gate[:, i], tmp[:].rearrange("p k e -> p e k"), AX))
        e.vlink(V.tensor_copy(r.tokid[:], e.cst[:, C_TOK + tiles[0]:C_TOK + TT]))
        dve.wait_ge(s_pos, 1)
        pos = r.posb[:, 0]
        rank = rank_ps.rearrange("p (t e) -> p t e", t=nt)
        e.vlink(V.tensor_tensor(pos, rank, M[:], ALU.mult))
        e.vlink(V.tensor_scalar(pos, pos, -1.0, None, ALU.add))
        for b in range(1, NBLK):
            V.tensor_scalar(r.posb[:, b], pos, -float(b * P), None, ALU.add)
        for i in range(nt):
            e.vlink(V.tensor_tensor(tmp[:], oh[:, i], e.bc(pos[:, i].unsqueeze(1), P, 8, NE), ALU.mult))
            e.vlink(V.reduce_sum(p8[:, i], tmp[:], AX))
        e.vlink(V.scalar_tensor_tensor(r.weight[:], p8[:], float(P), r.weight[:], ALU.is_lt, ALU.mult))
        e.vlink(V.tensor_scalar(p8[:], p8[:], float(P - 1), None, ALU.min))
        e.vlink(V.scalar_tensor_tensor(p8[:], f8[:], float(P), p8[:], ALU.mult, ALU.add))
        e.vlink(V.tensor_copy(r.yrow[:], p8[:]))
        cnt = ov[:, 3, 0]
        e.vlink(V.tensor_copy(cnt, count_ps))
        flag, cum = ov[:, 0], ov[:, 1]
        for b in range(3):
            last = V.tensor_scalar(flag[:, b], cnt, float((b + 1) * P), None, ALU.is_gt)
        e.vlink(last)
        fl = flag.rearrange("p b e -> p (b e)")
        cf = cum.rearrange("p b e -> p (b e)")
        ovt = ov[:, 2].rearrange("p b e -> p (b e)")
        e.vlink(V.tensor_tensor_scan(cf, e.bc(e.ones[:, 0:1], P, 3 * NE), fl, 0.0, ALU.mult, ALU.add))
        e.vlink(V.tensor_copy(oc[:, 2:3], cf[:, 3 * NE - 1:3 * NE]))
        e.vlink(V.scalar_tensor_tensor(cf, cf, e.cst[:, C_PIDX1:C_PIDX1 + 1], fl, ALU.is_equal, ALU.mult))
        for c in range(2):
            e.vlink(V.tensor_tensor(ovt, cf, e.cst[:, C_OVER + c * 192:C_OVER + c * 192 + 192], ALU.mult))
            e.vlink(V.reduce_sum(oc[:, c:c + 1], ovt, AX))
        V.scalar_tensor_tensor(oc[:, 1:2], oc[:, 1:2], float(nt * NE), oc[:, 0:1], ALU.mult, ALU.add
                               ).then_inc(s_oc, 1)
        for c in range(NE // EC):
            if c >= 2:
                dve.wait_ge(s_tok, c - 1)
            V.tensor_tensor(one[:, c % 2], e.bc(iota.unsqueeze(1).unsqueeze(1), P, nt, EC, P),
                            e.bc(pos[:, :, c * EC:c * EC + EC].unsqueeze(3), P, nt, EC, P), ALU.is_equal
                            ).then_inc(s_one, 1)
        dve.wait_ge(s_or, 1)
        dve.wait_ge(s_tok, NE // EC)
        V.tensor_copy(r.over[:], over_ps.rearrange("p (c i) -> p c i", c=3))
        V.tensor_copy(r.tok[:], tok_ps)

    @block.tensor
    def _(pe):
        pe.wait_ge(s_wr, 16)
        for i, t in enumerate(tiles):
            for k in range(KT):
                last = T.matmul(PS[:, 7, i * NE:i * NE + NE], e.hT[:, k, t * P:t * P + P],
                                wr[:, k * NE:k * NE + NE], start=k == 0, stop=k == KT - 1)
        last.then_inc(s_rt, 1)
        w = e.chunk_ready(pe, n)

        def ranks():
            pe.wait_ge(s_m, nt)
            for i in range(nt):
                for j in range(i + 1):
                    T.matmul(rank_ps[:, i * NE:i * NE + NE], e.cst[:, C_LE:C_LE + P] if j == i else e.ones, M[:, j],
                             start=j == 0, stop=j == i)
            for j in range(nt):
                last = T.matmul(count_ps, e.ones, M[:, j], start=j == 0, stop=j == nt - 1)
            last.then_inc(s_pos, 1)

        for i, t in enumerate(tiles):
            if i >= 1:
                pe.wait_ge(s_hta, i)
            for k in range(KT):
                last = T.transpose(PS[:, k // 4, (k % 4) * P:(k % 4) * P + P], e.hT[:, k, t * P:t * P + P], e.ident)
            last.then_inc(s_ht, 1)
            for k in range(KT):
                last = T.matmul(PS[:, 2 + i % 2, :], e.hT[:, k, t * P:t * P + P], w[:, k * 512:k * 512 + 512],
                                start=k == 0, stop=k == KT - 1)
            last.then_inc(s_g, 1)
            pe.wait_ge(s_ac, i + 1)
            for k in range(2):
                last = T.transpose(PS[:, 6, k * P:k * P + P], ac[:, i % 2, k * P:k * P + P], e.ident)
            last.then_inc(s_h, 1)
            pe.wait_ge(s_at, i + 1)
            if i >= 1:
                pe.wait_ge(s_ya, i)
            for j in range(2):
                for k in range(2):
                    x = KT * 512 + k * D + j * 512
                    last = T.matmul(PS[:, 4 + j, :], acT[:, i % 2, k], w[:, x:x + 512], start=k == 0, stop=k == 1)
            last.then_inc(s_dn, 1)
            if i == nt // 2 - 1:
                ranks()
        pe.wait_ge(s_oc, 1)
        for c in range(3):
            last = T.matmul(over_ps[:, c * P:c * P + P], oc[:, c:c + 1], e.ident, start=True, stop=True)
        last.then_inc(s_or, 1)
        for c in range(NE // EC):
            pe.wait_ge(s_one, c + 1)
            for x in range(EC):
                for i in range(nt):
                    last = T.matmul(tok_ps[:, c * EC + x:c * EC + x + 1], one[:, c % 2, i, x], r.tokid[:, i:i + 1],
                                    start=i == 0, stop=i == nt - 1)
            last.then_inc(s_tok, 1)

    @block.scalar
    def _(act):
        act.wait_ge(s_rt, 1)
        A.activation(S[:].rearrange("p t e -> p (t e)"), PS[:, 7, 0:nt * NE], ACT.Sigmoid).then_inc(s_S, 1)
        for i, t in enumerate(tiles):
            act.wait_ge(s_ht, i + 1)
            if i >= 2:
                act.wait_ge(s_hs[i % 2], 16 * (i // 2))
            A.activation(ht[:, i % 2, 0:512], PS[:, 0, :], ACT.Copy)
            A.activation(ht[:, i % 2, 512:D], PS[:, 1, :], ACT.Copy).then_inc(s_hta, 1)
            act.wait_ge(s_g, i + 1)
            if i >= 2:
                act.wait_ge(s_ac, i - 1)
            A.activation(sl[:, i % 2], PS[:, 2 + i % 2, 0:DE], ACT.Silu)
            A.activation(up[:, i % 2], PS[:, 2 + i % 2, DE:2 * DE], ACT.Copy).then_inc(s_sl, 1)
            act.wait_ge(s_h, i + 1)
            A.activation(acT[:, i % 2].rearrange("p k t -> p (k t)"), PS[:, 6, 0:2 * P], ACT.Copy).then_inc(s_at, 1)
            act.wait_ge(s_dn, i + 1)
            A.activation(r.shared[:, i, 0:512], PS[:, 4, :], ACT.Copy)
            A.activation(r.shared[:, i, 512:D], PS[:, 5, :], ACT.Copy).then_inc(s_ya, 1)

    @block.gpsimd
    def _(pool):
        for i in range(nt):
            pool.wait_ge(s_sl, i + 1)
            if i >= 2:
                pool.wait_ge(s_h, i - 1)
            G.tensor_tensor(ac[:, i % 2], sl[:, i % 2], up[:, i % 2], ALU.mult).then_inc(s_ac, 1)


def experts_stage(nc, a, e, r, b, l, slots):
    V, A, T, G, PS, sem = e.V, e.A, e.T, e.G, e.PS, e.sem
    with nc.Block() as block:
        s_t, s_xe, s_g, s_sl, s_ac, s_h, s_at, s_dn, s_ye, s_pi = (sem(f"{x}{l}") for x in (
            "tokens_transposed", "tokensT_ready", "gate_up_done", "silu_done", "act_ready", "act_transposed",
            "actT_ready", "down_done", "y_ready", "gather_index_ready"))
        s_xg = [e.kept_sem(f"tokens_gathered{i}_{l}") for i in range(2)]
        s_st = [sem(f"y_stored{i}_{l}") for i in range(2)]
        base = [16 * e.loads[q] for q in range(NSLOT)]
        for q in range(NSLOT):
            e.loads[q] += NE // NSLOT

        def groups(eng, body):
            with eng.Fori(0, NE // NSLOT - 1) as g:
                for q in range(NSLOT):
                    body(g, q)
            for q in range(NSLOT):
                body(NE // NSLOT - 1, q)

        def later(g, q, by):
            gg, qq = g + (q + by) // NSLOT, (q + by) % NSLOT
            return None if isinstance(g, int) and gg >= NE // NSLOT else (gg, qq)

        @block.sync
        def _(sp):
            with sp.Fori(1, NE // NSLOT) as g:
                for q in range(NSLOT):
                    sp.wait_ge(s_dn, 4 * g + q - 3 + 2)
                    sp.wait_ge(e.ld[q], 16)
                    sp.dma_start(slots[q][:], a["wexp"][l, g * NSLOT + q]).then_inc(e.ld[q], 16)

        @block.gpsimd
        def _(pool):
            def gather(g, q):
                p = q % 2
                pool.wait_ge(s_t, 4 * g + q + 1)
                G.tensor_copy(b.idx[:, p:p + 1], r.tok[:, bass.ds(g * NSLOT + q, 1)]).then_inc(s_pi, 1)
                pool.wait_ge(s_pi, 1)
                pool.sem_clear(s_pi)
                G.indirect_dma_start(b.xg[:, p], None, a["h_rows"],
                                     bass.IndirectOffsetOnAxis(ap=b.idx[:, p:p + 1], axis=0)).then_inc(s_xg[p], 16)
            groups(pool, gather)

        @block.tensor
        def _(pe):
            pe.sem_inc(s_t, 2)
            pe.sem_inc(s_g, 2)
            pe.sem_inc(s_h, 2)
            pe.sem_inc(s_dn, 2)

            def tokens(g, q):
                p = q % 2
                pe.wait_ge(s_xg[p], 32 * g + 16 * (q // 2 + 1))
                pe.wait_ge(s_xe, 8 * g + 2 * q + 2)
                for k in range(KT):
                    last = T.transpose(PS[:, k // 4, (k % 4) * P:(k % 4) * P + P], b.xg[:, p, k * P:k * P + P], e.ident)
                last.then_inc(s_t, 1)

            def gate_up(g, q):
                p = q % 2
                pe.wait_ge(e.ld[q], base[q] + 16 * g + 16)
                pe.wait_ge(s_xe, 8 * g + 2 * q + 4)
                pe.wait_ge(s_ac, 4 * g + q + 1)
                for k in range(KT):
                    last = T.matmul(PS[:, 2 + p, :], b.xT[:, p, k], slots[q][:, k * 512:k * 512 + 512],
                                    start=k == 0, stop=k == KT - 1)
                last.then_inc(s_g, 1)

            def act_t(g, q):
                p = q % 2
                pe.wait_ge(s_ac, 4 * g + q + 3)
                pe.wait_ge(s_at, 4 * g + q + 1)
                for k in range(2):
                    last = T.transpose(PS[:, 6, k * P:k * P + P], b.ac[:, p, k * P:k * P + P], e.ident)
                last.then_inc(s_h, 1)

            def down(g, q):
                p = q % 2
                pe.wait_ge(s_at, 4 * g + q + 2)
                pe.wait_ge(s_ye, 8 * g + 2 * q + 2)
                for j in range(2):
                    for k in range(2):
                        at = KT * 512 + k * D + j * 512
                        last = T.matmul(PS[:, 4 + j, :], b.acT[:, p, k], slots[q][:, at:at + 512],
                                        start=k == 0, stop=k == 1)
                last.then_inc(s_dn, 1)

            def step(g, q):
                if n := later(g, q, 1):
                    gate_up(*n)
                act_t(g, q)
                if n := later(g, q, 2):
                    tokens(*n)
                down(g, q)

            tokens(0, 0)
            tokens(0, 1)
            gate_up(0, 0)
            groups(pe, step)

        @block.scalar
        def _(act):
            act.sem_inc(s_xe, 2)
            act.sem_inc(s_ye, 2)
            act.sem_inc(s_st[0], 16)
            act.sem_inc(s_st[1], 16)

            def tokens(g, q):
                p = q % 2
                act.wait_ge(s_t, 4 * g + q + 3)
                act.wait_ge(s_g, 4 * g + q + 1)
                A.activation(b.xT[:, p, 0:4].rearrange("p k t -> p (k t)"), PS[:, 0, :], ACT.Copy).then_inc(s_xe, 1)

            def silu(g, q):
                p = q % 2
                act.wait_ge(s_g, 4 * g + q + 3)
                act.wait_ge(s_ac, 4 * g + q + 1)
                A.activation(b.sl[:, p], PS[:, 2 + p, 0:DE], ACT.Silu).then_inc(s_sl, 1)

            def store(g, q):
                p = q % 2
                act.wait_ge(s_dn, 4 * g + q + 3)
                act.wait_ge(s_st[p], 32 * g + 16 * (q // 2) + 16)
                A.activation(b.y[:, p, 0:512], PS[:, 4, :], ACT.Copy).then_inc(s_ye, 1)
                act.wait_ge(s_ye, 8 * g + 2 * q + 4)
                act.dma_start(a["y_rows"].rearrange("(x r) d -> x r d", r=P)[g * NSLOT + q], b.y[:, p]
                              ).then_inc(s_st[p], 16)

            def step(g, q):
                if n := later(g, q, 1):
                    silu(*n)
                if n := later(g, q, 2):
                    tokens(*n)
                store(g, q)

            tokens(0, 0)
            tokens(0, 1)
            silu(0, 0)
            groups(act, step)
            for p in range(2):
                act.wait_ge(s_st[p], 16 * (NE // 2) + 16)

        @block.vector
        def _(dve):
            dve.sem_inc(s_ac, 2)
            dve.sem_inc(s_at, 1)

            def tokens(g, q):
                p = q % 2
                dve.wait_ge(s_t, 4 * g + q + 3)
                dve.wait_ge(s_g, 4 * g + q + 1)
                V.tensor_copy(b.xT[:, p, 4:KT].rearrange("p k t -> p (k t)"), PS[:, 1, :]).then_inc(s_xe, 1)

            def product(g, q):
                p = q % 2
                dve.wait_ge(s_sl, 4 * g + q + 1)
                dve.wait_ge(s_h, 4 * g + q + 1)
                V.tensor_tensor(b.ac[:, p], b.sl[:, p], PS[:, 2 + p, DE:2 * DE], ALU.mult).then_inc(s_ac, 1)

            def act_t(g, q):
                p = q % 2
                dve.wait_ge(s_h, 4 * g + q + 3)
                dve.wait_ge(s_dn, 4 * g + q + 1)
                V.tensor_copy(b.acT[:, p].rearrange("p k t -> p (k t)"), PS[:, 6, 0:2 * P]).then_inc(s_at, 1)

            def store(g, q):
                p = q % 2
                dve.wait_ge(s_dn, 4 * g + q + 3)
                dve.wait_ge(s_st[p], 32 * g + 16 * (q // 2) + 16)
                V.tensor_copy(b.y[:, p, 512:D], PS[:, 5, :]).then_inc(s_ye, 1)

            def step(g, q):
                act_t(g, q)
                if n := later(g, q, 1):
                    product(*n)
                if n := later(g, q, 2):
                    tokens(*n)
                store(g, q)

            tokens(0, 0)
            tokens(0, 1)
            product(0, 0)
            groups(dve, step)


def overflow_stage(nc, a, e, r, b, l, nt, slots):
    V, A, T, G, PS, sem = e.V, e.A, e.T, e.G, e.PS, e.sem
    with ExitStack() as st, nc.Block() as block:
        pc = e.sb(st, f"over_pos{l}", [P, 2, nt])
        one = e.sb(st, f"over_onehot{l}", [P, nt, P], FP16)
        wone, woneT = (slots[1][:, i * nt * P:(i + 1) * nt * P].rearrange("p (t s) -> p t s", t=nt) for i in range(2))
        s_w, s_pc, s_one, s_tok, s_idx, s_t, s_xe, s_g, s_sl, s_ac, s_h, s_at, s_dn, s_ye, s_wt, s_wte, s_y, s_end = (
            sem(f"o_{x}{l}") for x in (
                "weights_loaded", "columns_ready", "onehot_ready", "tokens_found", "index_ready", "transposed",
                "xT_ready", "gate_up", "silu", "act", "actT", "actT_ready", "down", "y_ready", "weighted_transposed",
                "weightedT_ready", "y_at_tokens", "item_done"))
        s_xg = e.kept_sem(f"o_gathered_{l}")

        def items(eng, body, to_the_end=True):
            n = eng.value_load(r.over[0:1, 2, 0:1], min_val=0, max_val=MAXOVER)
            with eng.If(n > 0):
                with eng.Fori(0, n) as i:
                    body(i)
                    if to_the_end:
                        eng.wait_ge(s_end, i + 1)
                eng.nop()

        def field(eng, c, i, most):
            return eng.value_load(r.over[0:1, c, bass.ds(i, 1)], min_val=0, max_val=most)

        @block.sync
        def _(sp):
            def body(i):
                x = field(sp, 0, i, NE - 1)
                sp.wait_ge(s_dn, i + 1)
                sp.dma_start(slots[0][:], a["wexp"][l, x]).then_inc(s_w, 16)
            items(sp, body, False)

        @block.gpsimd
        def _(pool):
            def body(i):
                pool.wait_ge(s_idx, 1)
                pool.sem_clear(s_idx)
                G.indirect_dma_start(b.xg[:, 0], None, a["h_rows"],
                                     bass.IndirectOffsetOnAxis(ap=b.idx[:, 0:1], axis=0)).then_inc(s_xg, 16)
            items(pool, body)

        @block.vector
        def _(dve):
            def body(i):
                x = field(dve, 0, i, NE - 1)
                at = field(dve, 1, i, (NBLK - 1) * nt * NE + NE - 1)
                for t in range(nt):
                    V.tensor_copy(pc[:, 0, t:t + 1], r.posb[:].rearrange("p b t e -> p (b t e)")[:, bass.ds(at + t * NE, 1)])
                    last = V.tensor_copy(pc[:, 1, t:t + 1], r.gate[:, t, bass.ds(x, 1)])
                last.then_inc(s_pc, 1)
                dve.wait_ge(s_pc, i + 1)
                V.tensor_tensor(one[:], e.bc(e.iota.unsqueeze(1), P, nt, P), e.bc(pc[:, 0].unsqueeze(2), P, nt, P),
                                ALU.is_equal).then_inc(s_one, 1)
                dve.wait_ge(s_one, 2 * i + 1)
                V.tensor_tensor(wone, one[:], e.bc(pc[:, 1].unsqueeze(2), P, nt, P), ALU.mult).then_inc(s_one, 1)
                dve.wait_ge(s_tok, i + 1)
                V.tensor_copy(b.idx[:, 0:1], PS[:, 7, 0:1]).then_inc(s_idx, 1)
                dve.wait_ge(s_t, i + 1)
                V.tensor_copy(b.xT[:, 0, 4:KT].rearrange("p k t -> p (k t)"), PS[:, 1, :]).then_inc(s_xe, 1)
                dve.wait_ge(s_sl, i + 1)
                V.tensor_tensor(b.ac[:, 0], b.sl[:, 0], PS[:, 2, DE:2 * DE], ALU.mult).then_inc(s_ac, 1)
                dve.wait_ge(s_h, i + 1)
                V.tensor_copy(b.acT[:, 0].rearrange("p k t -> p (k t)"), PS[:, 6, 0:2 * P]).then_inc(s_at, 1)
                dve.wait_ge(s_dn, i + 2)
                V.tensor_copy(b.y[:, 0, 512:D], PS[:, 5, :]).then_inc(s_ye, 1)
                dve.wait_ge(s_y, i + 1)
                for t in range(nt):
                    for j in range(2):
                        ys = r.shared[:, t, j * 512:j * 512 + 512]
                        last = V.tensor_tensor(ys, ys, PS[:, 2 * t + j, :], ALU.add)
                last.then_inc(s_end, 1)
            items(dve, body)

        @block.tensor
        def _(pe):
            pe.sem_inc(s_dn, 1)

            def body(i):
                pe.wait_ge(s_one, 2 * i + 2)
                for t in range(nt):
                    last = T.matmul(PS[:, 7, 0:1], one[:, t], r.tokid[:, t:t + 1], start=t == 0, stop=t == nt - 1)
                last.then_inc(s_tok, 1)
                for t in range(nt):
                    last = T.transpose(PS[:, 3, t * P:t * P + P], wone[:, t], e.ident)
                last.then_inc(s_wt, 1)
                pe.wait_ge(s_xg, 16 * i + 16)
                for k in range(KT):
                    last = T.transpose(PS[:, k // 4, (k % 4) * P:(k % 4) * P + P], b.xg[:, 0, k * P:k * P + P], e.ident)
                last.then_inc(s_t, 1)
                pe.wait_ge(s_w, 16 * i + 16)
                pe.wait_ge(s_xe, 2 * i + 2)
                for k in range(KT):
                    last = T.matmul(PS[:, 2, :], b.xT[:, 0, k], slots[0][:, k * 512:k * 512 + 512],
                                    start=k == 0, stop=k == KT - 1)
                last.then_inc(s_g, 1)
                pe.wait_ge(s_ac, i + 1)
                for k in range(2):
                    last = T.transpose(PS[:, 6, k * P:k * P + P], b.ac[:, 0, k * P:k * P + P], e.ident)
                last.then_inc(s_h, 1)
                pe.wait_ge(s_at, i + 1)
                for j in range(2):
                    for k in range(2):
                        at = KT * 512 + k * D + j * 512
                        last = T.matmul(PS[:, 4 + j, :], b.acT[:, 0, k], slots[0][:, at:at + 512],
                                        start=k == 0, stop=k == 1)
                last.then_inc(s_dn, 1)
                pe.wait_ge(s_wte, i + 1)
                pe.wait_ge(s_ye, 2 * i + 2)
                for t in range(nt):
                    for j in range(2):
                        last = T.matmul(PS[:, 2 * t + j, :], woneT[:, t], b.y[:, 0, j * 512:j * 512 + 512],
                                        start=True, stop=True)
                last.then_inc(s_y, 1)
            items(pe, body)

        @block.scalar
        def _(act):
            def body(i):
                act.wait_ge(s_wt, i + 1)
                A.activation(woneT.rearrange("p t s -> p (t s)"), PS[:, 3, 0:nt * P], ACT.Copy).then_inc(s_wte, 1)
                act.wait_ge(s_t, i + 1)
                A.activation(b.xT[:, 0, 0:4].rearrange("p k t -> p (k t)"), PS[:, 0, :], ACT.Copy).then_inc(s_xe, 1)
                act.wait_ge(s_g, i + 1)
                A.activation(b.sl[:, 0], PS[:, 2, 0:DE], ACT.Silu).then_inc(s_sl, 1)
                act.wait_ge(s_dn, i + 2)
                A.activation(b.y[:, 0, 0:512], PS[:, 4, :], ACT.Copy).then_inc(s_ye, 1)
            items(act, body)


def combine_stage(nc, a, e, r, l, tiles):
    V, A, T, G, PS, sem = e.V, e.A, e.T, e.G, e.PS, e.sem
    NB = 4
    with ExitStack() as st, nc.Block() as block:
        yk = e.sb(st, f"y_gathered{l}", [P, NB, D])
        s_yk = [e.kept_sem(f"y_gathered{i}_{l}") for i in range(NB)]
        s_acc = sem(f"y_added{l}")
        units = [(i, k) for i in range(len(tiles)) for k in range(TOPK)]

        @block.sync
        def _(sp):
            if l < L - 1:
                e.sp_loads(sp, PLACE[l + 1, "in", 0] + RING)

        @block.gpsimd
        def _(pool):
            for u, (i, k) in enumerate(units):
                if u >= NB:
                    pool.wait_ge(s_acc, u - NB + 1)
                G.indirect_dma_start(yk[:, u % NB], None, a["y_rows"],
                                     bass.IndirectOffsetOnAxis(ap=r.yrow[:, i, k:k + 1], axis=0)
                                     ).then_inc(s_yk[u % NB], 16)

        @block.vector
        def _(dve):
            for u, (i, k) in enumerate(units):
                dve.wait_ge(s_yk[u % NB], 16 * (u // NB + 1))
                V.scalar_tensor_tensor(r.shared[:, i], yk[:, u % NB], r.weight[:, i, k:k + 1], r.shared[:, i],
                                       ALU.mult, ALU.add).then_inc(s_acc, 1)
                dve.wait_ge(s_acc, u + 1)
                if k == TOPK - 1:
                    t = tiles[i]
                    v = 0 if t < LAT0 else 1
                    e.vlink(V.tensor_tensor(r.shared[:, i], r.shared[:, i], r.rows[:, v], ALU.mult))
                    V.tensor_tensor(e.X[:, t], e.X[:, t], r.shared[:, i], ALU.add)


def final_norm(nc, a, e):
    V, A, T, PS, sem = e.V, e.A, e.T, e.PS, e.sem
    with ExitStack() as st, nc.Block() as block:
        g = e.sb(st, "g_final", [P, D])
        sq = e.sb(st, "final_sq", [P, 2, D])
        ms = e.sb(st, "final_ms", [P, 2])
        s_g, s_y, s_o = sem("g_final_loaded"), sem("final_ready"), e.s_written
        s_ms, s_rs = sem("final_mean_square"), sem("final_inv_rms")

        @block.sync
        def _(sp):
            sp.dma_start(g[:], a["gfinal"]).then_inc(s_g, 16)
            for i in range(2):
                sp.wait_ge(s_y, i + 1)
                sp.dma_start(a["out"][i * P:i * P + P, :], e.X[:, LAT0 + i]).then_inc(s_o, 16)
            sp.wait_ge(s_o, 32)

        @block.vector
        def _(dve):
            dve.wait_ge(s_g, 16)
            for i in range(2):
                x = e.X[:, LAT0 + i]
                V.tensor_tensor_reduce(out=sq[:, i], in0=x, in1=x, scale=1.0 / D, scalar=0.0, op0=ALU.mult,
                                       op1=ALU.add, accum_out=ms[:, i:i + 1]).then_inc(s_ms, 1)
            dve.wait_ge(s_ms, 2)
            dve.wait_ge(s_rs, 1)
            e.vlink(V.reciprocal(ms[:], ms[:]))
            for i in range(2):
                x = e.X[:, LAT0 + i]
                V.scalar_tensor_tensor(x, x, ms[:, i:i + 1], g[:], ALU.mult, ALU.mult).then_inc(s_y, 1)

        @block.scalar
        def _(act):
            act.wait_ge(s_ms, 2)
            A.activation(ms[:], ms[:], ACT.Sqrt, bias=e.eps).then_inc(s_rs, 1)


def constants():
    import numpy as np
    c = np.zeros((P, NCONST), np.float32)
    i = np.arange(P)
    c[:, C_ID:C_ID + P] = np.eye(P)
    c[:, C_ONES:C_ONES + P] = 1
    c[:, C_LE:C_LE + P] = i[:, None] <= i[None, :]
    c[:, C_GE:C_GE + P] = i[:, None] >= i[None, :]
    q = DH // 4
    half = (i // q) % 2
    for p in range(P):
        if half[p] == 0:
            c[p + q, C_ROT + p] = -1
        else:
            c[p - q, C_ROT + p] = 1
    tok = np.arange(NLAT)
    inv = (1.0 / (np.float32(10000.0) ** (np.arange(q, dtype=np.float32) / np.float32(q)))).astype(np.float32)
    pos = np.stack([tok // 64, tok % 64]).astype(np.float32)
    ang = pos[(i % DH) // (2 * q)] * inv[i % q][:, None]
    c[:, C_COS:C_COS + NLAT] = np.cos(ang.astype(np.float32))
    c[:, C_SIN:C_SIN + NLAT] = np.sin(ang.astype(np.float32))
    for b in range(2):
        at = C_BAND + b * NTOK + NCTX
        c[:, at:at + NLAT] = np.where(np.abs(i[:, None] + b * P - tok[None, :]) <= 128, 0.0, -BIG)
    c[:, C_MF:C_MF + P] = np.where(i[:, None] >= i[None, :], 0.0, -BIG)
    c[:, C_MB:C_MB + P] = np.where(i[:, None] <= i[None, :], 0.0, -BIG)
    c[:, C_IOTA:C_IOTA + P] = i[None, :]
    c[:, C_TOK:C_TOK + TT] = i[:, None] + P * np.arange(TT)[None, :]
    c[:, C_PIDX1] = i + 1
    b, x = np.divmod(np.arange(3 * NE), NE)
    c[:, C_OVER:C_OVER + 192] = x
    c[:, C_OVER + 192:C_OVER + 384] = b + 1
    return c


def pack(w, out=None):
    import numpy as np
    k, n = w.shape[0] // P, w.shape[1]
    return np.ascontiguousarray(w.reshape(k, P, n).transpose(1, 0, 2)).reshape(P, k * n)


def kernel(x, c, ctx, c_ctx, w_mod, b_mod, g_mix, g_ffn, w_in, b_gate, sink, lam_q1, lam_k1,
           lam_q2, lam_k2, g_diff, g_mlstm, w_a, w_b, w_c, w_out, w_router, b_router,
           w_exp_gate, w_exp_up, w_exp_down, w_sh_gate, w_sh_up, w_sh_down, g_final):
    import numpy as np
    import concourse.bacc as bacc
    from concourse.bass_utils import run_bass_kernel_spmd as run

    f = np.float32
    w_in = np.asarray(w_in)
    d = {}
    d["x"] = np.concatenate([np.asarray(ctx)[0], np.asarray(x)[0]], 0)
    d["cond"] = np.ascontiguousarray(np.stack([np.asarray(c_ctx), np.asarray(c)[0]], -1).reshape(KT, P, 2).transpose(1, 0, 2))
    d["const"] = constants()
    aq = np.concatenate([np.arange(h * DH, h * DH + DH) for j in range(4) for h in (j, j + 4)])
    o = np.cumsum([0, 512, 128, 128, 512, 512, 512, 512, 512, 512, 512, 16, 3072])
    r = [np.arange(o[i], o[i + 1]) for i in range(12)]
    cols = [aq, r[3], r[4], r[6], r[7], np.concatenate([r[1], r[2], r[10]]), r[5], r[8], r[9]]
    wseq = np.zeros((len(SEQ), P, SLOT), f)
    for n, (l, kind, i) in enumerate(SEQ):
        dst = wseq[n]
        if kind == "mod":
            dst[:, :KT * 512] = pack(np.asarray(w_mod[l])[:, i * 512:i * 512 + 512])
        elif kind == "in":
            dst[:, :KT * len(cols[i])] = pack(w_in[l][:, cols[i]])
        elif kind == "merge":
            j, b = divmod(i, 3)
            gc = o[11] + b * D + j * 512
            dst[:, :KT * 512] = pack(w_in[l][:, gc:gc + 512])
            dst[:, KT * 512:] = pack(np.asarray((w_a, w_b, w_c)[b])[l][:, j * 512:j * 512 + 512])
        elif kind == "out":
            dst[:, :KT * 512] = pack(np.asarray(w_out)[l][:, i * 512:i * 512 + 512])
        else:
            dst[:, :KT * 512] = pack(np.concatenate([np.asarray(w_sh_gate)[l], np.asarray(w_sh_up)[l]], 1))
            dst[:, KT * 512:] = pack(np.asarray(w_sh_down)[l])
    d["wseq"] = wseq
    wexp = np.empty((L, NE, P, SLOT), f)
    gu = wexp[..., :KT * 512].reshape(L, NE, P, KT, 2, DE)
    gu[..., 0, :] = np.asarray(w_exp_gate).reshape(L, NE, KT, P, DE).transpose(0, 1, 3, 2, 4)
    gu[..., 1, :] = np.asarray(w_exp_up).reshape(L, NE, KT, P, DE).transpose(0, 1, 3, 2, 4)
    wexp[..., KT * 512:].reshape(L, NE, P, 2, D)[:] = np.asarray(w_exp_down).reshape(L, NE, 2, P, D).transpose(0, 1, 3, 2, 4)
    d["wexp"] = wexp
    d["wr"] = np.stack([pack(np.asarray(w_router)[l]) for l in range(L)])
    row = np.concatenate([np.asarray(b_router), np.asarray(sink), np.asarray(g_diff), np.asarray(g_mlstm),
                          np.asarray(b_gate).reshape(L, 16), np.asarray(lam_q1), np.asarray(lam_k1),
                          np.asarray(lam_q2), np.asarray(lam_k2)], 1)
    d["rowp"] = np.ascontiguousarray(np.broadcast_to(row[:, None, :], (L, P, NROW)))
    d["colp"] = np.ascontiguousarray(np.concatenate(
        [np.asarray(g_mix).reshape(L, KT, P), np.asarray(g_ffn).reshape(L, KT, P)],
        1).transpose(0, 2, 1))
    d["bmod"] = np.ascontiguousarray(np.repeat(np.asarray(b_mod).reshape(L, NMOD, 1, 512), 2, axis=2))
    d["gfinal"] = np.ascontiguousarray(np.broadcast_to(np.asarray(g_final)[None], (P, D)))

    nc = bacc.Bacc("TRN2", target_bir_lowering=False, num_devices=1)
    a = {n: nc.dram_tensor("in_" + n, v.shape, mybir.dt.from_np(v.dtype), kind="ExternalInput").ap() for n, v in d.items()}
    a["out"] = nc.dram_tensor("out_0", (NLAT, D), F32, kind="ExternalOutput").ap()
    a["mod_rows"] = nc.dram_tensor("mod_rows", (L, 2, 6 * D), F32, kind="Internal").ap()
    a["h_rows"] = nc.dram_tensor("h_rows", (NTOK, D), F32, kind="Internal").ap()
    a["y_rows"] = nc.dram_tensor("y_rows", (NE * P, D), F32, kind="Internal").ap()
    build(nc, a)
    res = run(nc, [{"in_" + n: v for n, v in d.items()}], core_ids=[0])
    return res.results[0]["out_0"][None]
```

```python
import math
from contextlib import ExitStack

import concourse.bass as bass
from concourse import mybir

P = 128
D, L = 1024, 2
KT = D // P
NCTX = NLAT = 256
NTOK = NCTX + NLAT
TT = NTOK // P
LAT0 = NCTX // P
HB, DH = 4, 64
EPS = 1e-6
NE, NG, TOPK, DE = 64, 8, 8, 256
PER = NE // NG
ROUTED_SCALE = 2.5
SLOT = KT * 2 * DE + 2 * D
NSLOT = 4
RING = 2
NBLK = NTOK // P
MAXOVER = NTOK * TOPK // P
BIG = 1e30

AQ, BQ, BK, CQ, CK, MISC, BV, CV, CO = range(9)
NMOD = 12
MOD_FIRST = [(0, "mod", c) for c in range(4)]
MOD_BESIDE = [(0, "mod", c) for c in range(4, NMOD)] + [(1, "mod", c) for c in range(NMOD)]


def layer_chunks(l):
    return ([(l, "in", c) for c in range(CO)], [(l, "in", CO)] + [(l, "merge", c) for c in range(6)]
            + [(l, "out", c) for c in range(2)] + [(l, "shared", 0)])


SEQ = (MOD_FIRST + layer_chunks(0)[0] + MOD_BESIDE + layer_chunks(0)[1] + layer_chunks(1)[0] + layer_chunks(1)[1])
PLACE = {c: n for n, c in enumerate(SEQ)}


def chunk_size(chunk):
    kind, c = chunk[1:]
    return {"in": KT * (272 if c == MISC else 512), "merge": KT * 512 + 4 * 512, "shared": SLOT}.get(kind, KT * 512)


FILLS_A, FILLS_B = 8, 8

R_BROUTER, R_SINK, R_GDIFF, R_GMLSTM, R_BGATE, R_LAM = 0, 64, 72, 200, 712, 728
NROW = R_LAM + 4 * DH
C_ID, C_ONES, C_LE, C_GE, C_ROT, C_COS, C_SIN, C_BAND, C_MF, C_MB, C_IOTA = (
    0, 128, 256, 384, 512, 640, 896, 1152, 1152 + 1024, 2304, 2432)
C_TOK, C_PIDX1, C_OVER = 2560, 2564, 2568
NCONST = 2568 + 2 * 192

ALU = mybir.AluOpType
ACT = mybir.ActivationFunctionType
F32 = mybir.dt.float32
F32R = mybir.dt.float32r
FP16 = mybir.dt.float16
I32 = mybir.dt.int32
U32 = mybir.dt.uint32
AX = mybir.AxisListType.X


class Space:
    pass


def build(nc, a):
    ctx = ExitStack()
    with ctx:
        part_sems = []

        def sem(name):
            part_sems.append(nc.alloc_semaphore(name=name))
            return part_sems[-1]

        def kept_sem(name):
            return ctx.enter_context(nc.semaphore(name))

        def sb(stack, name, shape, dt=F32):
            return stack.enter_context(nc.sbuf_tensor(name, shape, dt))

        def sb_both(stack, name, shape):
            at = (nc.sbuf_base + 31) // 32 * 32
            full = sb(stack, name, shape)
            return full, nc.alloc_sbuf_tensor_at(name + "_r", shape, F32R, offset=at)

        V, A, T, G = nc.vector, nc.scalar, nc.tensor, nc.gpsimd
        PS = ctx.enter_context(nc.psum_tensor("banks", [P, 8, 512], F32))
        ring, ring_low = zip(*[sb_both(ctx, f"weights{i}", [P, SLOT]) for i in range(RING)])
        X = sb(ctx, "x_resident", [P, TT, D])
        hT, hTl = sb_both(ctx, "hT", [P, KT, NTOK])
        cst = sb(ctx, "constants", [P, NCONST])
        rowp = sb(ctx, "row_params", [P, NROW])
        colp = sb(ctx, "col_params", [P, L, 2 * KT])
        cc = sb(ctx, "cond_cols", [P, KT, 2])
        sc = sb(ctx, "silu_cond", [P, KT, 2])
        modc = sb(ctx, "mod_cols", [P, L, 6, KT, 2])
        Amix = sb(ctx, "a_mix", [P, KT, 2])
        Affn = sb(ctx, "a_ffn", [P, KT, 2])
        eps_t = sb(ctx, "epsilon", [P, 1])
        eps = eps_t[:]
        ident, ones = cst[:, C_ID:C_ID + P], cst[:, C_ONES:C_ONES + P]
        iota = cst[:, C_IOTA:C_IOTA + P]

        s_dve, s_act = kept_sem("dve_chain"), kept_sem("act_chain")
        ld = [kept_sem(f"slot_loaded{i}") for i in range(NSLOT)]
        loads = [0] * NSLOT
        freed = {}
        issued = [0]
        s_written = kept_sem("out_written")
        s_par = kept_sem("row_params_loaded")
        s_params = kept_sem("col_params_loaded")
        s_x, s_const = kept_sem("x_loaded"), kept_sem("constants_loaded")
        chain = [0, 0]

        def vlink(ins):
            chain[0] += 1
            ins.then_inc(s_dve, 1)
            V.wait_ge(s_dve, chain[0])

        def alink(ins):
            chain[1] += 1
            ins.then_inc(s_act, 1)
            A.wait_ge(s_act, chain[1])

        def bc(ap, *shape):
            return ap.to_broadcast(list(shape))

        def sp_loads(sp, upto):
            while issued[0] < min(upto, len(SEQ)):
                n = issued[0]
                l, kind, c = SEQ[n]
                if n >= RING:
                    if freed[n - RING] is not None:
                        sp.wait_ge(*freed[n - RING])
                size = chunk_size(SEQ[n])
                sp.dma_start(ring[n % RING][:, 0:size], a["wseq"][n, :, 0:size]).then_inc(ld[n % RING], 16)
                loads[n % RING] += 1
                if kind == "mod":
                    sp.dma_start(ring[n % RING][0:2, KT * 512:KT * 512 + 512], a["bmod"][l, c]).then_inc(ld[n % RING], 16)
                    loads[n % RING] += 1
                landed[n] = 16 * loads[n % RING]
                issued[0] += 1
        landed = {}

        def chunk_ready(pe, n):
            pe.wait_ge(ld[n % RING], landed[n])
            return ring[n % RING]

        def end_part():
            with nc.Block() as block:
                @block.sync
                def _(sp):
                    for s in part_sems:
                        sp.sem_clear(s)
            for s in part_sems:
                nc.release_semaphore(s)
            part_sems.clear()
            for n in freed:
                freed[n] = None


        with nc.Block() as block:
            s_c = sem("condition_loaded")

            @block.sync
            def _(sp):
                sp.dma_start(cc[:], a["cond"]).then_inc(s_c, 16)
                sp_loads(sp, RING)
                sp.dma_start(cst[:], a["const"]).then_inc(s_const, 16)
                sp.dma_start(colp[:], a["colp"].rearrange("l p k -> p l k")).then_inc(s_params, 16)
                sp.dma_start(X[:], a["x"].rearrange("(t p) d -> p t d", p=P)).then_inc(s_x, 16)

            @block.vector
            def _(dve):
                V.memset(eps_t[:], EPS)

            @block.scalar
            def _(act):
                act.wait_ge(s_c, 16)
                A.activation(sc[:], cc[:], ACT.Silu)

        e = Space()
        e.V, e.A, e.T, e.G, e.PS = V, A, T, G, PS
        e.ring, e.X, e.hT, e.cst, e.rowp, e.colp = ring, X, hT, cst, rowp, colp
        e.sc, e.modc, e.Amix, e.Affn, e.eps = sc, modc, Amix, Affn, eps
        e.ident, e.ones, e.iota = ident, ones, iota
        e.ld, e.loads, e.freed, e.s_written, e.s_par = ld, loads, freed, s_written, s_par
        e.sem, e.kept_sem, e.sb, e.vlink, e.alink, e.bc = sem, kept_sem, sb, vlink, alink, bc
        e.sp_loads, e.chunk_ready = sp_loads, chunk_ready
        e.s_x, e.s_const = s_x, s_const
        e.ring_low, e.hTl, e.sb_both = ring_low, hTl, sb_both
        e.s_params, e.end_part = s_params, end_part
        for l in range(L):
            layer(nc, a, e, l)
            end_part()
        final_norm(nc, a, e)


def layer(nc, a, e, l):
    need_ctx = l < L - 1
    tiles = list(range(TT)) if need_ctx else list(range(LAT0, TT))
    with ExitStack() as mix:
        e.hTh = e.sb(mix, f"hT_high{l}", [P, KT, NTOK], F32R)
        m = Space()
        m.aqT, m.aqT_r = e.sb_both(mix, f"aqT_{l}", [P, 4, NTOK])
        m.bqT, m.bqT_r = e.sb_both(mix, f"bqT_{l}", [P, 4, NTOK])
        m.cqT, m.cqT_r = e.sb_both(mix, f"cqT_{l}", [P, 4, NTOK])
        m.bkT = e.sb(mix, f"bkT_{l}", [P, 4, NTOK])
        m.ckT = e.sb(mix, f"ckT_{l}", [P, 4, NTOK])
        m.akT = e.sb(mix, f"akT_{l}", [P, 1, NTOK])
        m.misc = e.sb(mix, f"misc_{l}", [P, TT, 144])
        m.ck, m.ck_r = e.sb_both(mix, f"ck_{l}", [P, TT, 512])
        m.bv, m.bv_r = e.sb_both(mix, f"bv_{l}", [P, TT, 512])
        m.cv, m.cv_r = e.sb_both(mix, f"cv_{l}", [P, TT, 4, P + 1])
        if l == 0:
            e.fill = ModFill(nc, a, e)
            mod_stage(nc, a, e)
        norm_stage(nc, a, e, l, "mix", range(TT), e.Amix, 0)
        proj_stage(nc, a, e, m, l, tiles)
        attn_a_stage(nc, a, e, m, l, tiles)
        attn_b_stage(nc, a, e, m, l, tiles)
        mlstm_stage(nc, a, e, m, l, tiles)
        merge_stage(nc, a, e, m, l, tiles)
    e.end_part()
    norm_stage(nc, a, e, l, "ffn", tiles, e.Affn, 3)
    moe(nc, a, e, l, tiles)


def products(T, out, lhs, rhs, start, stop, weights_left=False):
    (lh, ll), (rh, rl) = lhs, rhs
    T.matmul(out, lh, rh, start=start, stop=False)
    second, third = ((lh, rl), (ll, rh)) if weights_left else ((ll, rh), (lh, rl))
    return T.matmul(out, *second, start=False, stop=False), T.matmul(out, *third, start=False, stop=stop)


class Split:

    def __init__(self, e, st, tag, chunks, blocks):
        self.e, self.chunks, self.blocks = e, chunks, blocks
        self.high = e.sb(st, f"weights_high_{tag}", [P, blocks, 512], F32R)
        self.s_high, self.s_split, self.s_used = (e.sem(f"{n}_{tag}") for n in (
            "weights_high_ready", "weights_split", "weights_block_used"))

    def round_high(self, act, c):
        n, blocks = self.chunks[c]
        w = self.e.chunk_ready(act, n)
        for b, (at, width) in enumerate(blocks):
            if c:
                act.wait_ge(self.s_used, (c - 1) * self.blocks + b + 1)
            self.e.A.activation(self.high[:, b, 0:width], w[:, at:at + width], ACT.Copy).then_inc(self.s_high, 1)

    def leave_low(self, dve, c):
        n, blocks = self.chunks[c]
        w = self.e.ring[n % RING]
        for b, (at, width) in enumerate(blocks):
            dve.wait_ge(self.s_high, c * self.blocks + b + 1)
            self.e.V.tensor_tensor(self.e.ring_low[n % RING][:, at:at + width], w[:, at:at + width],
                                   self.high[:, b, 0:width].bitcast(F32), ALU.subtract).then_inc(self.s_split, 1)

    def block(self, c, b, lo, hi):
        n, blocks = self.chunks[c]
        at = blocks[b][0]
        return self.high[:, b, lo:hi], self.e.ring_low[n % RING][:, at + lo:at + hi]

    def wait(self, pe, c, b):
        pe.wait_ge(self.s_split, c * self.blocks + b + 1)


class ModFill:

    def __init__(self, nc, a, e):
        self.nc, self.a, self.e = nc, a, e
        self.jobs = MOD_FIRST + MOD_BESIDE
        self.s_mm, self.s_rows, self.s_tr, self.s_cols = (e.sem(n) for n in (
            "mod_rows_done", "mod_rows_ready", "mod_transposed", "mod_cols_ready"))
        self.s_out = [e.sem(f"mod_rows_written{i}") for i in range(2)]
        self.at = {"mm": 0, "rows": 0, "tr": 0, "cols": 0, "store": 0}
        for i, c in enumerate(self.jobs):
            e.freed[PLACE[c]] = (self.s_rows, i + 1)

    def rows(self, i):
        return self.e.ring[PLACE[self.jobs[i]] % RING][0:2, KT * 512 + 512:KT * 512 + 1024]

    def products(self, pe, bank, lo=0, hi=KT):
        e, i = self.e, self.at["mm"]
        w = e.chunk_ready(pe, PLACE[self.jobs[i]])
        for k in range(lo, hi):
            last = e.T.matmul(e.PS[0:2, bank, :], e.sc[:, k, :], w[:, k * 512:k * 512 + 512], start=k == 0, stop=k == KT - 1)
        if hi == KT:
            last.then_inc(self.s_mm, 1)
            self.at["mm"] += 1

    def add_bias(self, dve, bank):
        e, i = self.e, self.at["rows"]
        dve.wait_ge(self.s_mm, i + 1)
        n = PLACE[self.jobs[i]]
        w = e.chunk_ready(dve, n)
        if i >= 2:
            dve.wait_ge(self.s_out[i % 2], 16 * (i // 2))
            dve.wait_ge(self.s_tr, i - 1)
        e.V.tensor_tensor(self.rows(i), e.PS[0:2, bank, :], w[0:2, KT * 512:KT * 512 + 512], ALU.add).then_inc(self.s_rows, 1)
        self.at["rows"] += 1

    def transpose(self, pe, bank):
        e, i = self.e, self.at["tr"]
        pe.wait_ge(self.s_rows, i + 1)
        for j in range(4):
            last = e.T.matmul(e.PS[:, bank, 2 * j:2 * j + 2], self.rows(i)[:, j * P:j * P + P], e.cst[0:2, C_ID:C_ID + 2],
                              start=True, stop=True)
        last.then_inc(self.s_tr, 1)
        self.at["tr"] += 1

    def store_cols(self, eng, bank, on_act=False):
        e, i = self.e, self.at["cols"]
        l, _, c = self.jobs[i]
        dst = e.modc[:, l, c // 2, 4 * (c % 2):4 * (c % 2) + 4]
        src = e.PS[:, bank, 0:8].rearrange("p (k v) -> p k v", v=2)
        eng.wait_ge(self.s_tr, i + 1)
        if on_act:
            e.A.activation(dst, src, ACT.Copy).then_inc(self.s_cols, 1)
        else:
            e.V.tensor_copy(dst, src).then_inc(self.s_cols, 1)
        self.at["cols"] += 1

    def wait_cols(self, pe):
        pe.wait_ge(self.s_cols, self.at["tr"])

    def write_rows(self, sp, n):
        for _ in range(n):
            i = self.at["store"]
            l, _, c = self.jobs[i]
            sp.wait_ge(self.s_rows, i + 1)
            sp.dma_start(self.a["mod_rows"][l, :, c * 512:c * 512 + 512], self.rows(i)).then_inc(self.s_out[i % 2], 16)
            self.at["store"] += 1
        if self.at["store"] == len(self.jobs):
            for i in range(2):
                sp.wait_ge(self.s_out[i], 16 * (len(self.jobs) // 2))


def mod_stage(nc, a, e):
    n = len(MOD_FIRST)
    with nc.Block() as block:
        @block.sync
        def _(sp):
            for i in range(n):
                e.sp_loads(sp, i + 1 + RING)
                e.fill.write_rows(sp, 1)
            e.sp_loads(sp, n + RING)

        @block.tensor
        def _(pe):
            for i in range(n):
                e.fill.products(pe, i)
                if i == 1:
                    pe.wait_ge(e.s_const, 16)
                if i:
                    e.fill.transpose(pe, 4 + (i - 1))
            e.fill.transpose(pe, 4 + n - 1)

        @block.vector
        def _(dve):
            for i in range(n):
                e.fill.add_bias(dve, i)
                if i:
                    e.fill.store_cols(dve, 4 + i - 1)
            e.fill.store_cols(dve, 4 + n - 1)


def norm_stage(nc, a, e, l, tag, tiles, scale, shift):
    V, A, T, PS, sem = e.V, e.A, e.T, e.PS, e.sem
    tiles = list(tiles)
    t0 = tiles[0]
    with ExitStack() as st, nc.Block() as block:
        squares = e.sb(st, f"squares_{tag}{l}", [P, 2, D])
        ms = e.sb(st, f"ms_{tag}{l}", [P, TT])
        dg = e.sb(st, f"inv_rms_diag_{tag}{l}", [P, TT, P])
        s_dg, s_tp = sem(f"inv_rms_diag_ready_{tag}{l}"), sem(f"transposed_{tag}{l}")
        s_hi = sem(f"h_high_ready_{tag}{l}")
        s_va, s_vb = sem(f"evac_dve_{tag}{l}"), sem(f"evac_act_{tag}{l}")
        s_ms, s_rs, s_sc = sem(f"mean_square_{tag}{l}"), sem(f"inv_rms_{tag}{l}"), sem(f"scale_ready_{tag}{l}")

        def evac(i, t, ks, on_dve, done):
            v = 0 if t < LAT0 else 1
            for k in ks:
                src = PS[:, 2 * i + k // 4, (k % 4) * P:(k % 4) * P + P]
                dst = e.hT[:, k, t * P:t * P + P]
                sc_, sh_ = scale[:, k, v:v + 1], e.modc[:, l, shift, k, v:v + 1]
                if on_dve:
                    last = V.tensor_scalar(dst, src, sc_, sh_, ALU.mult, ALU.add)
                else:
                    last = A.activation(dst, src, ACT.Identity, bias=sh_, scale=sc_)
            last.then_inc(done, 1)

        def low(dve, i):
            dve.wait_ge(s_hi, i + 1)
            cols = slice(tiles[i] * P, tiles[i] * P + P)
            V.tensor_tensor(e.hTl[:, :, cols], e.hT[:, :, cols], e.hTh[:, :, cols].bitcast(F32), ALU.subtract)

        if tag == "mix":
            @block.sync
            def _(sp):
                if l:
                    e.sp_loads(sp, PLACE[l, "in", 0] + RING)
                sp.dma_start(e.rowp[:], a["rowp"][l]).then_inc(e.s_par, 16)
                sp.wait_ge(e.s_par, 16 * (l + 1))

        @block.vector
        def _(dve):
            if l == 0:
                dve.wait_ge(e.s_params, 16)
                dve.wait_ge(e.s_x, 16)
            g = e.colp[:, l, 0:KT] if tag == "mix" else e.colp[:, l, KT:2 * KT]
            V.scalar_tensor_tensor(scale[:], e.modc[:, l, shift + 1], 1.0, e.bc(g.unsqueeze(2), P, KT, 2),
                                   ALU.add, ALU.mult).then_inc(s_sc, 1)
            dve.wait_ge(s_sc, 1)
            for i, t in enumerate(tiles[::2]):
                V.tensor_tensor_reduce(out=squares[:, 0], in0=e.X[:, t], in1=e.X[:, t], scale=1.0, scalar=0.0,
                                       op0=ALU.mult, op1=ALU.add, accum_out=ms[:, t:t + 1]).then_inc(s_ms, 1)
                dve.wait_ge(s_ms, i + 1)
            dve.wait_ge(s_rs, 1)
            e.vlink(V.reciprocal(ms[:, t0:TT], ms[:, t0:TT]))
            nt = len(tiles)
            V.tensor_tensor(dg[:, 0:nt], e.bc(e.ident.unsqueeze(1), P, nt, P), e.bc(ms[:, t0:TT].unsqueeze(2), P, nt, P),
                            ALU.mult).then_inc(s_dg, 1)
            for i, t in enumerate(tiles):
                dve.wait_ge(s_tp, i + 1)
                evac(i, t, range(0, 4), True, s_va)
                if tag == "mix" and i:
                    low(dve, i - 1)
            if tag == "mix":
                low(dve, len(tiles) - 1)

        @block.tensor
        def _(pe):
            pe.wait_ge(s_dg, 1)
            for i, t in enumerate(tiles):
                for k in range(KT):
                    last = T.matmul(PS[:, 2 * i + k // 4, (k % 4) * P:(k % 4) * P + P],
                                    e.X[:, t, k * P:k * P + P], dg[:, i], start=True, stop=True)
                last.then_inc(s_tp, 1)

        @block.scalar
        def _(act):
            act.wait_ge(s_sc, 1)
            for i, t in enumerate(tiles[1::2]):
                e.alink(A.activation(squares[:, 1], e.X[:, t], ACT.Square, accum_out=ms[:, t:t + 1]))
            act.wait_ge(s_ms, len(tiles[::2]))
            A.activation(ms[:, t0:TT], ms[:, t0:TT], ACT.Sqrt, bias=e.eps, scale=1.0 / D).then_inc(s_rs, 1)
            for i, t in enumerate(tiles):
                act.wait_ge(s_tp, i + 1)
                evac(i, t, range(4, KT), False, s_vb)
                if tag == "mix":
                    act.wait_ge(s_va, i + 1)
                    act.wait_ge(s_vb, i + 1)
                    A.activation(e.hTh[:, :, t * P:t * P + P], e.hT[:, :, t * P:t * P + P], ACT.Copy).then_inc(s_hi, 1)


def proj_stage(nc, a, e, m, l, tiles):
    V, A, T, PS, sem = e.V, e.A, e.T, e.PS, e.sem
    q0 = tiles[0] * P
    kscale = float(P) ** -0.5
    units = []
    for c, dst, rope, lo, sc in ((AQ, m.aqT, 1, q0, 1.0), (BQ, m.bqT, 1, q0, 1.0), (BK, m.bkT, 1, 0, 1.0),
                                 (CQ, m.cqT, 0, q0, 1.0), (CK, m.ckT, 0, 0, kscale)):
        for j in range(4):
            units.append(("T", c, 512, j * P, P, dst[:, j, :], rope, lo, sc))
        if c == CK:
            for t in range(TT):
                units.append(("tok", c, 512, 0, 512, m.ck[:, t], 0, t, kscale))
    units.append(("T", MISC, 272, 0, P, m.akT[:, 0], 1, 0, 1.0))
    for t in range(TT):
        units.append(("tok", MISC, 272, P, 144, m.misc[:, t], 0, t, 1.0))
    for t in range(TT):
        units.append(("tok", BV, 512, 0, 512, m.bv[:, t], 0, t, 1.0))
    for t in range(TT):
        units.append(("tok", CV, 512, 0, 512, m.cv[:, t, :, 0:P], 0, t, 1.0))
    ropes = [u for u, x in enumerate(units) if x[6]]

    with ExitStack() as st, nc.Block() as block:
        tmp = e.sb(st, f"rope_tmp{l}", [P, 2, NLAT])
        s_mm, s_ev = sem(f"proj_done{l}"), sem(f"proj_evacuated{l}")
        s_rot, s_rope = sem(f"rotated{l}"), sem(f"roped{l}")
        order = []
        for u, x in enumerate(units):
            e.freed[PLACE[l, "in", x[1]]] = (s_mm, u + 1)
            if x[1] not in order:
                order.append(x[1])
        first = [u for u, x in enumerate(units) if not u or units[u - 1][1] != x[1]]
        last_of = [u - 1 for u in first[1:]] + [len(units) - 1]
        split = Split(e, st, f"in{l}", [(PLACE[l, "in", c], [(k * units[u][2], units[u][2]) for k in range(KT)])
                                        for c, u in zip(order, first)], KT)

        @block.sync
        def _(sp):
            e.sp_loads(sp, PLACE[l, "in", CV] + 1 + RING)

        @block.tensor
        def _(pe):
            def rotate(u):
                r = ropes.index(u)
                pe.wait_ge(s_ev, u + 1)
                if r >= 2:
                    pe.wait_ge(s_rope, r - 1)
                T.matmul(PS[:, 4 + r % 2, 0:NLAT], e.cst[:, C_ROT:C_ROT + P], units[u][5][:, NCTX:NTOK],
                         start=True, stop=True).then_inc(s_rot, 1)

            for u, (kind, c, width, col, n, dst, rope, lo, sc) in enumerate(units):
                ci = order.index(c)
                if u >= 4:
                    pe.wait_ge(s_ev, u - 3)
                for k in range(KT):
                    if u in first:
                        split.wait(pe, ci, k)
                    wk = split.block(ci, k, col, col + n)
                    if kind == "T":
                        toks = slice(lo, NTOK)
                        used, last = products(T, PS[:, u % 4, toks], wk, (e.hTh[:, k, toks], e.hTl[:, k, toks]),
                                              k == 0, k == KT - 1, weights_left=True)
                    else:
                        toks = slice(lo * P, lo * P + P)
                        used, last = products(T, PS[:, u % 4, 0:n], (e.hTh[:, k, toks], e.hTl[:, k, toks]), wk,
                                              k == 0, k == KT - 1)
                    if u in last_of:
                        used.then_inc(split.s_used, 1)
                last.then_inc(s_mm, 1)
                if u >= 1 and units[u - 1][6]:
                    rotate(u - 1)

        @block.scalar
        def _(act):
            split.round_high(act, 0)
            for u, (kind, c, width, col, n, dst, rope, lo, sc) in enumerate(units):
                if u in last_of[:-1]:
                    split.round_high(act, last_of.index(u) + 1)
                act.wait_ge(s_mm, u + 1)
                if kind == "T":
                    A.activation(dst[:, lo:NTOK], PS[:, u % 4, lo:NTOK], ACT.Copy, scale=sc).then_inc(s_ev, 1)
                else:
                    src = PS[:, u % 4, 0:n]
                    if c == CV:
                        src = src.rearrange("p (h d) -> p h d", h=4)
                    A.activation(dst, src, ACT.Copy, scale=sc).then_inc(s_ev, 1)

        @block.vector
        def _(dve):
            V.memset(m.cv[:, :, :, P:P + 1], 1.0)
            split.leave_low(dve, 0)
            done = 1

            def rope(r, u):
                lat = units[u][5][:, NCTX:NTOK]
                dve.wait_ge(s_rot, r + 1)
                V.tensor_tensor(tmp[:, r % 2], PS[:, 4 + r % 2, 0:NLAT], e.cst[:, C_SIN:C_SIN + NLAT], ALU.mult)
                e.vlink(V.tensor_tensor(lat, lat, e.cst[:, C_COS:C_COS + NLAT], ALU.mult))
                V.tensor_tensor(lat, lat, tmp[:, r % 2], ALU.add).then_inc(s_rope, 1)

            for r, u in enumerate(ropes):
                while done < len(order) and last_of[done - 1] <= u + 1:
                    split.leave_low(dve, done)
                    done += 1
                rope(r, u)
            while done < len(order):
                split.leave_low(dve, done)
                done += 1


def attn_a_stage(nc, a, e, m, l, tiles):
    V, A, T, PS, sem = e.V, e.A, e.T, e.PS, e.sem
    units = [(t, g) for t in tiles for g in range(2)]
    fills = FILLS_A if l == 0 else 0
    with ExitStack() as st, nc.Block() as block:
        SS = e.sb(st, f"a_probs{l}", [P, 2, 4, NTOK])
        PT = e.sb(st, f"a_probsT{l}", [P, 4, 4, P])
        O = e.sb(st, f"a_out{l}", [P, 8, DH])
        stats = e.sb(st, f"a_stats{l}", [P, 2, 6, 4])
        s_sc, s_cp, s_m, s_ex, s_tr, s_pt, s_pv, s_o, s_ot, s_oev = (sem(f"{n}{l}") for n in (
            "a_scores", "a_scores_stored", "a_max", "a_exp", "a_transposed", "a_probsT_ready", "a_pv", "a_out_ready",
            "a_outT", "a_outT_stored"))
        MAX, NEGMAX, SINKED, SUM, INV, ESINK = range(6)

        def nk(t):
            return NTOK if t >= LAT0 else NCTX

        @block.sync
        def _(sp):
            for u in range(fills):
                e.fill.write_rows(sp, 1)
                e.sp_loads(sp, PLACE[MOD_BESIDE[0]] + u + 1 + RING)

        @block.tensor
        def _(pe):
            def scores(u):
                t, g = units[u]
                if u >= 1:
                    pe.wait_ge(s_cp, u)
                for h in range(4):
                    last = T.matmul(PS[:, h, 0:nk(t)], m.aqT[g * DH:g * DH + DH, h, t * P:t * P + P],
                                    m.akT[g * DH:g * DH + DH, 0, 0:nk(t)], start=True, stop=True)
                last.then_inc(s_sc, 1)

            scores(0)
            for u, (t, g) in enumerate(units):
                n = nk(t)
                if u + 1 < len(units):
                    scores(u + 1)
                if 1 <= u <= fills:
                    e.fill.transpose(pe, 7)
                pe.wait_ge(s_ex, u + 1)
                if u >= 1:
                    pe.wait_ge(s_o, u)
                if u >= 2:
                    pe.wait_ge(s_oev, u // 2)
                for h in range(4):
                    if h == 3 and 1 <= u <= fills:
                        e.fill.wait_cols(pe)
                    for k in range(n // P):
                        last = T.transpose(PS[:, 4 + h, k * P:k * P + P], SS[:, u % 2, h, k * P:k * P + P], e.ident)
                last.then_inc(s_tr, 1)
                pe.wait_ge(s_pt, 2 * u + 2)
                for h in range(4):
                    for k in range(n // P):
                        last = T.matmul(PS[:, 4, h * DH:h * DH + DH], PT[:, h, k, :],
                                        m.misc[:, k, g * DH:g * DH + DH], start=k == 0, stop=k == n // P - 1)
                last.then_inc(s_pv, 1)
                if u < fills:
                    e.fill.products(pe, 7)
                if g == 1:
                    i = u // 2
                    pe.wait_ge(s_o, u + 1)
                    for j in range(4):
                        last = T.transpose(PS[:, 5, j * P:j * P + P],
                                           O[:].rearrange("p h d -> p (h d)")[:, j * P:j * P + P], e.ident)
                    last.then_inc(s_ot, 1)
            if fills == len(units):
                e.fill.transpose(pe, 7)

        @block.vector
        def _(dve):
            def scaled(u):
                t, g = units[u]
                n = nk(t)
                S = SS[:, u % 2, :, 0:n]
                dve.wait_ge(s_sc, u + 1)
                if t >= LAT0:
                    band = e.cst[:, C_BAND + (t - LAT0) * NTOK:C_BAND + (t - LAT0) * NTOK + n]
                    V.scalar_tensor_tensor(S, PS[:, 0:4, 0:n], DH ** -0.5, e.bc(band.unsqueeze(1), P, 4, n),
                                           ALU.mult, ALU.add).then_inc(s_cp, 1)
                else:
                    V.tensor_scalar(S, PS[:, 0:4, 0:n], DH ** -0.5, None, ALU.mult).then_inc(s_cp, 1)
                dve.wait_ge(s_cp, u + 1)

            def maxima(u):
                t, g = units[u]
                mx = stats[:, u % 2]
                sink = e.rowp[:, R_SINK + 4 * g:R_SINK + 4 * g + 4]
                e.vlink(V.reduce_max(mx[:, MAX], SS[:, u % 2, :, 0:nk(t)], AX))
                e.vlink(V.tensor_tensor(mx[:, MAX], mx[:, MAX], sink, ALU.max))
                e.vlink(V.tensor_scalar(mx[:, NEGMAX], mx[:, MAX], -1.0, None, ALU.mult))
                V.tensor_tensor(mx[:, SINKED], sink, mx[:, MAX], ALU.subtract).then_inc(s_m, 1)

            scaled(0)
            maxima(0)
            for u, (t, g) in enumerate(units):
                n = nk(t)
                mx = stats[:, u % 2]
                if u + 1 < len(units):
                    scaled(u + 1)
                dve.wait_ge(s_ex, u + 1)
                e.vlink(V.tensor_tensor(mx[:, INV], mx[:, SUM], mx[:, ESINK], ALU.add))
                e.vlink(V.reciprocal(mx[:, INV], mx[:, INV]))
                dve.wait_ge(s_tr, u + 1)
                V.tensor_copy(PT[:, 0:2, 0:n // P].rearrange("p h k q -> p h (k q)"),
                              PS[:, 4:6, 0:n]).then_inc(s_pt, 1)
                if u + 1 < len(units):
                    maxima(u + 1)
                dve.wait_ge(s_pv, u + 1)
                V.tensor_tensor(O[:, 4 * g:4 * g + 4], PS[:, 4, 0:4 * DH].rearrange("p (h d) -> p h d", h=4),
                                e.bc(mx[:, INV].unsqueeze(2), P, 4, DH), ALU.mult).then_inc(s_o, 1)
                if g == 1:
                    dve.wait_ge(s_ot, u // 2 + 1)
                    V.tensor_copy(m.aqT[:, :, t * P:t * P + P],
                                  PS[:, 5, :].rearrange("p (j q) -> p j q", j=4)).then_inc(s_oev, 1)
                if u < fills:
                    e.fill.add_bias(dve, 7)

        @block.scalar
        def _(act):
            def exps(u):
                t, g = units[u]
                n = nk(t)
                S, mx = SS[:, u % 2], stats[:, u % 2]
                act.wait_ge(s_m, u + 1)
                for h in range(4):
                    A.activation(S[:, h, 0:n], S[:, h, 0:n], ACT.Exp, bias=mx[:, NEGMAX, h:h + 1],
                                 accum_out=mx[:, SUM, h:h + 1])
                A.activation(mx[:, ESINK], mx[:, SINKED], ACT.Exp).then_inc(s_ex, 1)

            exps(0)
            for u, (t, g) in enumerate(units):
                if 1 <= u <= fills:
                    e.fill.store_cols(act, 7, on_act=True)
                act.wait_ge(s_tr, u + 1)
                A.activation(PT[:, 2:4, 0:nk(t) // P].rearrange("p h k q -> p h (k q)"), PS[:, 6:8, 0:nk(t)],
                             ACT.Copy).then_inc(s_pt, 1)
                if u + 1 < len(units):
                    exps(u + 1)
            if fills == len(units):
                e.fill.store_cols(act, 7, on_act=True)


def attn_b_stage(nc, a, e, m, l, tiles):
    V, A, T, PS, sem = e.V, e.A, e.T, e.PS, e.sem
    lam_init = 0.8 - 0.6 * math.exp(-0.3 * l)
    with ExitStack() as st, nc.Block() as block:
        E = e.sb(st, f"b_probs{l}", [P, 2, 4, NTOK])
        O = e.sb(st, f"b_out{l}", [P, 4, P])
        mx = e.sb(st, f"b_stats{l}", [P, 8, 4])
        lam = e.sb(st, f"lam{l}", [P, 4])
        lt = e.sb(st, f"lam_tmp{l}", [P, 2, DH])
        gd = e.sb(st, f"g_diff_scaled{l}", [P, P])
        s_sc, s_m, s_ex, s_at, s_tr, s_pt, s_pv, s_o, s_ot, s_oev, s_l1, s_l2 = (sem(f"{n}{l}") for n in (
            "b_scores", "b_max", "b_exp", "b_att_ready", "b_transposed", "b_probsT_ready", "b_pv", "b_out_ready",
            "b_outT", "b_outT_stored", "lam_sums", "lam_exps"))
        PT = E[:, 1].rearrange("p h (k q) -> p h k q", k=4)
        fills = FILLS_B if l == 0 else 0

        def filled(u, i):
            return i * len(tiles) + u < fills

        @block.sync
        def _(sp):
            for f in range(fills):
                e.fill.write_rows(sp, 1)
                e.sp_loads(sp, PLACE[MOD_BESIDE[0]] + FILLS_A + f + 1 + RING)
        s_ms, s_rs = sem(f"b_mean_square{l}"), sem(f"b_inv_rms{l}")

        def nk(t):
            return NTOK if t >= LAT0 else NCTX

        @block.tensor
        def _(pe):
            for u, t in enumerate(tiles):
                n = nk(t)
                if u >= 1:
                    pe.wait_ge(s_oev, u)
                for s in range(2):
                    for h in range(4):
                        last = T.matmul(PS[:, 4 * s + h, 0:n], m.bqT[s * DH:s * DH + DH, h, t * P:t * P + P],
                                        m.bkT[s * DH:s * DH + DH, h, 0:n], start=True, stop=True)
                    last.then_inc(s_sc, 1)
                if filled(u, 0):
                    pe.wait_ge(s_ex, 2 * u + 1)
                    e.fill.products(pe, 3)
                pe.wait_ge(s_at, u + 1)
                for h in range(4):
                    for k in range(n // P):
                        last = T.transpose(PS[:, 4 + h, k * P:k * P + P], E[:, 0, h, k * P:k * P + P], e.ident)
                last.then_inc(s_tr, 1)
                if filled(u, 0):
                    e.fill.transpose(pe, 3)
                if filled(u, 1):
                    e.fill.products(pe, 2, 0, 3)
                pe.wait_ge(s_pt, 2 * u + 2)
                for h in range(4):
                    for k in range(n // P):
                        last = T.matmul(PS[:, 0, h * P:h * P + P], PT[:, h, k, :],
                                        m.bv[:, k, h * P:h * P + P], start=k == 0, stop=k == n // P - 1)
                last.then_inc(s_pv, 1)
                if filled(u, 1):
                    e.fill.products(pe, 2, 3, KT)
                pe.wait_ge(s_o, u + 1)
                for j in range(4):
                    last = T.transpose(PS[:, 1, j * P:j * P + P], O[:, j], e.ident)
                last.then_inc(s_ot, 1)
                if filled(u, 1):
                    e.fill.transpose(pe, 2)
                if filled(u, 0):
                    e.fill.wait_cols(pe)

        @block.vector
        def _(dve):
            lr = e.rowp[:, R_LAM:R_LAM + 4 * DH].rearrange("p (a b d) -> p a b d", a=2, b=2)
            e.vlink(V.tensor_tensor(lt[:], lr[:, :, 0], lr[:, :, 1], ALU.mult))
            V.reduce_sum(lam[:, 0:2], lt[:], AX).then_inc(s_l1, 1)
            dve.wait_ge(s_l2, 1)
            e.vlink(V.tensor_tensor(lam[:, 2:3], lam[:, 0:1], lam[:, 1:2], ALU.subtract))
            e.vlink(V.tensor_scalar(lam[:, 2:3], lam[:, 2:3], lam_init, None, ALU.add))
            e.vlink(V.tensor_scalar(gd[:], e.rowp[:, R_GDIFF:R_GDIFF + P], 1.0 - lam_init, None, ALU.mult))
            for u, t in enumerate(tiles):
                n = nk(t)
                for s in range(2):
                    dve.wait_ge(s_sc, 2 * u + s + 1)
                    e.vlink(V.reduce_max(mx[:, s], PS[:, 4 * s:4 * s + 4, 0:n], AX))
                    V.tensor_scalar(mx[:, s], mx[:, s], -DH ** -0.5, None, ALU.mult).then_inc(s_m, 1)
                dve.wait_ge(s_ex, 2 * u + 2)
                e.vlink(V.reciprocal(mx[:, 4:6], mx[:, 2:4]))
                e.vlink(V.tensor_tensor(mx[:, 6], mx[:, 2], mx[:, 5], ALU.mult))
                e.vlink(V.tensor_scalar(mx[:, 6], mx[:, 6], lam[:, 2:3], -1.0, ALU.mult, ALU.mult))
                for h in range(4):
                    last = V.scalar_tensor_tensor(E[:, 0, h, 0:n], E[:, 1, h, 0:n], mx[:, 6, h:h + 1],
                                                  E[:, 0, h, 0:n], ALU.mult, ALU.add)
                last.then_inc(s_at, 1)
                if filled(u, 0):
                    e.fill.add_bias(dve, 3)
                dve.wait_ge(s_tr, u + 1)
                V.tensor_copy(PT[:, 0:2, 0:n // P].rearrange("p h k q -> p h (k q)"), PS[:, 4:6, 0:n]).then_inc(s_pt, 1)
                if filled(u, 0):
                    e.fill.store_cols(dve, 3)
                dve.wait_ge(s_pv, u + 1)
                e.vlink(V.tensor_tensor(O[:], PS[:, 0, :].rearrange("p (h d) -> p h d", h=4),
                                        e.bc(mx[:, 4].unsqueeze(2), P, 4, P), ALU.mult))
                sq = E[:, 0, :, 0:P]
                e.vlink(V.tensor_tensor(sq, O[:], O[:], ALU.mult))
                e.vlink(V.reduce_sum(mx[:, 7], sq, AX))
                V.tensor_scalar(mx[:, 7], mx[:, 7], 1.0 / P, None, ALU.mult).then_inc(s_ms, 1)
                dve.wait_ge(s_rs, u + 1)
                e.vlink(V.reciprocal(mx[:, 7], mx[:, 7]))
                e.vlink(V.tensor_tensor(O[:], O[:], e.bc(mx[:, 7].unsqueeze(2), P, 4, P), ALU.mult))
                V.tensor_tensor(O[:], O[:], e.bc(gd[:].unsqueeze(1), P, 4, P), ALU.mult).then_inc(s_o, 1)
                if filled(u, 1):
                    e.fill.add_bias(dve, 2)
                dve.wait_ge(s_ot, u + 1)
                V.tensor_copy(m.bqT[:, :, t * P:t * P + P],
                              PS[:, 1, :].rearrange("p (j q) -> p j q", j=4)).then_inc(s_oev, 1)
                if filled(u, 1):
                    e.fill.store_cols(dve, 2)

        @block.scalar
        def _(act):
            act.wait_ge(s_l1, 1)
            A.activation(lam[:, 0:2], lam[:, 0:2], ACT.Exp).then_inc(s_l2, 1)
            for u, t in enumerate(tiles):
                n = nk(t)
                if u >= 1:
                    act.wait_ge(s_o, u)
                for s in range(2):
                    act.wait_ge(s_m, 2 * u + s + 1)
                    for h in range(4):
                        last = A.activation(E[:, s, h, 0:n], PS[:, 4 * s + h, 0:n], ACT.Exp, bias=mx[:, s, h:h + 1],
                                            scale=DH ** -0.5, accum_out=mx[:, 2 + s, h:h + 1])
                    last.then_inc(s_ex, 1)
                act.wait_ge(s_tr, u + 1)
                A.activation(PT[:, 2:4, 0:n // P].rearrange("p h k q -> p h (k q)"), PS[:, 6:8, 0:n],
                             ACT.Copy).then_inc(s_pt, 1)
                act.wait_ge(s_ms, u + 1)
                A.activation(mx[:, 7], mx[:, 7], ACT.Sqrt, bias=e.eps).then_inc(s_rs, 1)


def mlstm_stage(nc, a, e, m, l, tiles):
    V, A, T, PS, sem = e.V, e.A, e.T, e.PS, e.sem
    steps = [(d, t) for pair in zip((0, 1, 2, 3), (1, 0, 3, 2)) for d, t in enumerate(pair)]
    outs = [u for u, (d, t) in enumerate(steps) if t in tiles]
    NSTEP, LASTS = len(steps), len(steps) - 2
    H = m.bkT[:]
    Q = P + 1
    fills = len(MOD_BESIDE) - FILLS_A - FILLS_B if l == 0 else 0
    with ExitStack() as st, nc.Block() as block:
        gates = e.sb(st, f"gates{l}", [P, TT, 4, 4])
        logf = e.sb(st, f"logf{l}", [P, TT, 2, 4])
        neg = e.sb(st, f"min_f{l}", [P, TT, 2, 4])
        CC = e.sb(st, f"c_state{l}", [P, 2, 4, Q])
        DG = e.sb(st, f"diag{l}", [P, 2, 4, P])
        DM = e.sb(st, f"decay{l}", [P, 2, 4, P])
        PTT = e.sb(st, f"c_probsT{l}", [P, 2, 4, P])
        WK = e.sb(st, f"wk{l}", [P, 2, 4, P])
        NUM = e.sb(st, f"num{l}", [P, 2, 4, Q])
        Z = e.sb(st, f"c_stats{l}", [P, 2, 15, 4])
        (s_f1, s_f2, s_cum, s_r, s_rbc, s_mx, s_ex, s_sc, s_p, s_tr, s_pt, s_nm, s_st, s_wk, s_ds, s_nd) = (
            sem(f"{n}{l}") for n in (
                "f_in", "f_out", "c_cum", "c_r", "c_rbc", "c_maxes", "c_exps", "c_scores", "c_probs", "c_transposed",
                "c_probsT_ready", "c_nums", "c_state_done", "c_wk", "c_dstate", "c_num_done"))
        BCUM, BLAST, RR, MAXR, MAXD, MST, UU, WW, AIN, DECAY, WKE, EXM, DEN, TMP = range(14)

        def heads(ap):
            return ap.rearrange("p (h d) -> p h d", h=4)

        def num_bank(b, h):
            return PS[:, b + h // 2, (h % 2) * Q:(h % 2) * Q + Q]

        def num_pair(b, i):
            return PS[:, b + i, 0:2 * Q].rearrange("p (h q) -> p h q", h=2)

        def banks(u):
            return 4 * (u % 2), 4 * (u % 2) + 1, 4 * (u % 2) + 2, 4 * (u % 2) + 3

        @block.sync
        def _(sp):
            for f in range(fills):
                e.fill.write_rows(sp, 1)
                e.sp_loads(sp, min(PLACE[MOD_BESIDE[0]] + FILLS_A + FILLS_B + f + 1 + RING, PLACE[0, "in", CO] + 1))

        @block.tensor
        def _(pe):
            def start(u):
                d, t = steps[u]
                b0, b1, b2, b3 = banks(u)
                tri = e.cst[:, (C_LE if d == 0 else C_GE):(C_LE if d == 0 else C_GE) + P]
                if u >= 2:
                    pe.wait_ge(s_st, u - 1)
                T.matmul(PS[:, b2, 0:4], tri, logf[:, t, d], start=True, stop=True)
                T.matmul(PS[:, b2, 4:8], e.ones, logf[:, t, d], start=True, stop=True).then_inc(s_cum, 1)
                if u in outs:
                    for h in range(4):
                        last = T.matmul(PS[:, b1, h * P:h * P + P], m.cqT[:, h, t * P:t * P + P],
                                        m.ckT[:, h, t * P:t * P + P], start=True, stop=True)
                    last.then_inc(s_sc, 1)

            def rest(u):
                d, t = steps[u]
                b0, b1, b2, b3 = banks(u)
                if u in outs:
                    o = outs.index(u)
                    pe.wait_ge(s_p, o + 1)
                    for h in range(4):
                        last = T.transpose(PS[:, b0, h * P:h * P + P], DM[:, d, h], e.ident)
                    last.then_inc(s_tr, 1)
                    if u < fills:
                        e.fill.transpose(pe, b3)
                        e.fill.wait_cols(pe)
                    pe.wait_ge(s_pt, o + 1)
                    for h in range(4):
                        T.matmul(num_bank(b2, h), PTT[:, d, h], m.cv[:, t, h], start=True, stop=True)
                    for h in range(4):
                        last = T.matmul(num_bank(b0, h), m.cqT[:, h, t * P:t * P + P], CC[:, d, h], start=True, stop=True)
                    last.then_inc(s_nm, 1)
                if u >= LASTS:
                    return
                if u + 1 < fills:
                    e.fill.products(pe, banks(u + 1)[3], 0, 4)
                if u in outs:
                    pe.wait_ge(s_nd, o + 1)
                pe.wait_ge(s_wk, u + 1)
                for h in range(4):
                    last = T.matmul(num_bank(b2, h), WK[:, d, h], m.cv[:, t, h], start=True, stop=True)
                last.then_inc(s_ds, 1)

            pe.wait_ge(s_f2, 2)
            for u in range(NSTEP):
                start(u)
                if u == 0 and fills:
                    e.fill.products(pe, banks(0)[3])
                if 2 <= u <= fills:
                    e.fill.products(pe, banks(u - 1)[3], 4, KT)
                pe.wait_ge(s_r, u + 1)
                T.matmul(PS[:, banks(u)[0], :], e.ones, DG[:, u % 2].rearrange("p h s -> p (h s)"), start=True, stop=True
                         ).then_inc(s_rbc, 1)
                if u >= 1:
                    rest(u - 1)
            rest(NSTEP - 1)

        @block.vector
        def _(dve):
            bg = e.rowp[:, R_BGATE:R_BGATE + 16]
            e.vlink(V.tensor_tensor(gates[:].rearrange("p t g h -> p t (g h)"), m.misc[:, :, P:P + 16],
                                    e.bc(bg.unsqueeze(1), P, TT, 16), ALU.add))
            f = gates[:].rearrange("p t (d i) h -> p t d i h", i=2)[:, :, :, 1]
            e.vlink(V.tensor_scalar(logf[:], f, -1.0, None, ALU.mult))
            V.tensor_tensor(logf[:], logf[:], f, ALU.min).then_inc(s_f1, 1)
            e.vlink(V.tensor_scalar(neg[:], f, 0.0, None, ALU.min))
            dve.wait_ge(s_f2, 1)
            e.vlink(V.tensor_tensor(logf[:], neg[:], logf[:], ALU.subtract))
            V.memset(Z[:], 0.0)
            e.vlink(V.memset(CC[:], 0.0))
            dve.sem_inc(s_f2, 1)

            def begin(u):
                d, t = steps[u]
                z = Z[:, d]
                dve.wait_ge(s_cum, u + 1)
                e.vlink(V.tensor_copy(z[:, BCUM:BCUM + 2].rearrange("p a h -> p (a h)"), PS[:, banks(u)[2], 0:8]))
                e.vlink(V.tensor_tensor(z[:, RR], gates[:, t, 2 * d], z[:, BCUM], ALU.subtract))
                if u >= 2:
                    dve.wait_ge(s_rbc, u - 1)
                V.tensor_tensor(DG[:, d], e.bc(e.ident.unsqueeze(1), P, 4, P), e.bc(z[:, RR].unsqueeze(2), P, 4, P),
                                ALU.mult).then_inc(s_r, 1)

            def maxima(u):
                d, t = steps[u]
                z, dm = Z[:, d], DM[:, d]
                dve.wait_ge(s_rbc, u + 1)
                rb = heads(PS[:, banks(u)[0], :])
                e.vlink(V.reduce_max(z[:, MAXR], rb, AX))
                e.vlink(V.tensor_tensor(z[:, WW], z[:, MST], z[:, MAXR], ALU.max))
                if u in outs:
                    mask = e.cst[:, (C_MF if d == 0 else C_MB):(C_MF if d == 0 else C_MB) + P]
                    e.vlink(V.tensor_tensor(dm, rb, e.bc(mask.unsqueeze(1), P, 4, P), ALU.add))
                    e.vlink(V.reduce_max(z[:, MAXD], dm, AX))
                    e.vlink(V.tensor_tensor(z[:, UU], z[:, MST], z[:, MAXD], ALU.max))
                    V.tensor_tensor(dm, dm, e.bc(z[:, UU].unsqueeze(2), P, 4, P), ALU.subtract)
                    V.tensor_tensor(z[:, AIN], z[:, MST], z[:, UU], ALU.subtract)
                    e.vlink(V.tensor_tensor(z[:, TMP], z[:, BCUM], z[:, UU], ALU.add))
                    V.tensor_scalar(z[:, EXM], z[:, TMP], -1.0, None, ALU.mult)
                V.tensor_tensor(z[:, DECAY], z[:, MST], z[:, WW], ALU.subtract)
                V.tensor_tensor(z[:, WKE], z[:, RR], z[:, WW], ALU.subtract).then_inc(s_mx, 1)

            def probabilities(u):
                d, t = steps[u]
                z, dm = Z[:, d], DM[:, d]
                dve.wait_ge(s_ex, u + 1)
                if u in outs:
                    dve.wait_ge(s_sc, outs.index(u) + 1)
                    V.tensor_tensor(dm, heads(PS[:, banks(u)[1], :]), dm, ALU.mult).then_inc(s_p, 1)
                if u < LASTS:
                    e.vlink(V.tensor_tensor(z[:, MST], z[:, BLAST], z[:, WW], ALU.add))
                    V.tensor_tensor(WK[:, d], heads(m.ck[:, t]), e.bc(z[:, WKE].unsqueeze(2), P, 4, P), ALU.mult
                                    ).then_inc(s_wk, 1)
                if u < fills:
                    e.fill.add_bias(dve, banks(u)[3])

            def output(u):
                d, t = steps[u]
                z, num = Z[:, d], NUM[:, d]
                b0, b1, b2, b3 = banks(u)
                o = outs.index(u)
                if u < fills:
                    e.fill.store_cols(dve, b3)
                dve.wait_ge(s_nm, o + 1)
                for i in range(2):
                    e.vlink(V.tensor_tensor(num[:, 2 * i:2 * i + 2], num_pair(b0, i),
                                            e.bc(z[:, AIN, 2 * i:2 * i + 2].unsqueeze(2), P, 2, Q), ALU.mult))
                    last = V.tensor_tensor(num[:, 2 * i:2 * i + 2], num[:, 2 * i:2 * i + 2], num_pair(b2, i), ALU.add)
                last.then_inc(s_nd, 1)
                dve.wait_ge(s_nd, o + 1)
                den = num[:, :, P]
                e.vlink(V.tensor_scalar(z[:, TMP], den, -1.0, None, ALU.mult))
                e.vlink(V.tensor_tensor(z[:, TMP], z[:, TMP], den, ALU.max))
                e.vlink(V.tensor_tensor(z[:, TMP], z[:, TMP], z[:, EXM], ALU.max))
                e.vlink(V.reciprocal(z[:, DEN], z[:, TMP]))
                hs = H[:, t, :].rearrange("p (h d) -> p h d", h=4)
                scale = e.bc(z[:, DEN].unsqueeze(2), P, 4, P)
                if t not in [steps[x][1] for x in range(u)]:
                    V.tensor_tensor(hs, num[:, :, 0:P], scale, ALU.mult)
                else:
                    e.vlink(V.tensor_tensor(num[:, :, 0:P], num[:, :, 0:P], scale, ALU.mult))
                    V.tensor_tensor(hs, hs, num[:, :, 0:P], ALU.add)

            def state(u):
                d, t = steps[u]
                C = CC[:, d]
                e.vlink(V.tensor_tensor(C, C, e.bc(Z[:, d, DECAY].unsqueeze(2), P, 4, Q), ALU.mult))
                dve.wait_ge(s_ds, u + 1)
                b2 = banks(u)[2]
                V.tensor_tensor(C[:, 0:2], C[:, 0:2], num_pair(b2, 0), ALU.add)
                V.tensor_tensor(C[:, 2:4], C[:, 2:4], num_pair(b2, 1), ALU.add).then_inc(s_st, 1)
                dve.wait_ge(s_st, u + 1)

            for u in range(NSTEP + 1):
                if u < NSTEP:
                    begin(u)
                if u >= 1:
                    probabilities(u - 1)
                if u < NSTEP:
                    maxima(u)
                if u >= 1:
                    if u - 1 in outs:
                        output(u - 1)
                    if u - 1 < LASTS:
                        state(u - 1)

        @block.scalar
        def _(act):
            act.wait_ge(s_f1, 1)
            e.alink(A.activation(logf[:], logf[:], ACT.Exp))
            A.activation(logf[:], logf[:], ACT.Ln, bias=1.0).then_inc(s_f2, 1)

            def exps(u):
                d = u % 2
                act.wait_ge(s_mx, u + 1)
                if u in outs:
                    A.activation(DM[:, d], DM[:, d], ACT.Exp)
                A.activation(Z[:, d, AIN:EXM + 1], Z[:, d, AIN:EXM + 1], ACT.Exp).then_inc(s_ex, 1)

            exps(0)
            for u in range(NSTEP):
                if u in outs:
                    act.wait_ge(s_tr, outs.index(u) + 1)
                    A.activation(PTT[:, u % 2].rearrange("p h t -> p (h t)"), PS[:, banks(u)[0], :], ACT.Copy
                                 ).then_inc(s_pt, 1)
                if u + 1 < NSTEP:
                    exps(u + 1)

    with ExitStack() as st, nc.Block() as block:
        sg = e.sb(st, f"sig_o{l}", [P, 2, 512])
        sq = e.sb(st, f"c_sq{l}", [P, 4, P])
        ms = e.sb(st, f"c_ms{l}", [P, TT, 4])
        t0 = tiles[0]
        s_co, s_sg, s_oc, s_ot, s_oev = (sem(f"{n}{l}") for n in (
            "co_done", "co_sigmoid", "oc_ready", "ocT", "ocT_stored"))
        e.freed[PLACE[l, "in", CO]] = (s_co, len(tiles))
        split = Split(e, st, f"co{l}", [(PLACE[l, "in", CO], [(k * 512, 512) for k in range(KT)])], KT)
        s_ms, s_rs = sem(f"c_mean_square{l}"), sem(f"c_inv_rms{l}")

        @block.sync
        def _(sp):
            e.sp_loads(sp, PLACE[l, "in", CO] + 1 + RING)

        @block.tensor
        def _(pe):
            def back(i, t):
                pe.wait_ge(s_oc, i + 1)
                if i >= 2:
                    pe.wait_ge(s_oev, i - 1)
                for j in range(4):
                    last = T.transpose(PS[:, 4 + i % 2, j * P:j * P + P], H[:, t, j * P:j * P + P], e.ident)
                last.then_inc(s_ot, 1)

            for i, t in enumerate(tiles):
                for k in range(KT):
                    if not i:
                        split.wait(pe, 0, k)
                    toks = slice(t * P, t * P + P)
                    _, last = products(T, PS[:, i, :], (e.hTh[:, k, toks], e.hTl[:, k, toks]),
                                       split.block(0, k, 0, 512), k == 0, k == KT - 1)
                last.then_inc(s_co, 1)
                if i >= 1:
                    back(i - 1, tiles[i - 1])
            back(len(tiles) - 1, tiles[-1])

        @block.scalar
        def _(act):
            split.round_high(act, 0)
            act.wait_ge(s_ms, 1)
            A.activation(ms[:, t0:TT], ms[:, t0:TT], ACT.Sqrt, bias=e.eps).then_inc(s_rs, 1)
            for i, t in enumerate(tiles):
                act.wait_ge(s_co, i + 1)
                if i >= 2:
                    act.wait_ge(s_oc, i - 1)
                A.activation(sg[:, i % 2], PS[:, i, :], ACT.Sigmoid).then_inc(s_sg, 1)

        @block.vector
        def _(dve):
            gm = e.rowp[:, R_GMLSTM:R_GMLSTM + 512]
            split.leave_low(dve, 0)
            for t in tiles:
                hs = heads(H[:, t, :])
                e.vlink(V.tensor_tensor(sq[:], hs, hs, ALU.mult))
                e.vlink(V.reduce_sum(ms[:, t], sq[:], AX))
            V.tensor_scalar(ms[:, t0:TT], ms[:, t0:TT], 1.0 / P, None, ALU.mult).then_inc(s_ms, 1)
            dve.wait_ge(s_rs, 1)
            e.vlink(V.reciprocal(ms[:, t0:TT], ms[:, t0:TT]))
            for i, t in enumerate(tiles):
                hs = heads(H[:, t, :])
                e.vlink(V.tensor_tensor(hs, hs, e.bc(ms[:, t].unsqueeze(2), P, 4, P), ALU.mult))
                e.vlink(V.tensor_tensor(H[:, t, :], H[:, t, :], gm, ALU.mult))
                dve.wait_ge(s_sg, i + 1)
                V.tensor_tensor(H[:, t, :], H[:, t, :], sg[:, i % 2], ALU.mult).then_inc(s_oc, 1)
                dve.wait_ge(s_ot, i + 1)
                V.tensor_copy(m.cqT[:, :, t * P:t * P + P],
                              PS[:, 4 + i % 2, :].rearrange("p (j q) -> p j q", j=4)).then_inc(s_oev, 1)


def load_gate_rows(sp, a, l, which, dst, done):
    for v in range(2):
        sp.dma_start(dst[:, v], a["mod_rows"][l, v:v + 1, which * D:which * D + D].to_broadcast([P, D])).then_inc(done, 16)


def merge_stage(nc, a, e, m, l, tiles):
    V, A, T, PS, sem = e.V, e.A, e.T, e.PS, e.sem
    nt = len(tiles)
    srcs = [m.aqT, m.bqT, m.cqT]
    flat, flat_r = (x[:].rearrange("p t h q -> p (t h q)") for x in (m.cv, m.cv_r))
    high = [m.ck_r[:], m.bv_r[:], flat_r[:, 0:TT * 512].rearrange("p (j q) -> p j q", j=4)]
    low = [m.aqT_r, m.bqT_r, m.cqT_r]
    YY = [m.bkT[:], m.ckT[:]]
    with ExitStack() as st, nc.Block() as block:
        sg = [m.misc[:].rearrange("p t n -> p (t n)")[:, 0:512], m.akT[:, 0]]
        s_g, s_b, s_sg, s_y, s_hi, s_lo = (sem(f"{n}{l}") for n in (
            "gate_done", "branch_done", "gate_sigmoid", "y_updated", "branch_high_ready", "branch_split"))
        units = [(j, b, t) for j in range(2) for b in range(3) for t in tiles]
        NBK = KT + 4
        split = Split(e, st, f"merge{l}", [(PLACE[l, "merge", c], [(k * 512, 512) for k in range(NBK)]) for c in range(6)],
                      NBK)
        for c in range(6):
            e.freed[PLACE[l, "merge", c]] = (s_b, nt * (c + 1))

        @block.sync
        def _(sp):
            e.sp_loads(sp, PLACE[l, "out", 0] + RING)

        @block.tensor
        def _(pe):
            for u, (j, b, t) in enumerate(units):
                c = u // nt
                toks = slice(t * P, t * P + P)
                if u >= 2:
                    pe.wait_ge(s_y, u - 1)
                for k in range(NBK):
                    if u % nt == 0:
                        split.wait(pe, c, k)
                    if k < KT:
                        used, last = products(T, PS[:, u % 2, :], (e.hTh[:, k, toks], e.hTl[:, k, toks]),
                                              split.block(c, k, 0, 512), k == 0, k == KT - 1)
                    else:
                        x = k - KT
                        if x == 0:
                            pe.wait_ge(s_lo, b + 1)
                        used, last = products(T, PS[:, 2 + u % 2, :],
                                              (high[b][:, x, toks], low[b][:, x, toks]),
                                              split.block(c, k, 0, 512), x == 0, x == 3)
                    if u % nt == nt - 1:
                        used.then_inc(split.s_used, 1)
                    if k == KT - 1:
                        last.then_inc(s_g, 1)
                last.then_inc(s_b, 1)

        @block.scalar
        def _(act):
            def branch(b):
                A.activation(high[b][:, :, tiles[0] * P:].bitcast(F32R), srcs[b][:, :, tiles[0] * P:], ACT.Copy
                             ).then_inc(s_hi, 1)

            split.round_high(act, 0)
            for b in range(3):
                branch(b)
            for u in range(len(units)):
                if u % nt == nt - 1 and u // nt < 5:
                    split.round_high(act, u // nt + 1)
                act.wait_ge(s_g, u + 1)
                if u >= 2:
                    act.wait_ge(s_y, u - 1)
                A.activation(sg[u % 2], PS[:, u % 2, :], ACT.Sigmoid).then_inc(s_sg, 1)

        @block.vector
        def _(dve):
            split.leave_low(dve, 0)
            for b in range(3):
                dve.wait_ge(s_hi, b + 1)
                V.tensor_tensor(low[b][:, :, tiles[0] * P:], srcs[b][:, :, tiles[0] * P:],
                                high[b][:, :, tiles[0] * P:].bitcast(F32), ALU.subtract).then_inc(s_lo, 1)
            for u, (j, b, t) in enumerate(units):
                if u % nt == nt - 1 and u // nt < 5:
                    split.leave_low(dve, u // nt + 1)
                dve.wait_ge(s_sg, u + 1)
                dve.wait_ge(s_b, u + 1)
                if b == 0:
                    V.tensor_tensor(YY[j][:, t], PS[:, 2 + u % 2, :], sg[u % 2], ALU.mult).then_inc(s_y, 1)
                else:
                    e.vlink(V.tensor_tensor(sg[u % 2], PS[:, 2 + u % 2, :], sg[u % 2], ALU.mult))
                    V.tensor_tensor(YY[j][:, t], YY[j][:, t], sg[u % 2], ALU.add).then_inc(s_y, 1)

    with ExitStack() as st, nc.Block() as block:
        s_yt, s_yh, s_ys, s_out, s_xu, s_om, s_rows = (sem(f"{n}{l}") for n in (
            "yT", "yT_high_stored", "yT_low_stored", "out_done", "x_updated", "out_gated", "mix_rows_loaded"))
        YT = [m.aqT_r, m.bqT_r]
        rows = flat[:, 0:2 * D].rearrange("p (v d) -> p v d", v=2)
        og = e.sb(st, f"out_gated{l}", [P, 2, 512])
        split = Split(e, st, f"out{l}", [(PLACE[l, "out", j], [(k * 512, 512) for k in range(KT)]) for j in range(2)], KT)
        pieces = [(t, j) for t in tiles for j in range(2)]
        units = [(j, t) for j in range(2) for t in tiles]
        for j in range(2):
            e.freed[PLACE[l, "out", j]] = (s_out, nt * (j + 1))

        @block.sync
        def _(sp):
            load_gate_rows(sp, a, l, 2, rows, s_rows)
            e.sp_loads(sp, PLACE[l, "shared", 0] + 1)

        @block.tensor
        def _(pe):
            for i, (t, j) in enumerate(pieces):
                if i >= 4:
                    pe.wait_ge(s_ys, i - 3)
                for k in range(4):
                    last = T.transpose(PS[:, i % 4, k * P:k * P + P], YY[j][:, t, k * P:k * P + P], e.ident)
                last.then_inc(s_yt, 1)
            for u, (j, t) in enumerate(units):
                toks = slice(t * P, t * P + P)
                if j == 0:
                    pe.wait_ge(s_ys, 2 * (u + 1))
                if u >= 4:
                    pe.wait_ge(s_om, u - 3)
                for k in range(KT):
                    if u % nt == 0:
                        split.wait(pe, j, k)
                    yt = (high[k // 4][:, k % 4, toks], YT[k // 4][:, k % 4, toks])
                    used, last = products(T, PS[:, 4 + u % 4, :], yt, split.block(j, k, 0, 512), k == 0, k == KT - 1)
                    if u % nt == nt - 1:
                        used.then_inc(split.s_used, 1)
                last.then_inc(s_out, 1)

        @block.scalar
        def _(act):
            for i, (t, j) in enumerate(pieces):
                act.wait_ge(s_yt, i + 1)
                A.activation(high[j][:, :, t * P:t * P + P], PS[:, i % 4, :].rearrange("p (k q) -> p k q", k=4),
                             ACT.Copy).then_inc(s_yh, 1)
                if i == 1:
                    split.round_high(act, 0)
            split.round_high(act, 1)

        @block.vector
        def _(dve):
            for i, (t, j) in enumerate(pieces):
                dve.wait_ge(s_yh, i + 1)
                V.tensor_tensor(YT[j][:, :, t * P:t * P + P], PS[:, i % 4, :].rearrange("p (k q) -> p k q", k=4),
                                high[j][:, :, t * P:t * P + P].bitcast(F32), ALU.subtract).then_inc(s_ys, 1)
                if i == 1:
                    split.leave_low(dve, 0)
            dve.wait_ge(s_rows, 32)
            for u, (j, t) in enumerate(units):
                if u == nt - 1:
                    split.leave_low(dve, 1)
                v = 0 if t < LAT0 else 1
                dve.wait_ge(s_out, u + 1)
                V.tensor_tensor(og[:, u % 2], PS[:, 4 + u % 4, :], rows[:, v, j * 512:j * 512 + 512],
                                ALU.mult).then_inc(s_om, 1)
                dve.wait_ge(s_om, u + 1)
                xs = e.X[:, t, j * 512:j * 512 + 512]
                V.tensor_tensor(xs, xs, og[:, u % 2], ALU.add).then_inc(s_xu, 1)


def moe(nc, a, e, l, tiles):
    with ExitStack() as st:
        slots = [e.ring[0], e.ring[1]] + [e.sb(st, f"weights{i}_{l}", [P, SLOT]) for i in range(RING, NSLOT)]
        nt = len(tiles)
        r = Space()
        r.shared = e.sb(st, f"shared_out{l}", [P, nt, D])
        r.rows = e.sb(st, f"moe_rows{l}", [P, 2, D])
        r.weight = e.sb(st, f"route_weight{l}", [P, nt, TOPK])
        r.yrow = e.sb(st, f"y_row_index{l}", [P, nt, TOPK], I32)
        r.posb = e.sb(st, f"slot_position{l}", [P, NBLK, nt, NE])
        r.tokid = e.sb(st, f"token_id{l}", [P, nt], FP16)
        r.tok = e.sb(st, f"slot_token{l}", [P, NE], I32)
        r.over = e.sb(st, f"overflow_table{l}", [1, 3, P], I32)
        r.gate = e.sb(st, f"route_gate{l}", [P, nt, NE])
        with ExitStack() as st2, nc.Block() as block:
            S = e.sb(st2, f"scores{l}", [P, nt, NE])
            shared_route_stage(nc, a, e, r, l, tiles, S, slots, st2, block)
        with ExitStack() as st2:
            b = Space()
            b.xg, b.y = (e.hT[:, i:i + 4].rearrange("p k t -> p (k t)").rearrange("p (i d) -> p i d", i=2) for i in (0, 4))
            b.xT = e.sb(st2, f"gatheredT{l}", [P, 2, KT, P])
            b.sl = e.sb(st2, f"silu{l}", [P, 2, DE])
            b.ac = e.sb(st2, f"act{l}", [P, 2, DE])
            b.acT = e.sb(st2, f"actT{l}", [P, 2, 2, P])
            b.idx = e.sb(st2, f"gather_index{l}", [P, 2], I32)
            experts_stage(nc, a, e, r, b, l, slots)
            gathers = Gathers(a, e, r, l, nt, slots)
            overflow_combine_stage(nc, a, e, r, b, l, tiles, slots, gathers)


def shared_route_stage(nc, a, e, r, l, tiles, S, slots, st, block):
    V, A, T, G, PS, sem = e.V, e.A, e.T, e.G, e.PS, e.sem
    n = PLACE[l, "shared", 0]
    nt = len(tiles)
    iota = e.iota
    EC = 4

    last_slot = slots[NSLOT - 1]
    at = [0]

    def carve(cols, *shape):
        ap = last_slot[:, at[0]:at[0] + cols]
        at[0] += cols
        if len(shape) == 2:
            return ap.rearrange("p (i d) -> p i d", i=shape[0])
        if len(shape) == 3:
            return ap.rearrange("p (i k d) -> p i k d", i=shape[0], k=shape[1])
        return ap

    wr = carve(KT * NE)
    ht = carve(2 * D, 2, D)
    sl, up, ac = (carve(2 * DE, 2, DE) for _ in range(3))
    acT = carve(2 * DE, 2, 2, P)
    logits = last_slot[0:NE, at[0]:at[0] + nt * P]
    s_wr, s_rt, s_ht, s_hta, s_g, s_sl, s_ac, s_h, s_at, s_dn, s_ya = (sem(f"{x}{l}") for x in (
        "w_router_loaded", "router_done", "h_transposed", "h_token_ready", "sh_gate_up", "sh_silu_done",
        "sh_act_ready", "sh_act_transposed", "sh_actT_ready", "sh_down", "sh_stored"))
    s_hs = [sem(f"h_rows_written{i}_{l}") for i in range(2)]
    s_rows, s_lg, s_S = sem(f"moe_rows_loaded{l}"), sem(f"logits_stored{l}"), sem(f"scores_ready{l}")
    e.freed[n] = (s_dn, nt)

    sel = e.sb(st, f"sel{l}", [P, nt, NE])
    top = e.sb(st, f"group_top{l}", [P, nt, NG, 8])
    gs = e.sb(st, f"group_score{l}", [P, nt, NG])
    v8 = e.sb(st, f"top_values{l}", [P, nt, 8])
    i8 = e.sb(st, f"top_index{l}", [P, nt, 8], U32)
    f8 = e.sb(st, f"top_index_f{l}", [P, nt, 8])
    ohg = e.sb(st, f"group_onehot{l}", [P, nt, 4, NG])
    gm = e.sb(st, f"group_mask{l}", [P, nt, NG])
    oh = e.sb(st, f"expert_onehot{l}", [P, nt, 8, NE])
    tmp = e.sb(st, f"route_tmp{l}", [P, 8, NE])
    M = e.sb(st, f"expert_mask{l}", [P, nt, NE])
    ws = e.sb(st, f"weight_sum{l}", [P, nt])
    p8 = e.sb(st, f"top_pos{l}", [P, nt, 8])
    one = e.sb(st, f"slot_onehot{l}", [P, 2, nt, EC, P], FP16)
    ov = e.sb(st, f"over_tmp{l}", [P, 4, 3, NE])
    oc = e.sb(st, f"over_cols{l}", [P, 3])
    s_m, s_pos, s_one, s_tok, s_oc, s_or = (sem(f"{x}{l}") for x in (
        "masks_ready", "positions_done", "onehot_ready", "tokens_done", "over_cols_ready", "over_rows_done"))
    rank_ps, count_ps = PS[:, 7, 4 * NE:4 * NE + nt * NE], PS[:, 7, 0:NE]
    tok_ps, over_ps = PS[:, 7, NE:2 * NE], PS[0:1, 7, 2 * NE:2 * NE + 3 * P]

    @block.sync
    def _(sp):
        def expert(q):
            sp.dma_start(slots[q][:], a["wexp"][l, q]).then_inc(e.ld[q], 16)

        sp.dma_start(wr, a["wr"][l]).then_inc(s_wr, 16)
        load_gate_rows(sp, a, l, 5, r.rows, s_rows)
        expert((n + 1) % RING)
        expert(2)
        for i, t in enumerate(tiles):
            sp.wait_ge(s_hta, i + 1)
            sp.dma_start(a["h_rows"][t * P:t * P + P, :], ht[:, i % 2]).then_inc(s_hs[i % 2], 16)
        sp.wait_ge(s_dn, nt)
        expert(n % RING)
        for i in range(2):
            sp.wait_ge(s_hs[i], 16 * (nt // 2))
        sp.wait_ge(s_S, 1)
        expert(3)
        sp.wait_ge(s_rows, 32)

    @block.vector
    def _(dve):
        dve.wait_ge(s_S, 1)
        e.vlink(V.tensor_tensor(sel[:], S[:], e.bc(e.rowp[:, R_BROUTER:R_BROUTER + NE].unsqueeze(1), P, nt, NE), ALU.add))
        for i in range(nt):
            for g in range(NG):
                last = V.max(top[:, i, g], sel[:, i, g * PER:g * PER + PER])
        e.vlink(last)
        e.vlink(V.tensor_tensor(gs[:], top[:, :, :, 0], top[:, :, :, 1], ALU.add))
        for i in range(nt):
            last = V.max(v8[:, i], gs[:, i])
        e.vlink(last)
        for i in range(nt):
            last = V.max_index(i8[:, i], v8[:, i], gs[:, i])
        e.vlink(last)
        e.vlink(V.tensor_copy(f8[:], i8[:]))
        e.vlink(V.tensor_tensor(ohg[:], e.bc(iota[:, 0:NG].unsqueeze(1).unsqueeze(1), P, nt, 4, NG),
                                e.bc(f8[:, :, 0:4].unsqueeze(3), P, nt, 4, NG), ALU.is_equal))
        e.vlink(V.reduce_sum(gm[:], ohg[:].rearrange("p t k g -> p t g k"), AX))
        e.vlink(V.tensor_scalar(gm[:], gm[:], BIG, -BIG, ALU.mult, ALU.add))
        e.vlink(V.tensor_tensor(sel[:].rearrange("p t (g e) -> p t g e", g=NG),
                                sel[:].rearrange("p t (g e) -> p t g e", g=NG),
                                e.bc(gm[:].unsqueeze(3), P, nt, NG, PER), ALU.add))
        for i in range(nt):
            last = V.max(v8[:, i], sel[:, i])
        e.vlink(last)
        for i in range(nt):
            last = V.max_index(i8[:, i], v8[:, i], sel[:, i])
        e.vlink(last)
        e.vlink(V.tensor_copy(f8[:], i8[:]))
        for i in range(nt):
            e.vlink(V.tensor_tensor(oh[:, i], e.bc(iota[:, 0:NE].unsqueeze(1), P, 8, NE),
                                    e.bc(f8[:, i].unsqueeze(2), P, 8, NE), ALU.is_equal))
            V.reduce_sum(M[:, i], oh[:, i].rearrange("p k e -> p e k"), AX).then_inc(s_m, 1)
            e.vlink(V.tensor_tensor(tmp[:], oh[:, i], e.bc(S[:, i].unsqueeze(1), P, 8, NE), ALU.mult))
            e.vlink(V.reduce_sum(r.weight[:, i], tmp[:], AX))
        e.vlink(V.reduce_sum(ws[:], r.weight[:], AX))
        e.vlink(V.reciprocal(ws[:], ws[:]))
        e.vlink(V.tensor_scalar(ws[:], ws[:], ROUTED_SCALE, None, ALU.mult))
        e.vlink(V.tensor_tensor(r.weight[:], r.weight[:], e.bc(ws[:].unsqueeze(2), P, nt, 8), ALU.mult))
        for i in range(nt):
            e.vlink(V.tensor_tensor(tmp[:], oh[:, i], e.bc(r.weight[:, i].unsqueeze(2), P, 8, NE), ALU.mult))
            e.vlink(V.reduce_sum(r.gate[:, i], tmp[:].rearrange("p k e -> p e k"), AX))
        e.vlink(V.tensor_copy(r.tokid[:], e.cst[:, C_TOK + tiles[0]:C_TOK + TT]))
        dve.wait_ge(s_pos, 1)
        pos = r.posb[:, 0]
        rank = rank_ps.rearrange("p (t e) -> p t e", t=nt)
        e.vlink(V.tensor_tensor(pos, rank, M[:], ALU.mult))
        e.vlink(V.tensor_scalar(pos, pos, -1.0, None, ALU.add))
        for b in range(1, NBLK):
            V.tensor_scalar(r.posb[:, b], pos, -float(b * P), None, ALU.add)
        for i in range(nt):
            e.vlink(V.tensor_tensor(tmp[:], oh[:, i], e.bc(pos[:, i].unsqueeze(1), P, 8, NE), ALU.mult))
            e.vlink(V.reduce_sum(p8[:, i], tmp[:], AX))
        e.vlink(V.scalar_tensor_tensor(r.weight[:], p8[:], float(P), r.weight[:], ALU.is_lt, ALU.mult))
        e.vlink(V.tensor_scalar(p8[:], p8[:], float(P - 1), None, ALU.min))
        e.vlink(V.scalar_tensor_tensor(p8[:], f8[:], float(P), p8[:], ALU.mult, ALU.add))
        e.vlink(V.tensor_copy(r.yrow[:], p8[:]))
        cnt = ov[:, 3, 0]
        e.vlink(V.tensor_copy(cnt, count_ps))
        flag, cum = ov[:, 0], ov[:, 1]
        for b in range(3):
            last = V.tensor_scalar(flag[:, b], cnt, float((b + 1) * P), None, ALU.is_gt)
        e.vlink(last)
        fl = flag.rearrange("p b e -> p (b e)")
        cf = cum.rearrange("p b e -> p (b e)")
        ovt = ov[:, 2].rearrange("p b e -> p (b e)")
        e.vlink(V.tensor_tensor_scan(cf, e.bc(e.ones[:, 0:1], P, 3 * NE), fl, 0.0, ALU.mult, ALU.add))
        e.vlink(V.tensor_copy(oc[:, 2:3], cf[:, 3 * NE - 1:3 * NE]))
        e.vlink(V.scalar_tensor_tensor(cf, cf, e.cst[:, C_PIDX1:C_PIDX1 + 1], fl, ALU.is_equal, ALU.mult))
        for c in range(2):
            e.vlink(V.tensor_tensor(ovt, cf, e.cst[:, C_OVER + c * 192:C_OVER + c * 192 + 192], ALU.mult))
            e.vlink(V.reduce_sum(oc[:, c:c + 1], ovt, AX))
        V.scalar_tensor_tensor(oc[:, 1:2], oc[:, 1:2], float(nt * NE), oc[:, 0:1], ALU.mult, ALU.add
                               ).then_inc(s_oc, 1)
        for c in range(NE // EC):
            if c >= 2:
                dve.wait_ge(s_tok, c - 1)
            V.tensor_tensor(one[:, c % 2], e.bc(iota.unsqueeze(1).unsqueeze(1), P, nt, EC, P),
                            e.bc(pos[:, :, c * EC:c * EC + EC].unsqueeze(3), P, nt, EC, P), ALU.is_equal
                            ).then_inc(s_one, 1)
        dve.wait_ge(s_or, 1)
        dve.wait_ge(s_tok, NE // EC)
        V.tensor_copy(r.over[:], over_ps.rearrange("p (c i) -> p c i", c=3))
        V.tensor_copy(r.tok[:], tok_ps)

    @block.tensor
    def _(pe):
        BETWEEN = nt // 2

        def token_form(i):
            if i >= 1:
                pe.wait_ge(s_hta, i)
            for k in range(KT):
                last = T.transpose(PS[:, k // 4, (k % 4) * P:(k % 4) * P + P],
                                   e.hT[:, k, tiles[i] * P:tiles[i] * P + P], e.ident)
            last.then_inc(s_ht, 1)

        token_form(0)
        pe.wait_ge(s_wr, 16)
        for k in range(KT):
            last = T.matmul(PS[0:NE, 6, 0:nt * P], wr[:, k * NE:k * NE + NE], e.hT[:, k, tiles[0] * P:NTOK],
                            start=k == 0, stop=k == KT - 1)
        last.then_inc(s_rt, 1)
        pe.wait_ge(s_lg, 1)
        for i in range(nt):
            last = T.transpose(PS[:, 7, i * NE:i * NE + NE], logits[:, i * P:i * P + P], e.ident[0:NE, 0:NE])
        last.then_inc(s_rt, 1)
        w = e.chunk_ready(pe, n)

        def ranks():
            pe.wait_ge(s_m, nt)
            for i in range(nt):
                for j in range(i + 1):
                    T.matmul(rank_ps[:, i * NE:i * NE + NE], e.cst[:, C_LE:C_LE + P] if j == i else e.ones, M[:, j],
                             start=j == 0, stop=j == i)
            for j in range(nt):
                last = T.matmul(count_ps, e.ones, M[:, j], start=j == 0, stop=j == nt - 1)
            last.then_inc(s_pos, 1)

        done = [0]

        def slot_tokens():
            c = done[0]
            if c == 0:
                pe.wait_ge(s_oc, 1)
                for x in range(3):
                    last = T.matmul(over_ps[:, x * P:x * P + P], oc[:, x:x + 1], e.ident, start=True, stop=True)
                last.then_inc(s_or, 1)
            pe.wait_ge(s_one, c + 1)
            for x in range(EC):
                for i in range(nt):
                    last = T.matmul(tok_ps[:, c * EC + x:c * EC + x + 1], one[:, c % 2, i, x], r.tokid[:, i:i + 1],
                                    start=i == 0, stop=i == nt - 1)
            last.then_inc(s_tok, 1)
            done[0] += 1

        for i, t in enumerate(tiles):
            if i:
                token_form(i)
            for k in range(KT):
                last = T.matmul(PS[:, 2 + i % 2, :], e.hT[:, k, t * P:t * P + P], w[:, k * 512:k * 512 + 512],
                                start=k == 0, stop=k == KT - 1)
            last.then_inc(s_g, 1)
            if i == nt // 2 - 1:
                ranks()
            if i >= BETWEEN:
                slot_tokens()
            pe.wait_ge(s_ac, i + 1)
            for k in range(2):
                last = T.transpose(PS[:, 6, k * P:k * P + P], ac[:, i % 2, k * P:k * P + P], e.ident)
            last.then_inc(s_h, 1)
            if i > BETWEEN:
                slot_tokens()
            pe.wait_ge(s_at, i + 1)
            if i >= 1:
                pe.wait_ge(s_ya, i)
            for j in range(2):
                for k in range(2):
                    x = KT * 512 + k * D + j * 512
                    last = T.matmul(PS[:, 4 + j, :], acT[:, i % 2, k], w[:, x:x + 512], start=k == 0, stop=k == 1)
            last.then_inc(s_dn, 1)
            if i >= BETWEEN:
                slot_tokens()
        while done[0] < NE // EC:
            slot_tokens()

    @block.scalar
    def _(act):
        act.wait_ge(s_rt, 1)
        A.activation(logits, PS[0:NE, 6, 0:nt * P], ACT.Copy).then_inc(s_lg, 1)
        act.wait_ge(s_rt, 2)
        A.activation(S[:].rearrange("p t e -> p (t e)"), PS[:, 7, 0:nt * NE], ACT.Sigmoid).then_inc(s_S, 1)
        for i, t in enumerate(tiles):
            act.wait_ge(s_ht, i + 1)
            if i >= 2:
                act.wait_ge(s_hs[i % 2], 16 * (i // 2))
            A.activation(ht[:, i % 2, 0:512], PS[:, 0, :], ACT.Copy)
            A.activation(ht[:, i % 2, 512:D], PS[:, 1, :], ACT.Copy).then_inc(s_hta, 1)
            act.wait_ge(s_g, i + 1)
            if i >= 2:
                act.wait_ge(s_ac, i - 1)
            A.activation(sl[:, i % 2], PS[:, 2 + i % 2, 0:DE], ACT.Silu)
            A.activation(up[:, i % 2], PS[:, 2 + i % 2, DE:2 * DE], ACT.Copy).then_inc(s_sl, 1)
            act.wait_ge(s_h, i + 1)
            A.activation(acT[:, i % 2].rearrange("p k t -> p (k t)"), PS[:, 6, 0:2 * P], ACT.Copy).then_inc(s_at, 1)
            act.wait_ge(s_dn, i + 1)
            A.activation(r.shared[:, i, 0:512], PS[:, 4, :], ACT.Copy)
            A.activation(r.shared[:, i, 512:D], PS[:, 5, :], ACT.Copy).then_inc(s_ya, 1)

    @block.gpsimd
    def _(pool):
        for i in range(nt):
            pool.wait_ge(s_sl, i + 1)
            if i >= 2:
                pool.wait_ge(s_h, i - 1)
            G.tensor_tensor(ac[:, i % 2], sl[:, i % 2], up[:, i % 2], ALU.mult).then_inc(s_ac, 1)


def experts_stage(nc, a, e, r, b, l, slots):
    V, A, T, G, PS, sem = e.V, e.A, e.T, e.G, e.PS, e.sem
    with nc.Block() as block:
        s_t, s_xe, s_g, s_sl, s_ac, s_h, s_at, s_dn, s_ye, s_pi = (sem(f"{x}{l}") for x in (
            "tokens_transposed", "tokensT_ready", "gate_up_done", "silu_done", "act_ready", "act_transposed",
            "actT_ready", "down_done", "y_ready", "gather_index_ready"))
        s_xg = [e.kept_sem(f"tokens_gathered{i}_{l}") for i in range(2)]
        s_st = [sem(f"y_stored{i}_{l}") for i in range(2)]
        base = [16 * e.loads[q] for q in range(NSLOT)]
        for q in range(NSLOT):
            e.loads[q] += NE // NSLOT

        def groups(eng, body):
            with eng.Fori(0, NE // NSLOT - 1) as g:
                for q in range(NSLOT):
                    body(g, q)
            for q in range(NSLOT):
                body(NE // NSLOT - 1, q)

        def later(g, q, by):
            gg, qq = g + (q + by) // NSLOT, (q + by) % NSLOT
            return None if isinstance(g, int) and gg >= NE // NSLOT else (gg, qq)

        @block.sync
        def _(sp):
            with sp.Fori(1, NE // NSLOT) as g:
                for q in range(NSLOT):
                    sp.wait_ge(s_dn, 4 * g + q - 3 + 2)
                    sp.wait_ge(e.ld[q], 16)
                    sp.dma_start(slots[q][:], a["wexp"][l, g * NSLOT + q]).then_inc(e.ld[q], 16)

        @block.gpsimd
        def _(pool):
            def gather(g, q):
                p = q % 2
                pool.wait_ge(s_t, 4 * g + q + 1)
                G.tensor_copy(b.idx[:, p:p + 1], r.tok[:, bass.ds(g * NSLOT + q, 1)]).then_inc(s_pi, 1)
                pool.wait_ge(s_pi, 1)
                pool.sem_clear(s_pi)
                G.indirect_dma_start(b.xg[:, p], None, a["h_rows"],
                                     bass.IndirectOffsetOnAxis(ap=b.idx[:, p:p + 1], axis=0)).then_inc(s_xg[p], 16)
            groups(pool, gather)

        @block.tensor
        def _(pe):
            pe.sem_inc(s_t, 2)
            pe.sem_inc(s_g, 2)
            pe.sem_inc(s_h, 2)
            pe.sem_inc(s_dn, 2)

            def tokens(g, q):
                p = q % 2
                pe.wait_ge(s_xg[p], 32 * g + 16 * (q // 2 + 1))
                pe.wait_ge(s_xe, 8 * g + 2 * q + 2)
                for k in range(KT):
                    last = T.transpose(PS[:, k // 4, (k % 4) * P:(k % 4) * P + P], b.xg[:, p, k * P:k * P + P], e.ident)
                last.then_inc(s_t, 1)

            def gate_up(g, q):
                p = q % 2
                pe.wait_ge(e.ld[q], base[q] + 16 * g + 16)
                pe.wait_ge(s_xe, 8 * g + 2 * q + 4)
                pe.wait_ge(s_ac, 4 * g + q + 1)
                for k in range(KT):
                    last = T.matmul(PS[:, 2 + p, :], b.xT[:, p, k], slots[q][:, k * 512:k * 512 + 512],
                                    start=k == 0, stop=k == KT - 1)
                last.then_inc(s_g, 1)

            def act_t(g, q):
                p = q % 2
                pe.wait_ge(s_ac, 4 * g + q + 3)
                pe.wait_ge(s_at, 4 * g + q + 1)
                for k in range(2):
                    last = T.transpose(PS[:, 6, k * P:k * P + P], b.ac[:, p, k * P:k * P + P], e.ident)
                last.then_inc(s_h, 1)

            def down(g, q):
                p = q % 2
                pe.wait_ge(s_at, 4 * g + q + 2)
                pe.wait_ge(s_ye, 8 * g + 2 * q + 2)
                for j in range(2):
                    for k in range(2):
                        at = KT * 512 + k * D + j * 512
                        last = T.matmul(PS[:, 4 + j, :], b.acT[:, p, k], slots[q][:, at:at + 512],
                                        start=k == 0, stop=k == 1)
                last.then_inc(s_dn, 1)

            def step(g, q):
                if n := later(g, q, 1):
                    gate_up(*n)
                act_t(g, q)
                if n := later(g, q, 2):
                    tokens(*n)
                down(g, q)

            tokens(0, 0)
            tokens(0, 1)
            gate_up(0, 0)
            groups(pe, step)

        @block.scalar
        def _(act):
            act.sem_inc(s_xe, 2)
            act.sem_inc(s_ye, 2)
            act.sem_inc(s_st[0], 16)
            act.sem_inc(s_st[1], 16)

            def tokens(g, q):
                p = q % 2
                act.wait_ge(s_t, 4 * g + q + 3)
                act.wait_ge(s_g, 4 * g + q + 1)
                A.activation(b.xT[:, p, 0:4].rearrange("p k t -> p (k t)"), PS[:, 0, :], ACT.Copy).then_inc(s_xe, 1)

            def silu(g, q):
                p = q % 2
                act.wait_ge(s_g, 4 * g + q + 3)
                act.wait_ge(s_ac, 4 * g + q + 1)
                A.activation(b.sl[:, p], PS[:, 2 + p, 0:DE], ACT.Silu).then_inc(s_sl, 1)

            def store(g, q):
                p = q % 2
                act.wait_ge(s_dn, 4 * g + q + 3)
                act.wait_ge(s_st[p], 32 * g + 16 * (q // 2) + 16)
                A.activation(b.y[:, p, 0:512], PS[:, 4, :], ACT.Copy).then_inc(s_ye, 1)
                act.wait_ge(s_ye, 8 * g + 2 * q + 4)
                act.dma_start(a["y_rows"].rearrange("(x r) d -> x r d", r=P)[g * NSLOT + q], b.y[:, p]
                              ).then_inc(s_st[p], 16)

            def step(g, q):
                if n := later(g, q, 1):
                    silu(*n)
                if n := later(g, q, 2):
                    tokens(*n)
                store(g, q)

            tokens(0, 0)
            tokens(0, 1)
            silu(0, 0)
            groups(act, step)
            for p in range(2):
                act.wait_ge(s_st[p], 16 * (NE // 2) + 16)

        @block.vector
        def _(dve):
            dve.sem_inc(s_ac, 2)
            dve.sem_inc(s_at, 1)

            def tokens(g, q):
                p = q % 2
                dve.wait_ge(s_t, 4 * g + q + 3)
                dve.wait_ge(s_g, 4 * g + q + 1)
                V.tensor_copy(b.xT[:, p, 4:KT].rearrange("p k t -> p (k t)"), PS[:, 1, :]).then_inc(s_xe, 1)

            def product(g, q):
                p = q % 2
                dve.wait_ge(s_sl, 4 * g + q + 1)
                dve.wait_ge(s_h, 4 * g + q + 1)
                V.tensor_tensor(b.ac[:, p], b.sl[:, p], PS[:, 2 + p, DE:2 * DE], ALU.mult).then_inc(s_ac, 1)

            def act_t(g, q):
                p = q % 2
                dve.wait_ge(s_h, 4 * g + q + 3)
                dve.wait_ge(s_dn, 4 * g + q + 1)
                V.tensor_copy(b.acT[:, p].rearrange("p k t -> p (k t)"), PS[:, 6, 0:2 * P]).then_inc(s_at, 1)

            def store(g, q):
                p = q % 2
                dve.wait_ge(s_dn, 4 * g + q + 3)
                dve.wait_ge(s_st[p], 32 * g + 16 * (q // 2) + 16)
                V.tensor_copy(b.y[:, p, 512:D], PS[:, 5, :]).then_inc(s_ye, 1)

            def step(g, q):
                act_t(g, q)
                if n := later(g, q, 1):
                    product(*n)
                if n := later(g, q, 2):
                    tokens(*n)
                store(g, q)

            tokens(0, 0)
            tokens(0, 1)
            product(0, 0)
            groups(dve, step)


class Gathers:

    def __init__(self, a, e, r, l, nt, slots):
        self.a, self.e, self.r = a, e, r
        self.units = [(2 * h + i, k) for h in range(nt // 2) for k in range(TOPK) for i in range(2)]
        self.buffers = [slot[:, i * D:(i + 1) * D] for slot in slots[RING:] for i in range(SLOT // D)]
        self.depth = len(self.buffers)
        self.landed = [e.kept_sem(f"y_gathered{i}_{l}") for i in range(self.depth)]
        self.s_added = e.sem(f"y_added{l}")

    def start(self, pool, units):
        for u in units:
            i, k = self.units[u]
            if u >= self.depth:
                pool.wait_ge(self.s_added, u - self.depth + 1)
            self.e.G.indirect_dma_start(self.buffers[u % self.depth], None, self.a["y_rows"],
                                        bass.IndirectOffsetOnAxis(ap=self.r.yrow[:, i, k:k + 1], axis=0)
                                        ).then_inc(self.landed[u % self.depth], 16)


def overflow_combine_stage(nc, a, e, r, b, l, tiles, slots, gathers):
    V, A, T, G, PS, sem = e.V, e.A, e.T, e.G, e.PS, e.sem
    nt = len(tiles)
    with ExitStack() as st, nc.Block() as block:
        pc = e.sb(st, f"over_pos{l}", [P, 2, nt])
        one = e.sb(st, f"over_onehot{l}", [P, nt, P], FP16)
        wone, woneT = (slots[1][:, i * nt * P:(i + 1) * nt * P].rearrange("p (t s) -> p t s", t=nt) for i in range(2))
        s_w, s_pc, s_one, s_tok, s_idx, s_t, s_xe, s_g, s_sl, s_ac, s_h, s_at, s_dn, s_ye, s_wt, s_wte, s_y, s_end = (
            sem(f"o_{x}{l}") for x in (
                "weights_loaded", "columns_ready", "onehot_ready", "tokens_found", "index_ready", "transposed",
                "xT_ready", "gate_up", "silu", "act", "actT", "actT_ready", "down", "y_ready", "weighted_transposed",
                "weightedT_ready", "y_at_tokens", "item_done"))
        s_xg = e.kept_sem(f"o_gathered_{l}")

        def items(eng, body, to_the_end=True):
            n = eng.value_load(r.over[0:1, 2, 0:1], min_val=0, max_val=MAXOVER)
            with eng.If(n > 0):
                with eng.Fori(0, n) as i:
                    body(i)
                    if to_the_end:
                        eng.wait_ge(s_end, i + 1)
                eng.nop()

        def field(eng, c, i, most):
            return eng.value_load(r.over[0:1, c, bass.ds(i, 1)], min_val=0, max_val=most)

        @block.sync
        def _(sp):
            def body(i):
                x = field(sp, 0, i, NE - 1)
                sp.wait_ge(s_dn, i + 1)
                sp.dma_start(slots[0][:], a["wexp"][l, x]).then_inc(s_w, 16)
            items(sp, body, False)

        @block.gpsimd
        def _(pool):
            def body(i):
                pool.wait_ge(s_idx, 1)
                pool.sem_clear(s_idx)
                G.indirect_dma_start(b.xg[:, 0], None, a["h_rows"],
                                     bass.IndirectOffsetOnAxis(ap=b.idx[:, 0:1], axis=0)).then_inc(s_xg, 16)
            items(pool, body, False)
            gathers.start(pool, range(len(gathers.units)))

        @block.vector
        def _(dve):
            def body(i):
                x = field(dve, 0, i, NE - 1)
                at = field(dve, 1, i, (NBLK - 1) * nt * NE + NE - 1)
                for t in range(nt):
                    V.tensor_copy(pc[:, 0, t:t + 1], r.posb[:].rearrange("p b t e -> p (b t e)")[:, bass.ds(at + t * NE, 1)])
                    last = V.tensor_copy(pc[:, 1, t:t + 1], r.gate[:, t, bass.ds(x, 1)])
                last.then_inc(s_pc, 1)
                dve.wait_ge(s_pc, i + 1)
                V.tensor_tensor(one[:], e.bc(e.iota.unsqueeze(1), P, nt, P), e.bc(pc[:, 0].unsqueeze(2), P, nt, P),
                                ALU.is_equal).then_inc(s_one, 1)
                dve.wait_ge(s_one, 2 * i + 1)
                V.tensor_tensor(wone, one[:], e.bc(pc[:, 1].unsqueeze(2), P, nt, P), ALU.mult).then_inc(s_one, 1)
                dve.wait_ge(s_tok, i + 1)
                V.tensor_copy(b.idx[:, 0:1], PS[:, 7, 0:1]).then_inc(s_idx, 1)
                dve.wait_ge(s_t, i + 1)
                V.tensor_copy(b.xT[:, 0, 4:KT].rearrange("p k t -> p (k t)"), PS[:, 1, :]).then_inc(s_xe, 1)
                dve.wait_ge(s_sl, i + 1)
                V.tensor_tensor(b.ac[:, 0], b.sl[:, 0], PS[:, 2, DE:2 * DE], ALU.mult).then_inc(s_ac, 1)
                dve.wait_ge(s_h, i + 1)
                V.tensor_copy(b.acT[:, 0].rearrange("p k t -> p (k t)"), PS[:, 6, 0:2 * P]).then_inc(s_at, 1)
                dve.wait_ge(s_dn, i + 2)
                V.tensor_copy(b.y[:, 0, 512:D], PS[:, 5, :]).then_inc(s_ye, 1)
                for t in range(nt):
                    for j in range(2):
                        dve.wait_ge(s_y, 2 * nt * i + 2 * t + j + 1)
                        ys = r.shared[:, t, j * 512:j * 512 + 512]
                        last = V.tensor_tensor(ys, ys, PS[:, 2 * t + j, :], ALU.add)
                last.then_inc(s_end, 1)
            items(dve, body)

            units, depth, s_added = gathers.units, gathers.depth, gathers.s_added
            for u, (i, k) in enumerate(units):
                if u >= 2:
                    dve.wait_ge(s_added, u - 1)
                dve.wait_ge(gathers.landed[u % depth], 16 * (u // depth + 1))
                V.scalar_tensor_tensor(r.shared[:, i], gathers.buffers[u % depth], r.weight[:, i, k:k + 1], r.shared[:, i],
                                       ALU.mult, ALU.add).then_inc(s_added, 1)
                if k == TOPK - 1:
                    dve.wait_ge(s_added, u + 1)
                    t = tiles[i]
                    v = 0 if t < LAT0 else 1
                    e.vlink(V.tensor_tensor(r.shared[:, i], r.shared[:, i], r.rows[:, v], ALU.mult))
                    V.tensor_tensor(e.X[:, t], e.X[:, t], r.shared[:, i], ALU.add)

        @block.tensor
        def _(pe):
            pe.sem_inc(s_dn, 1)

            def body(i):
                pe.wait_ge(s_one, 2 * i + 2)
                for t in range(nt):
                    last = T.matmul(PS[:, 7, 0:1], one[:, t], r.tokid[:, t:t + 1], start=t == 0, stop=t == nt - 1)
                last.then_inc(s_tok, 1)
                for t in range(nt):
                    last = T.transpose(PS[:, 3, t * P:t * P + P], wone[:, t], e.ident)
                last.then_inc(s_wt, 1)
                pe.wait_ge(s_xg, 16 * i + 16)
                for k in range(KT):
                    last = T.transpose(PS[:, k // 4, (k % 4) * P:(k % 4) * P + P], b.xg[:, 0, k * P:k * P + P], e.ident)
                last.then_inc(s_t, 1)
                pe.wait_ge(s_w, 16 * i + 16)
                pe.wait_ge(s_xe, 2 * i + 2)
                for k in range(KT):
                    last = T.matmul(PS[:, 2, :], b.xT[:, 0, k], slots[0][:, k * 512:k * 512 + 512],
                                    start=k == 0, stop=k == KT - 1)
                last.then_inc(s_g, 1)
                pe.wait_ge(s_ac, i + 1)
                for k in range(2):
                    last = T.transpose(PS[:, 6, k * P:k * P + P], b.ac[:, 0, k * P:k * P + P], e.ident)
                last.then_inc(s_h, 1)
                pe.wait_ge(s_at, i + 1)
                for j in range(2):
                    for k in range(2):
                        at = KT * 512 + k * D + j * 512
                        last = T.matmul(PS[:, 4 + j, :], b.acT[:, 0, k], slots[0][:, at:at + 512],
                                        start=k == 0, stop=k == 1)
                last.then_inc(s_dn, 1)
                pe.wait_ge(s_wte, i + 1)
                pe.wait_ge(s_ye, 2 * i + 2)
                for t in range(nt):
                    for j in range(2):
                        T.matmul(PS[:, 2 * t + j, :], woneT[:, t], b.y[:, 0, j * 512:j * 512 + 512],
                                 start=True, stop=True).then_inc(s_y, 1)
            items(pe, body)

        @block.scalar
        def _(act):
            def body(i):
                act.wait_ge(s_wt, i + 1)
                A.activation(woneT.rearrange("p t s -> p (t s)"), PS[:, 3, 0:nt * P], ACT.Copy).then_inc(s_wte, 1)
                act.wait_ge(s_t, i + 1)
                A.activation(b.xT[:, 0, 0:4].rearrange("p k t -> p (k t)"), PS[:, 0, :], ACT.Copy).then_inc(s_xe, 1)
                act.wait_ge(s_g, i + 1)
                A.activation(b.sl[:, 0], PS[:, 2, 0:DE], ACT.Silu).then_inc(s_sl, 1)
                act.wait_ge(s_dn, i + 2)
                A.activation(b.y[:, 0, 0:512], PS[:, 4, :], ACT.Copy).then_inc(s_ye, 1)
            items(act, body)


def final_norm(nc, a, e):
    V, A, T, PS, sem = e.V, e.A, e.T, e.PS, e.sem
    with ExitStack() as st, nc.Block() as block:
        g = e.sb(st, "g_final", [P, D])
        sq = e.sb(st, "final_sq", [P, 2, D])
        ms = e.sb(st, "final_ms", [P, 2])
        s_g, s_y, s_o = sem("g_final_loaded"), sem("final_ready"), e.s_written
        s_ms, s_rs = sem("final_mean_square"), sem("final_inv_rms")

        @block.sync
        def _(sp):
            sp.dma_start(g[:], a["gfinal"]).then_inc(s_g, 16)
            for i in range(2):
                sp.wait_ge(s_y, i + 1)
                sp.dma_start(a["out"][i * P:i * P + P, :], e.X[:, LAT0 + i]).then_inc(s_o, 16)
            sp.wait_ge(s_o, 32)

        @block.vector
        def _(dve):
            dve.wait_ge(s_g, 16)
            for i in range(2):
                x = e.X[:, LAT0 + i]
                V.tensor_tensor_reduce(out=sq[:, i], in0=x, in1=x, scale=1.0 / D, scalar=0.0, op0=ALU.mult,
                                       op1=ALU.add, accum_out=ms[:, i:i + 1]).then_inc(s_ms, 1)
            dve.wait_ge(s_ms, 2)
            dve.wait_ge(s_rs, 1)
            e.vlink(V.reciprocal(ms[:], ms[:]))
            for i in range(2):
                x = e.X[:, LAT0 + i]
                V.scalar_tensor_tensor(x, x, ms[:, i:i + 1], g[:], ALU.mult, ALU.mult).then_inc(s_y, 1)

        @block.scalar
        def _(act):
            act.wait_ge(s_ms, 2)
            A.activation(ms[:], ms[:], ACT.Sqrt, bias=e.eps).then_inc(s_rs, 1)


def constants():
    import numpy as np
    c = np.zeros((P, NCONST), np.float32)
    i = np.arange(P)
    c[:, C_ID:C_ID + P] = np.eye(P)
    c[:, C_ONES:C_ONES + P] = 1
    c[:, C_LE:C_LE + P] = i[:, None] <= i[None, :]
    c[:, C_GE:C_GE + P] = i[:, None] >= i[None, :]
    q = DH // 4
    half = (i // q) % 2
    for p in range(P):
        if half[p] == 0:
            c[p + q, C_ROT + p] = -1
        else:
            c[p - q, C_ROT + p] = 1
    tok = np.arange(NLAT)
    inv = (1.0 / (np.float32(10000.0) ** (np.arange(q, dtype=np.float32) / np.float32(q)))).astype(np.float32)
    pos = np.stack([tok // 64, tok % 64]).astype(np.float32)
    ang = pos[(i % DH) // (2 * q)] * inv[i % q][:, None]
    c[:, C_COS:C_COS + NLAT] = np.cos(ang.astype(np.float32))
    c[:, C_SIN:C_SIN + NLAT] = np.sin(ang.astype(np.float32))
    for b in range(2):
        at = C_BAND + b * NTOK + NCTX
        c[:, at:at + NLAT] = np.where(np.abs(i[:, None] + b * P - tok[None, :]) <= 128, 0.0, -BIG)
    c[:, C_MF:C_MF + P] = np.where(i[:, None] >= i[None, :], 0.0, -BIG)
    c[:, C_MB:C_MB + P] = np.where(i[:, None] <= i[None, :], 0.0, -BIG)
    c[:, C_IOTA:C_IOTA + P] = i[None, :]
    c[:, C_TOK:C_TOK + TT] = i[:, None] + P * np.arange(TT)[None, :]
    c[:, C_PIDX1] = i + 1
    b, x = np.divmod(np.arange(3 * NE), NE)
    c[:, C_OVER:C_OVER + 192] = x
    c[:, C_OVER + 192:C_OVER + 384] = b + 1
    return c


def pack(w, out=None):
    import numpy as np
    k, n = w.shape[0] // P, w.shape[1]
    return np.ascontiguousarray(w.reshape(k, P, n).transpose(1, 0, 2)).reshape(P, k * n)


def kernel(x, c, ctx, c_ctx, w_mod, b_mod, g_mix, g_ffn, w_in, b_gate, sink, lam_q1, lam_k1,
           lam_q2, lam_k2, g_diff, g_mlstm, w_a, w_b, w_c, w_out, w_router, b_router,
           w_exp_gate, w_exp_up, w_exp_down, w_sh_gate, w_sh_up, w_sh_down, g_final):
    import numpy as np
    import concourse.bacc as bacc
    from concourse.bass_utils import run_bass_kernel_spmd as run

    f = np.float32
    w_in = np.asarray(w_in)
    d = {}
    d["x"] = np.concatenate([np.asarray(ctx)[0], np.asarray(x)[0]], 0)
    d["cond"] = np.ascontiguousarray(np.stack([np.asarray(c_ctx), np.asarray(c)[0]], -1).reshape(KT, P, 2).transpose(1, 0, 2))
    d["const"] = constants()
    aq = np.concatenate([np.arange(h * DH, h * DH + DH) for j in range(4) for h in (j, j + 4)])
    o = np.cumsum([0, 512, 128, 128, 512, 512, 512, 512, 512, 512, 512, 16, 3072])
    r = [np.arange(o[i], o[i + 1]) for i in range(12)]
    cols = [aq, r[3], r[4], r[6], r[7], np.concatenate([r[1], r[2], r[10]]), r[5], r[8], r[9]]
    wseq = np.zeros((len(SEQ), P, SLOT), f)
    for n, (l, kind, i) in enumerate(SEQ):
        dst = wseq[n]
        if kind == "mod":
            dst[:, :KT * 512] = pack(np.asarray(w_mod[l])[:, i * 512:i * 512 + 512])
        elif kind == "in":
            dst[:, :KT * len(cols[i])] = pack(w_in[l][:, cols[i]])
        elif kind == "merge":
            j, b = divmod(i, 3)
            gc = o[11] + b * D + j * 512
            dst[:, :KT * 512] = pack(w_in[l][:, gc:gc + 512])
            dst[:, KT * 512:] = pack(np.asarray((w_a, w_b, w_c)[b])[l][:, j * 512:j * 512 + 512])
        elif kind == "out":
            dst[:, :KT * 512] = pack(np.asarray(w_out)[l][:, i * 512:i * 512 + 512])
        else:
            dst[:, :KT * 512] = pack(np.concatenate([np.asarray(w_sh_gate)[l], np.asarray(w_sh_up)[l]], 1))
            dst[:, KT * 512:] = pack(np.asarray(w_sh_down)[l])
    d["wseq"] = wseq
    wexp = np.empty((L, NE, P, SLOT), f)
    gu = wexp[..., :KT * 512].reshape(L, NE, P, KT, 2, DE)
    gu[..., 0, :] = np.asarray(w_exp_gate).reshape(L, NE, KT, P, DE).transpose(0, 1, 3, 2, 4)
    gu[..., 1, :] = np.asarray(w_exp_up).reshape(L, NE, KT, P, DE).transpose(0, 1, 3, 2, 4)
    wexp[..., KT * 512:].reshape(L, NE, P, 2, D)[:] = np.asarray(w_exp_down).reshape(L, NE, 2, P, D).transpose(0, 1, 3, 2, 4)
    d["wexp"] = wexp
    d["wr"] = np.stack([pack(np.asarray(w_router)[l]) for l in range(L)])
    row = np.concatenate([np.asarray(b_router), np.asarray(sink), np.asarray(g_diff), np.asarray(g_mlstm),
                          np.asarray(b_gate).reshape(L, 16), np.asarray(lam_q1), np.asarray(lam_k1),
                          np.asarray(lam_q2), np.asarray(lam_k2)], 1)
    d["rowp"] = np.ascontiguousarray(np.broadcast_to(row[:, None, :], (L, P, NROW)))
    d["colp"] = np.ascontiguousarray(np.concatenate(
        [np.asarray(g_mix).reshape(L, KT, P), np.asarray(g_ffn).reshape(L, KT, P)],
        1).transpose(0, 2, 1))
    d["bmod"] = np.ascontiguousarray(np.repeat(np.asarray(b_mod).reshape(L, NMOD, 1, 512), 2, axis=2))
    d["gfinal"] = np.ascontiguousarray(np.broadcast_to(np.asarray(g_final)[None], (P, D)))

    nc = bacc.Bacc("TRN2", target_bir_lowering=False, num_devices=1)
    a = {n: nc.dram_tensor("in_" + n, v.shape, mybir.dt.from_np(v.dtype), kind="ExternalInput").ap() for n, v in d.items()}
    a["out"] = nc.dram_tensor("out_0", (NLAT, D), F32, kind="ExternalOutput").ap()
    a["mod_rows"] = nc.dram_tensor("mod_rows", (L, 2, 6 * D), F32, kind="Internal").ap()
    a["h_rows"] = nc.dram_tensor("h_rows", (NTOK, D), F32, kind="Internal").ap()
    a["y_rows"] = nc.dram_tensor("y_rows", (NE * P, D), F32, kind="Internal").ap()
    build(nc, a)
    res = run(nc, [{"in_" + n: v for n, v in d.items()}], core_ids=[0])
    return res.results[0]["out_0"][None]
```
